# Optimizing a Trainium2 kernel written in Bass

```python
import jax, jax.numpy as jnp
from jax import lax
import numpy as np

D_MODEL = 1024
BATCH = 1
SEQ = 512
DEPTH = 2

GRID_W = 64
CTX_LEN = 256
EPS = 1e-6

POOL_WINDOWS = (2, 4, 8, 16)
N_POOL_GROUPS = 4
POOL_GROUP_DIM = D_MODEL // 8
POOL_WIDTH = N_POOL_GROUPS * POOL_GROUP_DIM
N_FOURIER_HEADS = 4
FOURIER_HEAD_DIM = D_MODEL // 8
FOURIER_WIDTH = N_FOURIER_HEADS * FOURIER_HEAD_DIM
PF_WIDTH = POOL_WIDTH + FOURIER_WIDTH

HEAD_DIM = 128
N_Q_HEADS = D_MODEL // HEAD_DIM
N_KV_HEADS = 2
GQA_GROUP = N_Q_HEADS // N_KV_HEADS
Q_WIDTH = N_Q_HEADS * HEAD_DIM
KV_WIDTH = N_KV_HEADS * HEAD_DIM
QKV_WIDTH = Q_WIDTH + 2 * KV_WIDTH
Q_BLOCK = 128
ROPE_THETA = 10000.0
ROPE_PAIRS = HEAD_DIM // 4

D_FF = 2816
CONV_W = 3
N_MOD = 6

N_EVEN = (DEPTH + 1) // 2
N_ODD = DEPTH // 2

kernel_name = 'hybrid_pool_fourier_gqa_dit_prefix'

def rmsnorm(x, g):
    xf = x.astype(jnp.float32)
    y = xf * lax.rsqrt(jnp.mean(xf * xf, axis=-1, keepdims=True) + EPS)
    return (y * g.astype(jnp.float32)).astype(x.dtype)

def adaln(cvec, w, b):
    m = jax.nn.silu(cvec) @ w + b
    return [t[:, None, :] for t in jnp.split(m, N_MOD, axis=-1)]

def modulate(h, shift, scale):
    return h * (1.0 + scale) + shift

def centred_mean_minus_self(u, w):
    L = u.shape[1]
    uf = u.astype(jnp.float32)
    cs = jnp.pad(jnp.cumsum(uf, axis=1), ((0, 0), (1, 0), (0, 0)))
    t = jnp.arange(L)
    lo = jnp.clip(t - w // 2, 0, L)
    hi = jnp.clip(t + (w - 1 - w // 2) + 1, 0, L)
    s = jnp.take(cs, hi, axis=1) - jnp.take(cs, lo, axis=1)
    cnt = (hi - lo).astype(jnp.float32)[None, :, None]
    return (s / cnt - uf).astype(u.dtype)

def pool_fourier_mixer(h, w_in, pool_w, pool_scale, fourier_w, w_out):
    B, L, _ = h.shape
    u = h @ w_in
    u_pool = u[..., :POOL_WIDTH].reshape(B, L, N_POOL_GROUPS, POOL_GROUP_DIM)
    u_four = u[..., POOL_WIDTH:].reshape(B, L, N_FOURIER_HEADS, FOURIER_HEAD_DIM)
    pooled = jnp.stack([centred_mean_minus_self(u_pool[:, :, g], w)
                        for g, w in enumerate(POOL_WINDOWS)], axis=2)
    y_pool = jnp.einsum('blgc,gcd->blgd', pooled, pool_w) * pool_scale.reshape(N_POOL_GROUPS, POOL_GROUP_DIM)
    spec = jnp.fft.fftn(u_four.astype(jnp.float32), axes=(1, 3), norm='ortho').real.astype(h.dtype)
    y_four = jnp.einsum('blhc,hcd->blhd', spec, fourier_w)
    y = jnp.concatenate([y_pool.reshape(B, L, POOL_WIDTH), y_four.reshape(B, L, FOURIER_WIDTH)], axis=-1)
    return y @ w_out

def _rot_half(x, ang):
    x1, x2 = jnp.split(x, 2, axis=-1)
    ang = ang.reshape((ang.shape[0],) + (1,) * (x.ndim - 3) + (ang.shape[1],))
    cos = jnp.cos(ang).astype(x.dtype)
    sin = jnp.sin(ang).astype(x.dtype)
    return jnp.concatenate([x1 * cos - x2 * sin, x1 * sin + x2 * cos], axis=-1)

def rope_2d(x, ang_row, ang_col):
    xr, xc = jnp.split(x, 2, axis=-1)
    return jnp.concatenate([_rot_half(xr, ang_row), _rot_half(xc, ang_col)], axis=-1)

def _attend(q, k, v):
    s = jnp.einsum('bqkgd,bskd->bkgqs', q, k, preferred_element_type=jnp.float32) * (HEAD_DIM ** -0.5)
    p = jax.nn.softmax(s, axis=-1).astype(v.dtype)
    return jnp.einsum('bkgqs,bskd->bqkgd', p, v)

def attention_mixer(h_lat, h_ctx, w_qkv, q_g, k_g, w_o, ang_row, ang_col, need_ctx):
    B, L, _ = h_lat.shape
    C = h_ctx.shape[1]
    qkv = h_lat @ w_qkv
    q = rmsnorm(qkv[..., :Q_WIDTH].reshape(B, L, N_KV_HEADS, GQA_GROUP, HEAD_DIM), q_g)
    k = rmsnorm(qkv[..., Q_WIDTH:Q_WIDTH + KV_WIDTH].reshape(B, L, N_KV_HEADS, HEAD_DIM), k_g)
    v = qkv[..., Q_WIDTH + KV_WIDTH:].reshape(B, L, N_KV_HEADS, HEAD_DIM)
    q = rope_2d(q, ang_row, ang_col)
    k = rope_2d(k, ang_row, ang_col)
    kv_c = h_ctx @ w_qkv[:, Q_WIDTH:]
    k_c = rmsnorm(kv_c[..., :KV_WIDTH].reshape(B, C, N_KV_HEADS, HEAD_DIM), k_g)
    v_c = kv_c[..., KV_WIDTH:].reshape(B, C, N_KV_HEADS, HEAD_DIM)
    k_all = jnp.concatenate([k, k_c], axis=1)
    v_all = jnp.concatenate([v, v_c], axis=1)
    nb = L // Q_BLOCK
    qb = q.reshape(B, nb, Q_BLOCK, N_KV_HEADS, GQA_GROUP, HEAD_DIM).transpose(1, 0, 2, 3, 4, 5)
    o = lax.map(lambda qi: _attend(qi, k_all, v_all), qb)
    o = o.transpose(1, 0, 2, 3, 4, 5).reshape(B, L, Q_WIDTH)
    out_lat = o @ w_o
    out_ctx = None
    if need_ctx:
        q_c = rmsnorm((h_ctx @ w_qkv[:, :Q_WIDTH]).reshape(B, C, N_KV_HEADS, GQA_GROUP, HEAD_DIM), q_g)
        out_ctx = _attend(q_c, k_c, v_c).reshape(B, C, Q_WIDTH) @ w_o
    return out_lat, out_ctx

def conv_ffn(h, w_up, conv_w, conv_b, w_down):
    a = h @ w_up
    ap = jnp.pad(a, ((0, 0), (1, 1), (0, 0)))
    a = ap[:, :-2] * conv_w[0] + ap[:, 1:-1] * conv_w[1] + ap[:, 2:] * conv_w[2] + conv_b
    g, u = jnp.split(a, 2, axis=-1)
    return (jax.nn.silu(g) * u) @ w_down

def setup_inputs(seed: int = 0) -> dict:
    key = jax.random.key(seed)
    ks = jax.random.split(key, 24)
    f32 = jnp.float32
    nrm = lambda k, shape, s: jax.random.normal(k, shape, f32) * s
    D = D_MODEL
    return {
        'x': nrm(ks[0], (BATCH, SEQ, D), 1.0),
        'c': nrm(ks[1], (BATCH, D), 1.0),
        'ctx': nrm(ks[2], (BATCH, CTX_LEN, D), 1.0),
        'c_ctx': nrm(ks[3], (D,), 1.0),
        'ada_w': nrm(ks[4], (DEPTH, D, N_MOD * D), 0.5 * D ** -0.5),
        'ada_b': nrm(ks[5], (DEPTH, N_MOD * D), 0.01),
        'norm1_g': 1.0 + nrm(ks[6], (DEPTH, D), 0.02),
        'norm2_g': 1.0 + nrm(ks[7], (DEPTH, D), 0.02),
        'pf_w_in': nrm(ks[8], (N_EVEN, D, PF_WIDTH), D ** -0.5),
        'pool_w': nrm(ks[9], (N_EVEN, N_POOL_GROUPS, POOL_GROUP_DIM, POOL_GROUP_DIM), POOL_GROUP_DIM ** -0.5),
        'pool_scale': 1.0 + nrm(ks[10], (N_EVEN, POOL_WIDTH), 0.1),
        'fourier_w': nrm(ks[11], (N_EVEN, N_FOURIER_HEADS, FOURIER_HEAD_DIM, FOURIER_HEAD_DIM), FOURIER_HEAD_DIM ** -0.5),
        'pf_w_out': nrm(ks[12], (N_EVEN, PF_WIDTH, D), PF_WIDTH ** -0.5),
        'attn_w_qkv': nrm(ks[13], (N_ODD, D, QKV_WIDTH), D ** -0.5),
        'q_norm_g': 1.0 + nrm(ks[14], (N_ODD, HEAD_DIM), 0.02),
        'k_norm_g': 1.0 + nrm(ks[15], (N_ODD, HEAD_DIM), 0.02),
        'attn_w_o': nrm(ks[16], (N_ODD, Q_WIDTH, D), Q_WIDTH ** -0.5),
        'ffn_w_up': nrm(ks[17], (DEPTH, D, 2 * D_FF), D ** -0.5),
        'ffn_conv_w': nrm(ks[18], (DEPTH, CONV_W, 2 * D_FF), CONV_W ** -0.5),
        'ffn_conv_b': nrm(ks[19], (DEPTH, 2 * D_FF), 0.01),
        'ffn_w_down': nrm(ks[20], (DEPTH, D_FF, D), D_FF ** -0.5),
        'final_g': 1.0 + nrm(ks[21], (D,), 0.02),
    }

def reference(x, c, ctx, c_ctx, ada_w, ada_b, norm1_g, norm2_g, pf_w_in, pool_w, pool_scale,
              fourier_w, pf_w_out, attn_w_qkv, q_norm_g, k_norm_g, attn_w_o, ffn_w_up,
              ffn_conv_w, ffn_conv_b, ffn_w_down, final_g):
    L = x.shape[1]
    n_rows = L // GRID_W
    row = jnp.repeat(jnp.arange(n_rows), GRID_W).astype(jnp.float32)
    col = jnp.tile(jnp.arange(GRID_W), n_rows).astype(jnp.float32)
    freqs = ROPE_THETA ** (-jnp.arange(ROPE_PAIRS, dtype=jnp.float32) / ROPE_PAIRS)
    ang_row = row[:, None] * freqs[None, :]
    ang_col = col[:, None] * freqs[None, :]

    x_lat, x_ctx = x, ctx
    for i in range(DEPTH):
        need_ctx = i < DEPTH - 1
        j = i // 2
        ml = adaln(c, ada_w[i], ada_b[i])
        mc = adaln(c_ctx[None, :], ada_w[i], ada_b[i])
        h_lat = modulate(rmsnorm(x_lat, norm1_g[i]), ml[0], ml[1])
        if i % 2 == 0:
            y_lat = pool_fourier_mixer(h_lat, pf_w_in[j], pool_w[j], pool_scale[j], fourier_w[j], pf_w_out[j])
            x_lat = x_lat + ml[2] * y_lat
            if need_ctx:
                h_ctx = modulate(rmsnorm(x_ctx, norm1_g[i]), mc[0], mc[1])
                y_ctx = pool_fourier_mixer(h_ctx, pf_w_in[j], pool_w[j], pool_scale[j], fourier_w[j], pf_w_out[j])
                x_ctx = x_ctx + mc[2] * y_ctx
        else:
            h_ctx = modulate(rmsnorm(x_ctx, norm1_g[i]), mc[0], mc[1])
            y_lat, y_ctx = attention_mixer(h_lat, h_ctx, attn_w_qkv[j], q_norm_g[j], k_norm_g[j], attn_w_o[j],
                                           ang_row, ang_col, need_ctx)
            x_lat = x_lat + ml[2] * y_lat
            if need_ctx:
                x_ctx = x_ctx + mc[2] * y_ctx
        f_lat = conv_ffn(modulate(rmsnorm(x_lat, norm2_g[i]), ml[3], ml[4]),
                         ffn_w_up[i], ffn_conv_w[i], ffn_conv_b[i], ffn_w_down[i])
        x_lat = x_lat + ml[5] * f_lat
        if need_ctx:
            f_ctx = conv_ffn(modulate(rmsnorm(x_ctx, norm2_g[i]), mc[3], mc[4]),
                             ffn_w_up[i], ffn_conv_w[i], ffn_conv_b[i], ffn_w_down[i])
            x_ctx = x_ctx + mc[5] * f_ctx
    return rmsnorm(x_lat, final_g)


_drawn_inputs = setup_inputs


def setup_inputs(seed=0):
    import zlib

    import numpy as np

    out = dict(_drawn_inputs(seed))
    spreads = {}
    factors = {'ctx': 5.46,
     'ada_b': 3.967,
     'norm1_g': 8.0,
     'norm2_g': 6.721,
     'pool_scale': 2.69,
     'q_norm_g': 8.0,
     'k_norm_g': 8.0,
     'ffn_conv_b': 8.0,
     'final_g': 2.737}
    for name, (base, spread) in spreads.items():
        noise = np.random.default_rng([zlib.crc32(name.encode()), seed]).standard_normal(out[name].shape)
        drawn = base * np.exp(spread * noise) if base else spread * noise
        out[name] = __import__('jax').numpy.asarray(drawn.astype(out[name].dtype))
    for name, factor in factors.items():
        out[name] = (out[name] * factor).astype(out[name].dtype)
    return out
```

```python
from contextlib import ExitStack

import concourse.bass as bass
import numpy as np
from concourse import mybir

F32 = mybir.dt.float32
F32R = mybir.dt.float32r
BF16 = mybir.dt.bfloat16
ALU = mybir.AluOpType
ACT = mybir.ActivationFunctionType
AX_X = mybir.AxisListType.X

P = 128
D = 1024
KT = D // P
L = 512
C = 256
T = L + C
FF = 2816
FT = FF // P
GROUPS = (8, 8, 6)
NH, NKV, DH = 8, 2, 128
GQA = NH // NKV
GRID_W = 64
EPS = 1e-6
BW = 1024
RAW, RING = 2, 4
PAD = 8
UL, UC, UW = PAD, PAD + L + 2 * PAD, L + C + 4 * PAD
STREAMS = ((0, 0, L), (1, L, T))
LATENT = STREAMS[:1]



def numbered(names, start=0):
    return {n: start + i for i, n in enumerate(names)}


def plan():
    ffn = lambda l: [(k, l, gi, i) for gi, n in enumerate(GROUPS)
                     for k, m in (("up", 2 * n), ("down", KT)) for i in range(m)]
    blocks = (["df"] + [("four", h) for h in range(4)] + [("pin", g) for g in range(4)]
              + ["c0", "c1", "s0", "s1", "ctxdft", "poolw"] + [("out", m) for m in range(KT)] + ffn(0)
              + [("k", j) for j in range(NKV)] + [("v", j) for j in range(2)]
              + [("q", h) for h in range(NH)] + [("o", m) for m in range(KT)] + ffn(1))
    units = (["n0", "ab", ("four", 0), ("four", 1), ("va", 0), ("vb", 0), ("four", 2), ("va", 1), ("vb", 1),
              ("four", 3), ("va", 2), ("vb", 2), ("pin", 0), ("va", 3), ("vb", 3)] + [("pin", g) for g in (1, 2, 3)]
             + ["dft0", "dft1", "dftc"] + [("poolw", g) for g in range(4)] + [("out", m) for m in range(KT)]
             + ["n1"] + ffn(0) + ["n2"])
    heads = [("k", j) for j in range(NKV)] + [("q", h) for h in range(NH)]
    units += [("k", 0), ("k", 1), ("ss", 0), "v0", ("ss", 1), "v1"]
    for h in range(NH):
        units += [("q", h)] + ([("ss", 1 + h)] if h else [])
    units += [("ss", 9)]
    n = NH * 4
    for i in range(n + 3):
        units += [("s", i)] * (i < n) + [("t", i - 2)] * (2 <= i < n + 2)
        if i >= 6 and (i - 6) % 4 == 0:
            units += [("pv", (i - 6) // 4)]
    units += [("o", m) for m in range(KT)] + ["n3"] + ffn(1) + ["n4"]
    splits = ([("h", 0, k) for k in range(KT)] + ["ab", ("u", 0), ("u", 1), ("va", 0), ("vb", 0), ("u", 2),
              ("va", 1), ("vb", 1), ("u", 3), ("va", 2), ("vb", 2), ("va", 3), ("vb", 3)]
              + [("pool", g) for g in range(4)] + ["dft0", "dft1", "dftc"] + [("y", g) for g in range(4)]
              + [("h", 1, k) for k in range(KT)] + [("g", 0, p) for p in range(FT)]
              + [("h", 2, k) for k in range(KT)] + [("k", 0), "v0", ("k", 1), "v1"] + [("q", h) for h in range(NH)])
    for i in range(2, n + 3):
        splits += [("t", i - 2)] * (i < n + 2)
        if i >= 6 and (i - 6) % 4 == 0:
            splits += [("pv", (i - 6) // 4)]
    splits += [("h", 3, k) for k in range(KT)] + [("g", 1, p) for p in range(FT)]
    return numbered(blocks), numbered(units), numbered(splits), heads


BLK, UNIT, SPLIT, HEADS = plan()
NB = len(BLK)

SHIFT = (0, 24, 48, 72)
GATE = {("mixer", 0): 16, ("ffn", 0): 40, ("mixer", 1): 64, ("ffn", 1): 88}


def kind(unit_name):
    return unit_name if isinstance(unit_name, str) else unit_name[0]


FREED = {n for name, n in UNIT.items() if kind(name) in ("pin", "out", "up", "down", "o")}


BOTH = 64


def dots_after(t, both=None):
    return 2 * (t + 1) if (t < BOTH if both is None else both) else BOTH + t + 1


def freed_before(n):
    return 1 + sum(m in FREED for m in range(n % 4, n, 4))

V_ADAB, V_N1, V_N2, V_FG = 0, 96, 112, 128
V_PS, V_QG, V_KG, V_EDGE = 136, 140, 141, 142
V_CONV = V_EDGE + 64
NORM_G = (V_N1, V_N2, V_N1 + KT, V_N2 + KT)
NVEC = V_CONV + 4 * 2 * FT
M_MODS = NVEC
M_GAIN = M_MODS + 192
M_ACC = M_GAIN + 64
M_STAT = M_ACC + 8
M_EPS = M_STAT + 16
M_ONES = M_EPS + 1
NSMALL = M_ONES + P
T_COS, T_SIN, T_ID, T_CONV = 0, L, 2 * L, 2 * L + P
NTAB = T_CONV + 4 * 2 * FT


def program(nc, xt, cvec, wstream, adaw, vecs, tabs, out):
    with ExitStack() as ctx:
        def sb(name, shape, dt=F32):
            return ctx.enter_context(nc.sbuf_tensor(name, shape, dt))

        def sem(name):
            return ctx.enter_context(nc.semaphore(name))

        x = sb("x", [P, KT, T])
        h_hi, h_lo = sb("h_hi", [P, KT, T], F32R), sb("h_lo", [P, KT, T], F32R)
        g_hi, g_lo = sb("g_hi", [P, KT, T], F32R), sb("g_lo", [P, KT, T], F32R)
        w_hi, w_lo = sb("w_hi", [P, RING, BW], F32R), sb("w_lo", [P, RING, BW], F32R)
        w_raw = sb("w_raw", [P, RAW, BW])
        uv_hi, uv_lo = sb("uv_hi", [P, T + BW], F32R), sb("uv_lo", [P, T + BW], F32R)
        ada_raw = sb("ada_raw", [P, 2 * BW])
        junk = sb("junk", [P, BW], BF16)
        cond = sb("cond", [P, 2 * BW])
        scratch = sb("scratch", [P, 4 * UW])
        small = sb("small", [P, NSMALL])
        psum = ctx.enter_context(nc.psum_tensor("psum", [P, 4, BW], F32))

        x_landed = [sem(f"x_landed{i}") for i in range(2)]
        vecs_landed, cond_landed = sem("vecs_landed"), sem("cond_landed")
        tabs_landed = sem("tabs_landed")
        w_landed = [sem(f"w_landed{i}") for i in range(RAW)]
        ada_landed = [sem(f"ada_landed{i}") for i in range(2)]
        rot_landed = [sem(f"rot_landed{i}") for i in range(2)]
        out_stored = sem("out_stored")
        w_hi_ready, w_lo_ready = sem("w_hi_ready"), sem("w_lo_ready")
        dft_block_used = sem("dft_block_used")
        unit_ready = sem("unit_ready")
        unit_free = [sem(f"unit_free{i}") for i in range(4)]
        hi_ready, lo_ready = sem("hi_ready"), sem("lo_ready")
        cond_ready, dots_ready, mods_ready = sem("cond_ready"), sem("dots_ready"), sem("mods_ready")
        gain_ready, rms_ready, rstd_ready, scaled = sem("gain_ready"), sem("rms_ready"), sem("rstd_ready"), sem("scaled")
        squared, square_used, sumsq_added = sem("squared"), sem("square_used"), sem("sumsq_added")
        pads_ready, u_copied, window_step, pooled = sem("pads_ready"), sem("u_copied"), sem("window_step"), sem("pooled")
        center_tap, left_tap, silu_done, product_ready = sem("center_tap"), sem("left_tap"), sem("silu_done"), sem("product_ready")
        head_gained, head_squared, head_rms, head_rstd = sem("head_gained"), sem("head_squared"), sem("head_rms"), sem("head_rstd")
        rope_step, head_ready = sem("rope_step"), sem("head_ready")
        max_found, max_ready, exp_ready, inv_ready, probs_ready = (
            sem("max_found"), sem("max_ready"), sem("exp_ready"), sem("inv_ready"), sem("probs_ready"))
        eps_ready, final_ready = sem("eps_ready"), sem("final_ready")

        def view(buf, at, n):
            return buf[:, at:at + n]

        ones = view(small, M_ONES, P)
        eps = view(small, M_EPS, 1)
        mods = view(small, M_MODS, 192).rearrange("p (t s) -> p t s", s=2)
        gains = view(small, M_GAIN, 64).rearrange("p (n k s) -> p n k s", n=4, s=2)
        ada_acc = view(small, M_ACC, 8).rearrange("p (j s) -> p j s", s=2)
        stat = view(small, M_STAT, 16).rearrange("p (r s) -> p r s", s=4)
        cos, sin = view(ada_raw, T_COS, L), view(ada_raw, T_SIN, L)
        ident = view(ada_raw, T_ID, P)
        conv = [view(small, V_CONV, 8 * FT).rearrange("p (t c) -> p t c", c=4),
                view(ada_raw, T_CONV, 8 * FT).rearrange("p (t c) -> p t c", c=4)]
        edge = view(small, V_EDGE, 64).rearrange("p (g e c) -> p g e c", g=4, e=2)
        tile_ = [scratch[:, i * T:(i + 1) * T] for i in range(4)]
        upad = [scratch[:, i * UW:(i + 1) * UW] for i in range(4)]
        headbuf = [scratch[:, i * T:(i + 1) * T] for i in range(2)]
        rotated = [scratch[:, 2 * T + i * L:2 * T + (i + 1) * L] for i in range(2)]
        head_sq, head_inv, head_sin = view(cond, 0, T), view(cond, T, T), view(cond, 2 * T, L)
        probs = [scratch[:, i * T:(i + 1) * T] for i in range(2)]
        u_part = [b[:, 0:T] for b in (uv_hi, uv_lo)]
        ab = [b[:, T:T + BW].rearrange("p (h c) -> p h c", h=4) for b in (uv_hi, uv_lo)]
        vv = [b[:, :, :].rearrange("p a b -> p (a b)").rearrange("p (t h c) -> p t h c", t=6, h=4) for b in (g_hi, g_lo)]
        gflat = [b[:, :, :].rearrange("p a b -> p (a b)") for b in (g_hi, g_lo)]
        hflat = [b[:, :, :].rearrange("p a b -> p (a b)") for b in (h_hi, h_lo)]
        qo = [b[:, 0:NH * L].rearrange("p (h t) -> p h t", h=NH) for b in gflat]
        kk = [b[:, NH * L:NH * L + NKV * T].rearrange("p (h t) -> p h t", h=NKV) for b in gflat]
        v_ = [b[:, 0:6 * NKV * DH].rearrange("p (t c) -> p t c", t=6) for b in (uv_hi, uv_lo)]
        pt = [b[:, :].rearrange("p (r k q) -> p r k q", r=2, k=6) for b in hflat]

        def slot(n):
            return psum[:, n % 4, :]

        def col(buf, i):
            return buf[:, bass.ds(i, 1)]

        def tile3(buf, i):
            return buf[:, bass.ds(i, 1), :].rearrange("p o n -> p (o n)")

        def used_at(b):
            name = next(n for n, i in BLK.items() if i == b)
            if name in ("c0", "c1", "s0"):
                return dft_block_used, ("c0", "c1", "s0").index(name) + 1
            unit = {"df": "ab", "s1": "dft1", "ctxdft": "dftc", "poolw": ("poolw", 3), ("v", 0): "v1", ("v", 1): "v1"}.get(name, name)
            return unit_ready, UNIT[unit] + 1

        def released(n):
            name = next(u for u, i in UNIT.items() if i == n)
            k = kind(name)
            if n in FREED:
                return unit_free[n % 4], freed_before(n) + 1
            if k in ("k", "q"):
                return head_squared, HEADS.index(name) + 1
            if k == "ss":
                return head_rms, name[1] + 1
            if k == "s":
                return exp_ready, name[1] + 1
            if k[0] == "n":
                return rms_ready, int(k[1:]) + 1
            split = {"four": ("u", name[1]), "poolw": ("y", name[1])}.get(k, name)
            return lo_ready, SPLIT[split] + 1

        def wait_part(eng, name):
            eng.wait_ge(lo_ready, SPLIT[name] + 1)

        block = ctx.enter_context(nc.Block())

        @block.sync
        def _(sp):
            sp.dma_start(x[:, 0:4, :], xt[:, 0:4, :]).then_inc(x_landed[0], 16)
            sp.dma_start(x[:, 4:8, :], xt[:, 4:8, :]).then_inc(x_landed[1], 16)
            for b in range(RAW):
                sp.dma_start(w_raw[:, b, :], wstream[b]).then_inc(w_landed[b], 16)
            pairs = (NB + RAW - 1) // RAW
            with sp.Fori(1, NB // RAW) as i:
                for b in range(RAW):
                    sp.wait_ge(w_lo_ready, i * RAW + (b + 1 - RAW))
                    sp.dma_start(w_raw[:, b, :], wstream[bass.ds(i * RAW + b, 1)].rearrange("o p n -> p (o n)")).then_inc(w_landed[b], 16)
            for b in range(NB // RAW * RAW, NB):
                sp.wait_ge(w_lo_ready, b + 1 - RAW)
                sp.dma_start(w_raw[:, b % RAW, :], wstream[b]).then_inc(w_landed[b % RAW], 16)

        @block.gpsimd
        def _(pool):
            nc.gpsimd.memset(ones, 1.0).then_inc(eps_ready, 1)
            nc.gpsimd.memset(eps, EPS).then_inc(eps_ready, 1)

            def lo_part(slot_, wait):
                pool.wait_ge(w_hi_ready, wait)
                nc.gpsimd.tensor_tensor(w_lo[:, slot_, :], w_raw[:, slot_ % RAW, :], w_hi[:, slot_, :].bitcast(F32),
                                        ALU.subtract).then_inc(w_lo_ready, 1)

            with pool.Fori(0, NB // RING) as i:
                for j in range(RING):
                    lo_part(j, i * RING + (j + 1))
            for b in range(NB // RING * RING, NB):
                lo_part(b % RING, b + 1)

        @block.scalar
        def _(act):
            act.dma_start(small[:, 0:NVEC], vecs).then_inc(vecs_landed, 16)
            act.dma_start(cond[:, :], cvec).then_inc(cond_landed, 16)

            def w_split(b, i=None):
                s, turns = b % RING, 0 if i is None else i * (RING // RAW)
                act.wait_ge(w_landed[s % RAW], (b // RAW + 1) * 16 + (0 if i is None else i * (16 * RING // RAW)))
                nc.scalar.activation(w_hi[:, s, :], w_raw[:, s % RAW, :], ACT.Copy).then_inc(w_hi_ready, 1)

            def w_next(b):
                if b + RING - 1 >= NB:
                    return
                if b >= 1:
                    act.wait_ge(*used_at(b - 1))
                w_split(b + RING - 1)

            def ada_load(t, i=None, waits=True, both=None):
                if waits:
                    n = dots_after(t - 2, both)
                    act.wait_ge(dots_ready, n if i is None else i * (4 * (1 + both)) + n)
                src = adaw[t] if i is None else adaw[bass.ds(i * 4 + t, 1)].rearrange("o p n -> p (o n)")
                act.dma_start(ada_raw[:, (t % 2) * BW:(t % 2 + 1) * BW], src).then_inc(ada_landed[t % 2], 16)

            def unit(name):
                act.wait_ge(unit_ready, UNIT[name] + 1)

            ada_load(0, waits=False)
            ada_load(1, waits=False)
            for b in range(RING - 1):
                w_split(b)
            w_next(0)
            act.wait_ge(cond_landed, 16)
            nc.scalar.activation(cond[:, :], cond[:, :], ACT.Silu).then_inc(cond_ready, 1)
            for k in range(KT):
                act.wait_ge(x_landed[k // 4], 16)
                if k >= 2:
                    act.wait_ge(square_used, k - 1)
                nc.scalar.activation(tile_[k % 2], x[:, k, :], ACT.Square).then_inc(squared, 1)

            def rms(n, streams, pads=False):
                unit(f"n{n}")
                if n == 0:
                    act.wait_ge(eps_ready, 2)
                end = streams[-1][2]
                nc.scalar.activation(tile_[3][:, 0:end], slot(UNIT[f"n{n}"])[:, 0:end], ACT.Sqrt,
                                     bias=eps, scale=1.0 / D).then_inc(rms_ready, 1)

            def h_hi_parts(n, streams):
                act.wait_ge(gain_ready, n + 1)
                for k in range(KT):
                    act.wait_ge(scaled, KT * n + k + 1)
                    for s, a, e in streams:
                        ins = nc.scalar.activation(h_hi[:, k, a:e], tile_[k % 2][:, a:e], ACT.Identity,
                                                   bias=mods[:, SHIFT[n] + k, s:s + 1])
                    ins.then_inc(hi_ready, 1)

            rms(0, STREAMS)
            for t in range(2, 18):
                ada_load(t)
            h_hi_parts(0, STREAMS)

            unit("ab")
            for z in range(2):
                ins = nc.scalar.activation(ab[0][:, :, z * P:(z + 1) * P],
                                           slot(UNIT["ab"])[:, z * L:(z + 1) * L].rearrange("p (h c) -> p h c", h=4), ACT.Copy)
            ins.then_inc(hi_ready, 1)

            def v_hi(kind, h):
                n = UNIT[(kind, h)]
                unit((kind, h))
                t0, nt = (0, 4) if kind == "va" else (4, 2)
                nc.scalar.activation(vv[0][:, t0:t0 + nt, h, :],
                                     slot(n)[:, 0:nt * C].rearrange("p (t c) -> p t c", t=nt), ACT.Copy).then_inc(hi_ready, 1)

            def u_hi(h):
                w_next(BLK[("four", h)])
                unit(("four", h))
                if h >= 1:
                    unit(("vb", h - 1))
                nc.scalar.activation(u_part[0], slot(UNIT[("four", h)])[:, 0:T], ACT.Copy).then_inc(hi_ready, 1)

            def u_copy(g):
                w_next(BLK[("pin", g)])
                unit(("pin", g))
                if g == 0:
                    act.wait_ge(pads_ready, 2)
                if g >= 2:
                    act.wait_ge(lo_ready, SPLIT[("pool", g - 2)] + 1)
                n = UNIT[("pin", g)]
                nc.scalar.activation(upad[g % 2][:, UL:UL + L], slot(n)[:, 0:L], ACT.Copy).then_inc(u_copied, 1)
                nc.scalar.activation(upad[g % 2][:, UC:UC + C], slot(n)[:, L:T], ACT.Copy).then_inc(unit_free[n % 4], 1)

            def pool_hi(g):
                act.wait_ge(pooled, g + 1)
                nc.scalar.activation(h_hi[:, g, 0:L], upad[g % 2][:, UL:UL + L], ACT.Copy)
                nc.scalar.activation(h_hi[:, g, L:T], upad[g % 2][:, UC:UC + C], ACT.Copy).then_inc(hi_ready, 1)

            ada = iter(range(18, 48))

            def ada_loads(n):
                for _ in range(n):
                    t = next(ada, None)
                    if t is not None:
                        ada_load(t)

            ada_loads(0)
            u_hi(0); ada_loads(2); u_hi(1); ada_loads(2)
            v_hi("va", 0); v_hi("vb", 0); u_hi(2); ada_loads(2)
            v_hi("va", 1); v_hi("vb", 1); u_hi(3); ada_loads(2)
            v_hi("va", 2); v_hi("vb", 2); u_copy(0); ada_loads(2)
            v_hi("va", 3); v_hi("vb", 3)
            u_copy(1); ada_loads(2)
            pool_hi(0); u_copy(2)
            pool_hi(1); u_copy(3)
            w_next(BLK["c0"])
            pool_hi(2)
            w_next(BLK["c1"])
            pool_hi(3)
            w_next(BLK["s0"])
            w_next(BLK["s1"])
            for z in range(2):
                unit(f"dft{z}")
                nc.scalar.activation(h_hi[:, 4 + 2 * z:6 + 2 * z, 0:L],
                                     slot(UNIT[f"dft{z}"]).rearrange("p (h t) -> p h t", h=2), ACT.Copy).then_inc(hi_ready, 1)
            w_next(BLK["ctxdft"])
            unit("dftc")
            nc.scalar.activation(h_hi[:, 4:8, L:T], slot(UNIT["dftc"]).rearrange("p (h t) -> p h t", h=4),
                                 ACT.Copy).then_inc(hi_ready, 1)
            w_next(BLK["poolw"])
            for g in range(4):
                unit(("poolw", g))
                nc.scalar.activation(h_hi[:, g, :], slot(UNIT[("poolw", g)])[:, 0:T], ACT.Copy,
                                     scale=col(small, V_PS + g)).then_inc(hi_ready, 1)

            def trunk_squares(n, first_unit, m, i=None):
                nn, end = first_unit + m, T if n <= 2 else L
                turn = lambda step, v: v if i is None else i * step + v
                act.wait_ge(unit_free[nn % 4], turn(1, freed_before(nn) + 1))
                act.wait_ge(sumsq_added, turn(4, (KT + 1) * (n - 1) + 1 + m))
                nc.scalar.activation(tile_[m % 2][:, 0:end], tile3(x, turn(4, m))[:, 0:end], ACT.Square).then_inc(squared, 1)

            def out_phase(first_block, first_unit, n, ada_tiles=None):
                with act.Fori(0, KT // 4) as i:
                    for j in range(4):
                        act.wait_ge(unit_ready, i * 4 + (first_unit + j))
                        w_split(first_block + j + RING - 1, i)
                        if ada_tiles is not None:
                            for z in range(2):
                                t = ada_tiles + 2 * j + z
                                act.wait_ge(dots_ready, i * 16 + dots_after(t - 2))
                                act.dma_start(ada_raw[:, (t % 2) * BW:(t % 2 + 1) * BW],
                                              adaw[bass.ds(i * 8 + t, 1)].rearrange("o p n -> p (o n)")).then_inc(ada_landed[t % 2], 16)
                        if n is not None:
                            trunk_squares(n, first_unit, j, i)

            ada_loads(2)
            out_phase(BLK[("out", 0)], UNIT[("out", 0)], 1, 32)

            def ffn(l, streams):
                end = streams[-1][2]
                for gi, n in enumerate(GROUPS):
                    first_b, first_u = BLK[("up", l, gi, 0)], UNIT[("up", l, gi, 0)]
                    p0 = sum(GROUPS[:gi])
                    if gi == 0:
                        act.wait_ge(lo_ready, SPLIT[("h", 1 + 2 * l, KT - 1)] + 1)
                    with act.Fori(0, n // 2) as i:
                        for q in range(2):
                            for z in range(2):
                                j = 2 * q + z
                                nn = first_u + j
                                act.wait_ge(unit_ready, i * 4 + nn)
                                w_split(first_b + j + RING - 1, i)
                                if l == 0:
                                    ada_load(48 + 2 * p0 + j, i, both=gi == 0)
                                if z == 0:
                                    act.wait_ge(lo_ready, i * 2 + (SPLIT[("g", l, p0)] + q - 1))
                                act.wait_ge(unit_ready, i * 4 + (nn + 1))
                                ct = conv[l]
                                cc = i * 4 + (2 * p0 + j)
                                nc.scalar.activation(
                                    tile_[2 * q + z][:, 0:end], slot(nn)[:, 0:end], ACT.Identity,
                                    bias=ct[:, bass.ds(cc, 1), 3:4].rearrange("p a b -> p (a b)"),
                                    scale=ct[:, bass.ds(cc, 1), 1:2].rearrange("p a b -> p (a b)")).then_inc(center_tap, 1)
                            nn = first_u + 2 * q
                            act.wait_ge(unit_free[nn % 4], i + (freed_before(nn) + 1))
                            nc.scalar.activation(tile_[2 * q][:, 0:end], tile_[2 * q][:, 0:end], ACT.Silu).then_inc(silu_done, 1)
                            act.wait_ge(product_ready, i * 2 + (FT * l + p0 + q + 1))
                            nc.scalar.activation(g_hi[:, bass.ds(i * 2 + q, 1), 0:end].rearrange("p o n -> p (o n)"),
                                                 tile_[2 * q + 1][:, 0:end], ACT.Copy).then_inc(hi_ready, 1)
                    first_b, first_u = BLK[("down", l, gi, 0)], UNIT[("down", l, gi, 0)]
                    last = gi == len(GROUPS) - 1
                    if last and l == 1:
                        for m in range(KT):
                            if first_b + m + RING - 1 < NB:
                                act.wait_ge(unit_ready, first_u + m)
                                w_split(first_b + m + RING - 1)
                            trunk_squares(4, first_u, m)
                    else:
                        if last:
                            for t in range(4):
                                ada_load(92 + t)
                        out_phase(first_b, first_u, 2 if last else None)

            rms(1, STREAMS)
            h_hi_parts(1, STREAMS)
            ffn(0, STREAMS)
            rms(2, STREAMS)
            act.wait_ge(dots_ready, dots_after(95))
            act.dma_start(ada_raw[:, 0:NTAB], tabs).then_inc(tabs_landed, 16)
            h_hi_parts(2, STREAMS)

            def swap(i):
                act.wait_ge(head_gained, i + 1)
                for q in range(4):
                    dst, src = 32 * q, 32 * (q ^ 1)
                    act.dma_start(rotated[i % 2][dst:dst + 32, :], headbuf[i % 2][src:src + 32, 0:L]).then_inc(rot_landed[i % 2], 16)

            def head_in(i):
                kind, j = HEADS[i]
                n, end = UNIT[HEADS[i]], T if kind == "k" else L
                w_next(BLK[HEADS[i]])
                unit(HEADS[i])
                if i == 0:
                    act.wait_ge(lo_ready, SPLIT[("h", 2, KT - 1)] + 1)
                if i >= 2:
                    wait_part(act, HEADS[i - 2])
                nc.scalar.activation(headbuf[i % 2][:, 0:end], slot(n)[:, 0:end], ACT.Copy,
                                     scale=col(small, V_KG if kind == "k" else V_QG)).then_inc(head_gained, 1)
                if i >= 1:
                    act.wait_ge(unit_ready, UNIT[("ss", i - 1)] + 1)
                nc.scalar.activation(head_sq[:, 0:end], slot(n)[:, 0:end], ACT.Square).then_inc(head_squared, 1)
                swap(i)

            def head_root(i):
                n, end = UNIT[("ss", i)], T if HEADS[i][0] == "k" else L
                unit(("ss", i))
                if i >= 1:
                    act.wait_ge(head_ready, i)
                nc.scalar.activation(head_inv[:, 0:end], slot(n)[:, 0:end], ACT.Sqrt, bias=eps,
                                     scale=1.0 / DH).then_inc(head_rms, 1)

            def head_hi(i):
                kind, j = HEADS[i]
                end = T if kind == "k" else L
                act.wait_ge(head_ready, i + 1)
                dst = kk[0][:, j, :] if kind == "k" else qo[0][:, j, :]
                nc.scalar.activation(dst, headbuf[i % 2][:, 0:end], ACT.Copy).then_inc(hi_ready, 1)

            def v_part(z):
                n, t0, nt = UNIT[f"v{z}"], 4 * z, 4 - 2 * z
                unit(f"v{z}")
                nc.scalar.activation(v_[0][:, t0:t0 + nt, :], slot(n)[:, 0:nt * C].rearrange("p (t c) -> p t c", t=nt),
                                     ACT.Copy).then_inc(hi_ready, 1)

            head_in(0)
            head_in(1)
            w_next(BLK[("v", 0)])
            head_root(0)
            head_hi(0)
            v_part(0)
            head_root(1)
            head_hi(1)
            v_part(1)
            w_next(BLK[("v", 1)])
            for h in range(NH):
                head_in(2 + h)
                if h:
                    head_root(1 + h)
                    head_hi(1 + h)
            head_root(NH + 1)
            head_hi(NH + 1)

            scale = float(DH) ** -0.5

            def exps(i):
                act.wait_ge(max_ready, i + 1)
                if i >= 2:
                    unit(("t", i - 2))
                nc.scalar.activation(probs[i % 2], slot(UNIT[("s", i)])[:, 0:T], ACT.Exp, bias=stat[:, i % 4, 0:1],
                                     scale=scale, accum_out=stat[:, i % 4, 1:2]).then_inc(exp_ready, 1)

            def t_hi(i):
                unit(("t", i))
                h, qt = i // 4, i % 4
                if qt == 0 and h >= 2:
                    unit(("pv", h - 2))
                nc.scalar.activation(pt[0][:, h % 2, :, qt * P:(qt + 1) * P],
                                     slot(UNIT[("t", i)])[:, 0:T].rearrange("p (k q) -> p k q", k=6), ACT.Copy).then_inc(hi_ready, 1)

            n = NH * 4
            for i in range(n + 3):
                if i < n:
                    exps(i)
                if 2 <= i < n + 2:
                    t_hi(i - 2)
                if i >= 6 and (i - 6) % 4 == 0:
                    h = (i - 6) // 4
                    unit(("pv", h))
                    nc.scalar.activation(qo[0][:, h, :], slot(UNIT[("pv", h)])[:, 0:L], ACT.Copy).then_inc(hi_ready, 1)
            out_phase(BLK[("o", 0)], UNIT[("o", 0)], 3)
            rms(3, LATENT)
            h_hi_parts(3, LATENT)
            ffn(1, LATENT)
            rms(4, LATENT)
            for k in range(KT):
                act.wait_ge(scaled, KT * 4 + k + 1)
                act.dma_start(out[:, k, :], x[:, k, 0:L]).then_inc(out_stored, 16)
            act.wait_ge(out_stored, 16 * KT)

        @block.tensor
        def _(pe):
            def claim(n, i=None):
                if i is not None:
                    pe.wait_ge(unit_free[n % 4], i + freed_before(n))
                elif n >= 4:
                    pe.wait_ge(*released(n - 4))

            def claim_ahead(n):
                for m in range(n - 4, n):
                    if m not in FREED:
                        pe.wait_ge(*released(m))

            def weights(b, i=None):
                pe.wait_ge(w_lo_ready, b + 1 if i is None else i * RING + (b + 1))

            def mm3(dst, w, a, start, stop):
                nc.tensor.matmul(dst, w[0], a[0], start=start, stop=False)
                nc.tensor.matmul(dst, w[0], a[1], start=False, stop=False)
                return nc.tensor.matmul(dst, w[1], a[0], start=False, stop=stop)

            def wtile(b, k, m=P):
                return [w[:, b % RING, k * m:(k + 1) * m] for w in (w_hi, w_lo)]

            def ones_sum(n, src, spans, start=True, stop=True):
                for a, e in spans:
                    ins = nc.tensor.matmul(slot(n)[:, a:e], ones, src[:, a:e], start=start, stop=stop)
                return ins

            spans = lambda streams: [(a, e) for _, a, e in streams]

            def out_tile(n, b, src, ks, streams, parts=None, i=None, per_k=None):
                claim(n, i)
                weights(b, i)
                for kx, k in enumerate(ks):
                    if per_k is not None:
                        pe.wait_ge(lo_ready, per_k(kx))
                    for a, e in spans(streams):
                        ins = mm3(slot(n)[:, a:e], wtile(b, kx), [s[:, k, a:e] for s in src], kx == 0, kx == len(ks) - 1)
                ins.then_inc(unit_ready, 1)

            h_, g_ = (h_hi, h_lo), (g_hi, g_lo)
            pe.wait_ge(eps_ready, 2)
            for k in range(KT):
                pe.wait_ge(squared, k + 1)
                for a, e in spans(STREAMS):
                    ins = nc.tensor.matmul(slot(0)[:, a:e], ones, tile_[k % 2][:, a:e], start=k == 0, stop=k == KT - 1)
                ins.then_inc(square_used if k < KT - 1 else unit_ready, 1)

            weights(BLK["df"])
            n = UNIT["ab"]
            for z in range(2):
                ins = mm3(slot(n)[:, z * L:(z + 1) * L], wtile(BLK["df"], z),
                          [w[:, BLK["df"] % RING, 2 * P:2 * P + L] for w in (w_hi, w_lo)], True, True)
            ins.then_inc(unit_ready, 1)

            def v_units(h):
                wait_part(pe, ("u", h))
                if h == 0:
                    wait_part(pe, "ab")
                for kind, tiles in (("va", range(4)), ("vb", range(4, 6))):
                    n = UNIT[(kind, h)]
                    claim(n)
                    for c, t in enumerate(tiles):
                        ins = mm3(slot(n)[:, c * C:(c + 1) * C], [u[:, t * P:(t + 1) * P] for u in u_part],
                                  [a[:, h, :] for a in ab], True, True)
                    ins.then_inc(unit_ready, 1)

            def h_tile(name, b, n_norm=None):
                per_k = None
                if n_norm is not None:
                    per_k = lambda k: SPLIT[("h", n_norm, k)] + 1
                out_tile(UNIT[name], b, h_, range(KT), STREAMS, per_k=per_k)

            h_tile(("four", 0), BLK[("four", 0)], 0)
            h_tile(("four", 1), BLK[("four", 1)])
            v_units(0)
            h_tile(("four", 2), BLK[("four", 2)])
            v_units(1)
            h_tile(("four", 3), BLK[("four", 3)])
            v_units(2)
            h_tile(("pin", 0), BLK[("pin", 0)])
            v_units(3)
            for g in (1, 2, 3):
                h_tile(("pin", g), BLK[("pin", g)])
            wait_part(pe, ("vb", 3))
            claim(UNIT["dft0"])
            claim(UNIT["dft1"])
            for bx, b in enumerate(("c0", "c1", "s0", "s1")):
                weights(BLK[b])
                z = bx // 2
                for h in range(4):
                    for y in range(2):
                        t = 2 * (bx % 2) + y
                        ins = mm3(slot(UNIT[f"dft{h // 2}"])[:, (h % 2) * L:(h % 2 + 1) * L],
                                  [v[:, t, h, z * P:(z + 1) * P] for v in vv], wtile(BLK[b], y, L),
                                  bx == 0 and y == 0, bx == 3 and y == 1)
                        if bx == 3 and y == 1 and h == 1:
                            ins.then_inc(unit_ready, 1)
                if bx < 3:
                    ins.then_inc(dft_block_used, 1)
            ins.then_inc(unit_ready, 1)
            n, b = UNIT["dftc"], BLK["ctxdft"]
            claim(n)
            weights(b)
            for h in range(4):
                for q in range(4):
                    z, t = q // 2, q % 2
                    ins = mm3(slot(n)[:, h * C:(h + 1) * C], [v[:, 4 + t, h, z * P:(z + 1) * P] for v in vv],
                              wtile(b, q, C), q == 0, q == 3)
            ins.then_inc(unit_ready, 1)
            weights(BLK["poolw"])
            for g in range(4):
                n = UNIT[("poolw", g)]
                claim(n)
                wait_part(pe, ("pool", g))
                for a, e in spans(STREAMS):
                    ins = mm3(slot(n)[:, a:e], wtile(BLK["poolw"], g), [s[:, g, a:e] for s in h_], True, True)
                ins.then_inc(unit_ready, 1)

            def out_phase(b, n, src, nk, streams, per_k):
                claim_ahead(n)
                with pe.Fori(0, KT // 4) as i:
                    for j in range(4):
                        out_tile(n + j, b + j, src, range(nk), streams, i=i, per_k=per_k if j == 0 else None)

            def norm_sum(nn, streams):
                n = UNIT[f"n{nn}"]
                claim(n)
                pe.wait_ge(sumsq_added, (KT + 1) * nn)
                for a, e in spans(streams):
                    ins = nc.tensor.matmul(slot(n)[:, a:e], ones, tile_[2][:, a:e], start=True, stop=True)
                ins.then_inc(unit_ready, 1)

            out_phase(BLK[("out", 0)], UNIT[("out", 0)], h_, KT, STREAMS, lambda k: SPLIT[("y", 3)] + 1)
            norm_sum(1, STREAMS)

            def ffn(l, streams):
                for gi, ng in enumerate(GROUPS):
                    b, n = BLK[("up", l, gi, 0)], UNIT[("up", l, gi, 0)]
                    p0 = sum(GROUPS[:gi])
                    per_k = (lambda k: SPLIT[("h", 1 + 2 * l, k)] + 1) if gi == 0 else None
                    claim_ahead(n)
                    with pe.Fori(0, ng // 2) as i:
                        for j in range(4):
                            out_tile(n + j, b + j, h_, range(KT), streams, i=i, per_k=per_k if j == 0 else None)
                    out_phase(BLK[("down", l, gi, 0)], UNIT[("down", l, gi, 0)], g_, ng, streams,
                              lambda k: SPLIT[("g", l, p0)] + k + 1)

            ffn(0, STREAMS)
            norm_sum(2, STREAMS)

            def head_sum(i):
                n, end = UNIT[("ss", i)], T if HEADS[i][0] == "k" else L
                claim(n)
                pe.wait_ge(head_squared, i + 1)
                for a, e in ((0, L), (L, T))[:1 + (end == T)]:
                    ins = nc.tensor.matmul(slot(n)[:, a:e], ones, head_sq[:, a:e], start=True, stop=True)
                ins.then_inc(unit_ready, 1)

            def v_tiles(z):
                n = UNIT[f"v{z}"]
                claim(n)
                weights(BLK[("v", 1)])
                for c, t in enumerate(range(4 * z, 6 if z else 4)):
                    for k in range(KT):
                        ins = mm3(slot(n)[:, c * C:(c + 1) * C], [s[:, k, t * P:(t + 1) * P] for s in h_],
                                  wtile(BLK[("v", k // 4)], k % 4, C), k == 0, k == KT - 1)
                ins.then_inc(unit_ready, 1)

            h_tile(("k", 0), BLK[("k", 0)], 2)
            h_tile(("k", 1), BLK[("k", 1)])
            head_sum(0)
            v_tiles(0)
            head_sum(1)
            v_tiles(1)
            for h in range(NH):
                out_tile(UNIT[("q", h)], BLK[("q", h)], h_, range(KT), LATENT)
                if h:
                    head_sum(1 + h)
            head_sum(NH + 1)

            def scores(i):
                n, h, qt = UNIT[("s", i)], i // 4, i % 4
                claim(n)
                wait_part(pe, ("q", h))
                for a, e in spans(STREAMS):
                    ins = mm3(slot(n)[:, a:e], [q[:, h, qt * P:(qt + 1) * P] for q in qo],
                              [k[:, h // GQA, a:e] for k in kk], True, True)
                ins.then_inc(unit_ready, 1)

            def transposes(i):
                n = UNIT[("t", i)]
                claim(n)
                pe.wait_ge(probs_ready, i + 1)
                if i == 0:
                    pe.wait_ge(tabs_landed, 16)
                for k in range(6):
                    ins = nc.tensor.transpose(slot(n)[:, k * P:(k + 1) * P], probs[i % 2][:, k * P:(k + 1) * P], ident)
                ins.then_inc(unit_ready, 1)

            def weighted(h):
                n = UNIT[("pv", h)]
                claim(n)
                wait_part(pe, ("t", 4 * h + 3))
                for k in range(6):
                    ins = mm3(slot(n)[:, 0:L], [v[:, k, (h // GQA) * DH:(h // GQA + 1) * DH] for v in v_],
                              [p[:, h % 2, k, :] for p in pt], k == 0, k == 5)
                ins.then_inc(unit_ready, 1)

            n = NH * 4
            for i in range(n + 3):
                if i < n:
                    scores(i)
                if 2 <= i < n + 2:
                    transposes(i - 2)
                if i >= 6 and (i - 6) % 4 == 0:
                    weighted((i - 6) // 4)
            out_phase(BLK[("o", 0)], UNIT[("o", 0)], qo, NH, LATENT, lambda k: SPLIT[("pv", k)] + 1)
            norm_sum(3, LATENT)
            ffn(1, LATENT)
            norm_sum(4, LATENT)

        @block.vector
        def _(dve):
            V = nc.vector

            def unit(name):
                dve.wait_ge(unit_ready, UNIT[name] + 1)

            for z in range(4):
                V.memset(stat[:, z, :], 0.0).then_inc(unit_free[z], 1)

            def ada_tile(t, j, both, i=None, per=4):
                turns = 0 if i is None else i * (16 * per // 2)
                dve.wait_ge(ada_landed[t % 2], 16 * (t // 2 + 1) + turns)
                w = ada_raw[:, (t % 2) * BW:(t % 2 + 1) * BW]
                if t % 4 == 0 and t:
                    dve.wait_ge(mods_ready, t // 4 if i is None else i * (per // 4) + t // 4)
                for s in range(1 + both):
                    n = dots_after(t, both) - both + s
                    if n > 1:
                        dve.wait_ge(dots_ready, n - 1 if i is None else i * (per * (1 + both)) + (n - 1))
                    V.tensor_tensor_reduce(junk[:, :], w, cond[:, s * BW:(s + 1) * BW], 1.0, 0.0, ALU.mult,
                                           ALU.add, ada_acc[:, j, s:s + 1]).then_inc(dots_ready, 1)

            def ada_add(t0, both, i=None, per=4):
                n = dots_after(t0 + 3, both)
                dve.wait_ge(dots_ready, n if i is None else i * (per * (1 + both)) + n)
                tt = t0 if i is None else i * per + t0
                for s in range(1 + both):
                    ins = V.tensor_tensor(mods[:, bass.ds(tt, 4), s], ada_acc[:, :, s],
                                          small[:, bass.ds(V_ADAB + tt, 4)], ALU.add)
                ins.then_inc(mods_ready, 1)

            def gain(n, streams):
                dve.wait_ge(mods_ready, (SHIFT[n] + 2 * KT) // 4)
                for s, _, _ in streams:
                    ins = V.scalar_tensor_tensor(gains[:, n, :, s], mods[:, SHIFT[n] + KT:SHIFT[n] + 2 * KT, s], 1.0,
                                                 small[:, NORM_G[n]:NORM_G[n] + KT], ALU.add, ALU.mult)
                ins.then_inc(gain_ready, 1)

            def rstd(n, end):
                dve.wait_ge(rms_ready, n + 1)
                V.reciprocal(tile_[3][:, 0:end], tile_[3][:, 0:end]).then_inc(rstd_ready, 1)

            def norm(n, streams):
                end = streams[-1][2]
                rstd(n, end)
                dve.wait_ge(rstd_ready, n + 1)
                dve.wait_ge(gain_ready, n + 1)

                def scale_x(k):
                    if k >= 2:
                        dve.wait_ge(lo_ready, SPLIT[("h", n, k - 2)] + 1)
                    for s, a, e in streams:
                        ins = V.scalar_tensor_tensor(tile_[k % 2][:, a:e], x[:, k, a:e], gains[:, n, k, s:s + 1],
                                                     tile_[3][:, a:e], ALU.mult, ALU.mult)
                    ins.then_inc(scaled, 1)

                scale_x(0)
                for k in range(KT):
                    if k + 1 < KT:
                        scale_x(k + 1)
                    dve.wait_ge(hi_ready, SPLIT[("h", n, k)] + 1)
                    for s, a, e in streams:
                        ins = V.scalar_tensor_tensor(h_lo[:, k, a:e], tile_[k % 2][:, a:e], mods[:, SHIFT[n] + k, s:s + 1],
                                                     h_hi[:, k, a:e].bitcast(F32), ALU.add, ALU.subtract)
                    ins.then_inc(lo_ready, 1)

            dve.wait_ge(vecs_landed, 16)
            dve.wait_ge(cond_ready, 1)
            for t0 in range(0, 16, 4):
                for j in range(4):
                    ada_tile(t0 + j, j, True)
                ada_add(t0, True)
            gain(0, STREAMS)
            norm(0, STREAMS)
            dve.wait_ge(lo_ready, SPLIT[("h", 0, KT - 1)] + 1)
            for z in range(2):
                V.memset(upad[z], 0.0).then_inc(pads_ready, 1)

            def lo_of(name, dst, src, hi, n=None):
                dve.wait_ge(hi_ready, SPLIT[name] + 1)
                V.tensor_tensor(dst, src, hi.bitcast(F32), ALU.subtract).then_inc(lo_ready, 1)

            ada = iter(range(16, 32))

            def ada_tiles(count):
                for _ in range(count):
                    t = next(ada, None)
                    if t is None:
                        return
                    ada_tile(t, t % 4, True)
                    if t % 4 == 3:
                        ada_add(t - 3, True)

            n = UNIT["ab"]
            dve.wait_ge(hi_ready, SPLIT["ab"] + 1)
            for z in range(2):
                ins = V.tensor_tensor(ab[1][:, :, z * P:(z + 1) * P],
                                      slot(n)[:, z * L:(z + 1) * L].rearrange("p (h c) -> p h c", h=4),
                                      ab[0][:, :, z * P:(z + 1) * P].bitcast(F32), ALU.subtract)
            ins.then_inc(lo_ready, 1)

            def u_lo(h):
                n = UNIT[("four", h)]
                lo_of(("u", h), u_part[1], slot(n)[:, 0:T], u_part[0])
    
            def v_lo(kind, h):
                n = UNIT[(kind, h)]
                t0, nt = (0, 4) if kind == "va" else (4, 2)
                lo_of((kind, h), vv[1][:, t0:t0 + nt, h, :], slot(n)[:, 0:nt * C].rearrange("p (t c) -> p t c", t=nt),
                      vv[0][:, t0:t0 + nt, h, :])
    
            steps = [0]

            def step(ins):
                ins.then_inc(window_step, 1)
                steps[0] += 1

            def pool_group(g):
                u, a, b = upad[g % 2], upad[2], upad[3]
                n = UNIT[("pin", g)]
                dve.wait_ge(u_copied, g + 1)
                if g:
                    dve.wait_ge(pooled, g)
                dve.wait_ge(*released(n))
                step(V.tensor_tensor(a[:, 1:UW], u[:, 0:UW - 1], u[:, 1:UW], ALU.add))
                src, dst, lo, hi = a, b, 1, UW
                for q in range(g):
                    d = 1 << q
                    dve.wait_ge(window_step, steps[0])
                    step(V.tensor_tensor(dst[:, lo + d:hi - d], src[:, lo:hi - 2 * d], src[:, lo + 2 * d:hi], ALU.add))
                    src, dst, lo, hi = dst, src, lo + d, hi - d
                dve.wait_ge(window_step, steps[0])
                for e0, side in ((UL, 0), (UL + L - PAD, 1), (UC, 0), (UC + C - PAD, 1)):
                    ins = V.tensor_tensor(src[:, e0:e0 + PAD], src[:, e0:e0 + PAD], edge[:, g, side, :], ALU.mult)
                step(ins)
                dve.wait_ge(window_step, steps[0])
                for e0, m in ((UL, L), (UC, C)):
                    ins = V.scalar_tensor_tensor(u[:, e0:e0 + m], src[:, e0:e0 + m], 1.0 / (2 << g), u[:, e0:e0 + m],
                                                 ALU.mult, ALU.subtract)
                ins.then_inc(pooled, 1)

            def pool_lo(g):
                dve.wait_ge(hi_ready, SPLIT[("pool", g)] + 1)
                for e0, a, m in ((UL, 0, L), (UC, L, C)):
                    ins = V.tensor_tensor(h_lo[:, g, a:a + m], upad[g % 2][:, e0:e0 + m], h_hi[:, g, a:a + m].bitcast(F32),
                                          ALU.subtract)
                ins.then_inc(lo_ready, 1)

            u_lo(0); ada_tiles(2); u_lo(1); ada_tiles(2)
            v_lo("va", 0); v_lo("vb", 0); u_lo(2); ada_tiles(2)
            v_lo("va", 1); v_lo("vb", 1); u_lo(3); ada_tiles(2)
            v_lo("va", 2); v_lo("vb", 2); ada_tiles(2)
            v_lo("va", 3); v_lo("vb", 3); ada_tiles(2)
            unit(("pin", 3))
            for g in range(4):
                pool_group(g)
                pool_lo(g)
            for z in range(2):
                n = UNIT[f"dft{z}"]
                lo_of(f"dft{z}", h_lo[:, 4 + 2 * z:6 + 2 * z, 0:L], slot(n).rearrange("p (h t) -> p h t", h=2),
                      h_hi[:, 4 + 2 * z:6 + 2 * z, 0:L])
                n = UNIT["dftc"]
            lo_of("dftc", h_lo[:, 4:8, L:T], slot(n).rearrange("p (h t) -> p h t", h=4), h_hi[:, 4:8, L:T])
            for g in range(4):
                n = UNIT[("poolw", g)]
                dve.wait_ge(hi_ready, SPLIT[("y", g)] + 1)
                V.scalar_tensor_tensor(h_lo[:, g, :], slot(n)[:, 0:T], col(small, V_PS + g), h_hi[:, g, :].bitcast(F32),
                                       ALU.mult, ALU.subtract).then_inc(lo_ready, 1)
                ada_tiles(4)

            def add_square(n, m, i=None):
                turn = lambda step, v: v if i is None else i * step + v
                end = T if n <= 2 else L
                dve.wait_ge(squared, turn(4, KT * n + m + 1))
                dve.wait_ge(sumsq_added, turn(4, (KT + 1) * (n - 1) + 1 + m))
                V.tensor_tensor(tile_[2][:, 0:end], tile_[2][:, 0:end], tile_[m % 2][:, 0:end], ALU.add).then_inc(sumsq_added, 1)

            def update(nn, gate, m, streams, i=None):
                turn = lambda step, v: v if i is None else i * step + v
                dve.wait_ge(unit_ready, turn(4, nn + 1))
                xm = tile3(x, turn(4, m))
                for s, a, e in streams:
                    g = mods[:, bass.ds(turn(4, gate + m), 1), s]
                    ins = V.scalar_tensor_tensor(xm[:, a:e], slot(nn)[:, a:e], g, xm[:, a:e], ALU.mult, ALU.add)
                ins.then_inc(unit_free[nn % 4], 1)

            def out_phase(first_unit, gate, streams, n, ada_tiles=None):
                dve.wait_ge(mods_ready, gate // 4 + 2)
                if n is not None:
                    if n == 3:
                        dve.wait_ge(probs_ready, NH * 4)
                        dve.wait_ge(head_ready, len(HEADS))
                    else:
                        dve.wait_ge(lo_ready, {1: SPLIT[("y", 3)], 2: SPLIT[("g", 0, FT - 1)], 4: SPLIT[("g", 1, FT - 1)]}[n] + 1)
                    V.memset(tile_[2], 0.0).then_inc(sumsq_added, 1)
                with dve.Fori(0, KT // 4) as i:
                    for j in range(4):
                        if ada_tiles is not None:
                            for z in range(2):
                                t = ada_tiles + 2 * j + z
                                ada_tile(t, t % 4, True, i, 8)
                            if j % 2:
                                ada_add(ada_tiles + 4 * (j // 2), True, i, 8)
                        update(first_unit + j, gate, j, streams, i)
                        if n is not None:
                            add_square(n, j, i)

            def ffn(l, streams):
                ct = conv[l]
                for gi, ng in enumerate(GROUPS):
                    first_u = UNIT[("up", l, gi, 0)]
                    p0 = sum(GROUPS[:gi])
                    with dve.Fori(0, ng // 2) as i:
                        for q in range(2):
                            for z in range(2):
                                j = 2 * q + z
                                nn, t = first_u + j, tile_[j]
                                v = 2 * (FT * l + p0) + j
                                dve.wait_ge(center_tap, i * 4 + (v + 1))
                                w0, w2 = (ct[:, bass.ds(i * 4 + (2 * p0 + j), 1), c:c + 1].rearrange("p a b -> p (a b)") for c in (0, 2))
                                for _, a, e in streams:
                                    ins = V.scalar_tensor_tensor(t[:, a + 1:e], slot(nn)[:, a:e - 1], w0, t[:, a + 1:e],
                                                                 ALU.mult, ALU.add)
                                ins.then_inc(left_tap, 1)
                                dve.wait_ge(left_tap, i * 4 + (v + 1))
                                for _, a, e in streams:
                                    ins = V.scalar_tensor_tensor(t[:, a:e - 1], slot(nn)[:, a + 1:e], w2, t[:, a:e - 1],
                                                                 ALU.mult, ALU.add)
                                ins.then_inc(unit_free[nn % 4], 1)
                                if l == 0:
                                    ada_tile(48 + 2 * p0 + j, j, gi == 0, i)
                            if l == 0 and q == 1:
                                ada_add(48 + 2 * p0, gi == 0, i)
                            p = FT * l + p0 + q
                            nn = first_u + 2 * q + 1
                            dve.wait_ge(silu_done, i * 2 + (p + 1))
                            dve.wait_ge(unit_free[nn % 4], i + (freed_before(nn) + 1))
                            end = streams[-1][2]
                            V.tensor_tensor(tile_[2 * q + 1][:, 0:end], tile_[2 * q][:, 0:end], tile_[2 * q + 1][:, 0:end],
                                            ALU.mult).then_inc(product_ready, 1)
                            dve.wait_ge(hi_ready, i * 2 + (SPLIT[("g", l, p0)] + q + 1))
                            V.tensor_tensor(tile3(g_lo, i * 2 + q)[:, 0:end], tile_[2 * q + 1][:, 0:end],
                                            tile3(g_hi, i * 2 + q)[:, 0:end].bitcast(F32), ALU.subtract).then_inc(lo_ready, 1)
                    first_u, last = UNIT[("down", l, gi, 0)], gi == len(GROUPS) - 1
                    if last and l == 0:
                        for t in range(92, 96):
                            ada_tile(t, t % 4, False)
                        ada_add(92, False)
                    out_phase(first_u, GATE[("ffn", l)], streams, 2 + 2 * l if last else None)

            out_phase(UNIT[("out", 0)], GATE[("mixer", 0)], STREAMS, 1, 32)
            gain(1, STREAMS)
            norm(1, STREAMS)
            ffn(0, STREAMS)
            gain(2, STREAMS)
            norm(2, STREAMS)

            def head(i):
                kind_, j = HEADS[i]
                end, buf = T if kind_ == "k" else L, headbuf[i % 2]
                dve.wait_ge(head_gained, i + 1)
                dve.wait_ge(rot_landed[i % 2], 64 * (i // 2 + 1))
                if i == 0:
                    dve.wait_ge(tabs_landed, 16)
                if i:
                    dve.wait_ge(rope_step, 3 * i)
                V.tensor_tensor(head_sin, rotated[i % 2], sin, ALU.mult).then_inc(rope_step, 1)
                V.tensor_tensor(buf[:, 0:L], buf[:, 0:L], cos, ALU.mult).then_inc(rope_step, 1)
                dve.wait_ge(rope_step, 3 * i + 2)
                V.tensor_tensor(buf[:, 0:L], buf[:, 0:L], head_sin, ALU.add).then_inc(rope_step, 1)
                dve.wait_ge(head_rms, i + 1)
                V.reciprocal(head_inv[:, 0:end], head_inv[:, 0:end]).then_inc(head_rstd, 1)
                dve.wait_ge(head_rstd, i + 1)
                dve.wait_ge(rope_step, 3 * i + 3)
                V.tensor_tensor(buf[:, 0:end], buf[:, 0:end], head_inv[:, 0:end], ALU.mult).then_inc(head_ready, 1)
                dst, hi = (kk[1][:, j, :], kk[0][:, j, :]) if kind_ == "k" else (qo[1][:, j, :], qo[0][:, j, :])
                lo_of(HEADS[i], dst, buf[:, 0:end], hi)

            def v_lo_part(z):
                n, t0, nt = UNIT[f"v{z}"], 4 * z, 4 - 2 * z
                lo_of(f"v{z}", v_[1][:, t0:t0 + nt, :], slot(n)[:, 0:nt * C].rearrange("p (t c) -> p t c", t=nt),
                      v_[0][:, t0:t0 + nt, :])

            head(0)
            v_lo_part(0)
            head(1)
            v_lo_part(1)
            for h in range(NH):
                head(2 + h)

            scale = float(DH) ** -0.5

            def row_max(i):
                unit(("s", i))
                r = stat[:, i % 4, :]
                V.reduce_max(r[:, 3:4], slot(UNIT[("s", i)])[:, 0:T], AX_X).then_inc(max_found, 1)
                dve.wait_ge(max_found, i + 1)
                V.tensor_scalar(r[:, 0:1], r[:, 3:4], -scale, None, ALU.mult).then_inc(max_ready, 1)

            def normalise(i):
                dve.wait_ge(exp_ready, i + 1)
                r = stat[:, i % 4, :]
                V.reciprocal(r[:, 2:3], r[:, 1:2]).then_inc(inv_ready, 1)
                dve.wait_ge(inv_ready, i + 1)
                V.tensor_scalar(probs[i % 2], probs[i % 2], r[:, 2:3], None, ALU.mult).then_inc(probs_ready, 1)

            n = NH * 4
            for i in range(n + 3):
                if i < n:
                    row_max(i)
                if 1 <= i <= n:
                    normalise(i - 1)
                if 2 <= i < n + 2:
                    k = i - 2
                    cols = slice(k % 4 * P, (k % 4 + 1) * P)
                    lo_of(("t", k), pt[1][:, k // 4 % 2, :, cols],
                          slot(UNIT[("t", k)])[:, 0:T].rearrange("p (k q) -> p k q", k=6), pt[0][:, k // 4 % 2, :, cols])
                if i >= 6 and (i - 6) % 4 == 0:
                    h = (i - 6) // 4
                    lo_of(("pv", h), qo[1][:, h, :], slot(UNIT[("pv", h)])[:, 0:L], qo[0][:, h, :])
            out_phase(UNIT[("o", 0)], GATE[("mixer", 1)], LATENT, 3)
            gain(3, LATENT)
            norm(3, LATENT)
            ffn(1, LATENT)
            rstd(4, L)
            dve.wait_ge(rstd_ready, 5)
            for k in range(KT):
                V.scalar_tensor_tensor(x[:, k, 0:L], x[:, k, 0:L], col(small, V_FG + k), tile_[3][:, 0:L],
                                       ALU.mult, ALU.mult).then_inc(scaled, 1)




def dft(n):
    a = 2 * np.pi * (np.outer(np.arange(n), np.arange(n)) % n) / n
    return np.cos(a), np.sin(a)


def window_edges():
    e = np.ones((4, 2, PAD))
    for g in range(4):
        w = 2 << g
        for side, ts in enumerate((range(PAD), range(L - PAD, L))):
            for c, t in enumerate(ts):
                e[g, side, c] = w / (min(t + w - w // 2, L) - max(t - w // 2, 0))
    return e.astype(np.float32)


def rotary():
    pairs = DH // 4
    freqs = np.float32(10000.0) ** (-np.arange(pairs, dtype=np.float32) / np.float32(pairs))
    t = np.arange(L)
    ang = [(p.astype(np.float32)[:, None] * freqs[None, :]).T.astype(np.float64) for p in (t // GRID_W, t % GRID_W)]
    cos = np.concatenate([np.cos(ang[0])] * 2 + [np.cos(ang[1])] * 2)
    sin = np.concatenate([-np.sin(ang[0]), np.sin(ang[0]), -np.sin(ang[1]), np.sin(ang[1])])
    return cos.astype(np.float32), sin.astype(np.float32)


def by_partition(v):
    return np.asarray(v).reshape(-1, P).T


def lay_out(x, c, ctx, c_ctx, ada_w, ada_b, norm1_g, norm2_g, pf_w_in, pool_w, pool_scale, fourier_w, pf_w_out,
            attn_w_qkv, q_norm_g, k_norm_g, attn_w_o, ffn_w_up, ffn_conv_w, ffn_conv_b, ffn_w_down, final_g):
    f = np.float32
    feature_tiles = lambda a: a.T.reshape(KT, P, -1).transpose(1, 0, 2)
    xt = np.concatenate([feature_tiles(x[0]), feature_tiles(ctx[0])], axis=2)
    cvec = np.ascontiguousarray(np.broadcast_to(np.concatenate([c[0], c_ctx])[None], (P, 2 * D)))
    adaw = np.concatenate([ada_w[l].T.reshape(-1, P, D) for l in range(2)])

    w = np.zeros((NB, P, BW), f)

    def put(name, tile):
        t = tile.reshape(P, -1)
        w[BLK[name], :, :t.shape[1]] = t

    def column_block(a, m, width=P):
        return a[:, m * width:(m + 1) * width].reshape(-1, P, width).transpose(1, 0, 2)

    cc, ss = dft(DH)
    heads = lambda a: a.transpose(1, 0, 2).reshape(P, -1)
    put("df", np.concatenate([cc.astype(f), (-ss).astype(f), heads(fourier_w[0])], axis=1))
    put("poolw", heads(pool_w[0]))
    for h in range(4):
        put(("four", h), column_block(pf_w_in[0], 4 + h))
        put(("pin", h), column_block(pf_w_in[0], h))
    for n, names in ((L, ("c0", "c1", "s0", "s1")), (C, ("ctxdft",))):
        m = [(t / np.sqrt(n * DH)).astype(f).reshape(n // P, P, n).transpose(1, 0, 2).reshape(P, -1) for t in dft(n)]
        m = np.concatenate(m, axis=1)
        for b, name in enumerate(names):
            put(name, m[:, b * BW:(b + 1) * BW])
    qkv = attn_w_qkv[0]
    kv = qkv[:, NH * DH:]
    for m in range(KT):
        put(("out", m), column_block(pf_w_out[0], m))
        put(("q", m), column_block(qkv, m))
        put(("o", m), column_block(attn_w_o[0], m))
    for j in range(NKV):
        put(("k", j), column_block(kv, j))
        put(("v", j), column_block(kv[:, NKV * DH:], 0, NKV * DH)[:, 4 * j:4 * j + 4])
    convs = []
    for l in range(2):
        for gi, n in enumerate(GROUPS):
            p0 = sum(GROUPS[:gi])
            for i in range(2 * n):
                put(("up", l, gi, i), column_block(ffn_w_up[l], p0 + i // 2 + FT * (i % 2)))
            for m in range(KT):
                put(("down", l, gi, m), column_block(ffn_w_down[l][p0 * P:(p0 + n) * P], m))
        taps = np.concatenate([ffn_conv_w[l], ffn_conv_b[l][None]]).reshape(4, 2, FT, P)
        convs.append(taps.transpose(3, 2, 1, 0).reshape(P, -1))
    edges = np.broadcast_to(window_edges().reshape(1, -1), (P, 64))
    vecs = np.concatenate([by_partition(ada_b), by_partition(norm1_g), by_partition(norm2_g), by_partition(final_g),
                           by_partition(pool_scale), by_partition(q_norm_g), by_partition(k_norm_g), edges, convs[0]], axis=1)
    cos, sin = rotary()
    tabs = np.concatenate([cos, sin, np.eye(P, dtype=f), convs[1]], axis=1)
    assert vecs.shape[1] == NVEC and tabs.shape[1] == NTAB
    return {"xt": xt, "cvec": cvec, "wstream": w, "adaw": adaw, "vecs": vecs, "tabs": tabs}


def kernel(**inputs):
    import concourse.bacc as bacc
    from concourse.bass_utils import run_bass_kernel_spmd

    arrays = {k: np.ascontiguousarray(v) for k, v in lay_out(**{k: np.asarray(v) for k, v in inputs.items()}).items()}
    nc = bacc.Bacc("TRN2", target_bir_lowering=False, num_devices=1)
    args = [nc.dram_tensor(k, a.shape, F32, kind="ExternalInput").ap() for k, a in arrays.items()]
    out = nc.dram_tensor("out", (P, KT, L), F32, kind="ExternalOutput").ap()
    program(nc, *args, out)
    got = run_bass_kernel_spmd(nc, [arrays], core_ids=[0]).results[0]["out"]
    return np.ascontiguousarray(got.transpose(2, 1, 0).reshape(1, L, D))
```

```python
from contextlib import ExitStack

import concourse.bass as bass
import numpy as np
from concourse import mybir

F32 = mybir.dt.float32
F32R = mybir.dt.float32r
BF16 = mybir.dt.bfloat16
ALU = mybir.AluOpType
ACT = mybir.ActivationFunctionType
AX_X = mybir.AxisListType.X

P = 128
D = 1024
KT = D // P
L = 512
C = 256
T = L + C
FF = 2816
FT = FF // P
GROUPS = (8, 8, 6)
NH, NKV, DH = 8, 2, 128
GQA = NH // NKV
GRID_W = 64
EPS = 1e-6
BW = 1024
RAW, RING = 2, 4
ADA = 4
DMA_SCRATCH = 2048
LAG = 3
PAD = 8
UL, UC, UW = PAD, PAD + L + 2 * PAD, L + C + 4 * PAD
STREAMS = ((0, 0, L), (1, L, T))
LATENT = STREAMS[:1]



def numbered(names, start=0):
    return {n: start + i for i, n in enumerate(names)}


def plan():
    ffn = lambda l: [(k, l, gi, i) for gi, n in enumerate(GROUPS)
                     for k, m in (("up", 2 * n), ("down", KT)) for i in range(m)]
    blocks = (["df", ("four", 0), ("pin", 0)] + [("four", h) for h in (1, 2, 3)] + [("pin", g) for g in (1, 2, 3)]
              + ["c0", "c1", "s0", "s1", "ctxdft", "poolw"] + [("out", m) for m in range(KT)] + ffn(0)
              + [("k", j) for j in range(NKV)] + [("v", j) for j in range(2)]
              + [("q", h) for h in range(NH)] + [("o", m) for m in range(KT)] + ffn(1))
    units = (["n0", "ab", ("four", 0), ("pin", 0), ("four", 1), ("va", 0), ("vb", 0), ("four", 2), ("va", 1), ("vb", 1),
              ("four", 3), ("va", 2), ("vb", 2), ("pin", 1), ("va", 3), ("vb", 3), ("pin", 2), ("pin", 3)]
             + ["dft0", "dft1", "dftc"] + [("poolw", g) for g in range(4)] + [("out", m) for m in range(KT)]
             + ["n1"] + ffn(0) + ["n2"])
    heads = [("k", j) for j in range(NKV)] + [("q", h) for h in range(NH)]
    units += [("k", 0), ("k", 1), ("ss", 0), "v0", ("ss", 1), "v1"]
    for h in range(NH):
        units += [("q", h)] + ([("ss", 1 + h)] if h else [])
    units += [("ss", 9)]
    n = NH * 4
    for i in range(n + LAG + 2):
        units += [("s", i)] * (i < n) + [("t", i - LAG)] * (LAG <= i < n + LAG)
        if i >= LAG + 5 and (i - LAG) % 4 == 1:
            units += [("pv", (i - LAG) // 4 - 1)]
    units += [("o", m) for m in range(KT)] + ["n3"] + ffn(1) + ["n4"]
    splits = (["ab"] + [("h", 0, k) for k in range(KT)] + [ ("u", 0), ("u", 1), ("va", 0), ("vb", 0), ("u", 2),
              ("va", 1), ("vb", 1), ("u", 3), ("va", 2), ("vb", 2), ("va", 3), ("vb", 3)]
              + [("pool", g) for g in range(4)] + ["dft0", "dft1", "dftc"] + [("y", g) for g in range(4)]
              + [("h", 1, k) for k in range(KT)] + [("g", 0, p) for p in range(FT)]
              + [("h", 2, k) for k in range(KT)] + [("k", 0), "v0", ("k", 1), "v1"] + [("q", h) for h in range(NH)])
    for i in range(LAG, n + LAG + 2):
        splits += [("t", i - LAG)] * (i < n + LAG)
        if i >= LAG + 5 and (i - LAG) % 4 == 1:
            splits += [("pv", (i - LAG) // 4 - 1)]
    splits += [("h", 3, k) for k in range(KT)] + [("g", 1, p) for p in range(FT)]
    return numbered(blocks), numbered(units), numbered(splits), heads


BLK, UNIT, SPLIT, HEADS = plan()
NB = len(BLK)

SHIFT = (0, 24, 48, 72)
GATE = {("mixer", 0): 16, ("ffn", 0): 40, ("mixer", 1): 64, ("ffn", 1): 88}


def kind(unit_name):
    return unit_name if isinstance(unit_name, str) else unit_name[0]


FREED = {n for name, n in UNIT.items() if kind(name) in ("pin", "out", "up", "down", "o")}


ADA_START = 18
ADA_UP, ADA_DOWN = (40, 64, 80), 56
BOTH = 64


def dots_after(t, both=None):
    return 2 * (t + 1) if (t < BOTH if both is None else both) else BOTH + t + 1


def freed_before(n):
    return 1 + sum(m in FREED for m in range(n % 4, n, 4))

V_ADAB, V_N1, V_N2, V_FG = 0, 96, 112, 128
V_PS, V_QG, V_KG, V_EDGE = 136, 140, 141, 142
V_CONV = V_EDGE + 64
NORM_G = (V_N1, V_N2, V_N1 + KT, V_N2 + KT)
NVEC = V_CONV + 4 * 2 * FT
M_MODS = NVEC
M_GAIN = M_MODS + 192
M_ACC = M_GAIN + 64
M_STAT = M_ACC + 8
M_EPS = M_STAT + 16
M_EPSQ = M_EPS + 1
M_QS = M_EPSQ + 1
M_ONES = M_QS + 4 * NH
NSMALL = M_ONES + P
T_COS, T_SIN, T_ID, T_CONV = 0, L, 2 * L, 2 * L + P
NTAB = T_CONV + 4 * 2 * FT


def program(nc, xt, cvec, wstream, adaw, vecs, tabs, out):
    with ExitStack() as ctx:
        def sb(name, shape, dt=F32):
            return ctx.enter_context(nc.sbuf_tensor(name, shape, dt))

        def sem(name):
            return ctx.enter_context(nc.semaphore(name))

        x = sb("x", [P, KT, T])
        h_hi, h_lo = sb("h_hi", [P, KT, T], F32R), sb("h_lo", [P, KT, T], F32R)
        g_hi, g_lo = sb("g_hi", [P, KT, T], F32R), sb("g_lo", [P, KT, T], F32R)
        w_hi, w_lo = sb("w_hi", [P, RING, BW], F32R), sb("w_lo", [P, RING, BW], F32R)
        w_raw = sb("w_raw", [P, RAW, BW])
        uv_hi, uv_lo = sb("uv_hi", [P, T + BW], F32R), sb("uv_lo", [P, T + BW], F32R)
        ada_raw = sb("ada_raw", [P, ADA * BW])
        junk = sb("junk", [P, BW], BF16)
        cond = sb("cond", [P, 2 * BW])
        scratch = sb("scratch", [P, 4 * UW])
        small = sb("small", [P, NSMALL])
        psum = ctx.enter_context(nc.psum_tensor("psum", [P, 4, BW], F32))

        x_landed = [sem(f"x_landed{i}") for i in range(4)]
        vecs_landed, cond_landed = sem("vecs_landed"), [sem(f"cond_landed{i}") for i in range(2)]
        tabs_landed = sem("tabs_landed")
        w_landed = [sem(f"w_landed{i}") for i in range(RAW)]
        ada_landed = [sem(f"ada_landed{i}") for i in range(ADA)]
        rot_landed = [sem(f"rot_landed{i}") for i in range(2)]
        out_stored = sem("out_stored")
        w_hi_ready, w_lo_ready = sem("w_hi_ready"), sem("w_lo_ready")
        dft_block_used = sem("dft_block_used")
        unit_ready = sem("unit_ready")
        unit_free = [sem(f"unit_free{i}") for i in range(4)]
        hi_ready, lo_ready = sem("hi_ready"), sem("lo_ready")
        cond_ready, dots_ready, mods_ready = sem("cond_ready"), sem("dots_ready"), sem("mods_ready")
        gain_ready, rms_ready, rstd_ready, scaled = sem("gain_ready"), sem("rms_ready"), sem("rstd_ready"), sem("scaled")
        squared, square_used, sumsq_added = sem("squared"), sem("square_used"), sem("sumsq_added")
        pads_ready, u_copied, window_step, pooled = sem("pads_ready"), sem("u_copied"), sem("window_step"), sem("pooled")
        center_tap, left_tap, silu_done, product_ready = sem("center_tap"), sem("left_tap"), sem("silu_done"), sem("product_ready")
        head_gained, head_squared, head_rms, head_rstd = sem("head_gained"), sem("head_squared"), sem("head_rms"), sem("head_rstd")
        rope_step, head_ready = sem("rope_step"), sem("head_ready")
        max_found, max_ready, exp_ready, inv_ready, probs_ready = (
            sem("max_found"), sem("max_ready"), sem("exp_ready"), sem("inv_ready"), sem("probs_ready"))
        eps_ready, final_ready = sem("eps_ready"), sem("final_ready")

        def view(buf, at, n):
            return buf[:, at:at + n]

        ones = view(small, M_ONES, P)
        eps = view(small, M_EPS, 1)
        mods = view(small, M_MODS, 192).rearrange("p (t s) -> p t s", s=2)
        gains = view(small, M_GAIN, 64).rearrange("p (n k s) -> p n k s", n=4, s=2)
        ada_acc = view(small, M_ACC, 8).rearrange("p (j s) -> p j s", s=2)
        eps_q = view(small, M_EPSQ, 1)
        q_scale = view(small, M_QS, 4 * NH)
        stat = view(small, M_STAT, 16).rearrange("p (r s) -> p r s", s=4)
        cos, sin = view(ada_raw, T_COS, L), view(ada_raw, T_SIN, L)
        ident = view(ada_raw, T_ID, P)
        conv = [view(small, V_CONV, 8 * FT).rearrange("p (t c) -> p t c", c=4),
                view(ada_raw, T_CONV, 8 * FT).rearrange("p (t c) -> p t c", c=4)]
        edge = view(small, V_EDGE, 64).rearrange("p (g e c) -> p g e c", g=4, e=2)
        tile_ = [scratch[:, i * T:(i + 1) * T] for i in range(4)]
        upad = [scratch[:, i * UW:(i + 1) * UW] for i in range(4)]
        headbuf = [scratch[:, i * T:(i + 1) * T] for i in range(2)]
        rotated = [scratch[:, 2 * T + i * L:2 * T + (i + 1) * L] for i in range(2)]
        head_sq, head_inv, head_sin = view(cond, 0, T), view(cond, T, T), view(cond, 2 * T, L)
        probs = tile_
        u_part = [b[:, 0:T] for b in (uv_hi, uv_lo)]
        ab = [b[:, T:T + BW].rearrange("p (h c) -> p h c", h=4) for b in (uv_hi, uv_lo)]
        vv = [b[:, :, :].rearrange("p a b -> p (a b)").rearrange("p (t h c) -> p t h c", t=6, h=4) for b in (g_hi, g_lo)]
        gflat = [b[:, :, :].rearrange("p a b -> p (a b)") for b in (g_hi, g_lo)]
        hflat = [b[:, :, :].rearrange("p a b -> p (a b)") for b in (h_hi, h_lo)]
        qo = [b[:, 0:NH * L].rearrange("p (h t) -> p h t", h=NH) for b in gflat]
        kk = [b[:, NH * L:NH * L + NKV * T].rearrange("p (h t) -> p h t", h=NKV) for b in gflat]
        v_ = [b[:, 0:6 * NKV * DH].rearrange("p (t c) -> p t c", t=6) for b in (uv_hi, uv_lo)]
        pt = [b[:, :].rearrange("p (r k q) -> p r k q", r=2, k=6) for b in hflat]

        def slot(n):
            return psum[:, n % 4, :]

        def col(buf, i):
            return buf[:, bass.ds(i, 1)]

        def tile3(buf, i):
            return buf[:, bass.ds(i, 1), :].rearrange("p o n -> p (o n)")

        def used_at(b):
            name = next(n for n, i in BLK.items() if i == b)
            if name in ("c0", "c1", "s0"):
                return dft_block_used, ("c0", "c1", "s0").index(name) + 1
            unit = {"df": "ab", "s1": "dft1", "ctxdft": "dftc", "poolw": ("poolw", 3), ("v", 0): "v1", ("v", 1): "v1"}.get(name, name)
            return unit_ready, UNIT[unit] + 1

        def released(n):
            name = next(u for u, i in UNIT.items() if i == n)
            k = kind(name)
            if n in FREED:
                return unit_free[n % 4], freed_before(n) + 1
            if k in ("k", "q"):
                return head_squared, HEADS.index(name) + 1
            if k == "ss":
                return head_rms, name[1] + 1
            if k == "s":
                return exp_ready, name[1] + 1
            if k[0] == "n":
                return rms_ready, int(k[1:]) + 1
            split = {"four": ("u", name[1]), "poolw": ("y", name[1])}.get(k, name)
            return lo_ready, SPLIT[split] + 1

        def wait_part(eng, name):
            eng.wait_ge(lo_ready, SPLIT[name] + 1)

        block = ctx.enter_context(nc.Block())

        @block.sync
        def _(sp):
            def ada_first(t):
                sp.dma_start(ada_raw[:, (t % ADA) * BW:(t % ADA + 1) * BW], adaw[t]).then_inc(ada_landed[t % ADA], 16)

            for t in range(ADA):
                if t < 2:
                    sp.dma_start(cond[:, t * BW:(t + 1) * BW], cvec[:, t * BW:(t + 1) * BW]).then_inc(cond_landed[t], 16)
                ada_first(t)
            sp.dma_start(small[:, 0:NVEC], vecs).then_inc(vecs_landed, 16)
            for t in range(ADA, ADA_START):
                if t < ADA + 4:
                    q = t - ADA
                    sp.dma_start(x[:, 2 * q:2 * q + 2, :], xt[:, 2 * q:2 * q + 2, :]).then_inc(x_landed[q], 16)
                elif t < ADA + 4 + RAW:
                    b = t - ADA - 4
                    sp.dma_start(w_raw[:, b, :], wstream[b]).then_inc(w_landed[b], 16)
                sp.wait_ge(dots_ready, dots_after(t - ADA))
                ada_first(t)
            with sp.Fori(1, NB // RAW) as i:
                for b in range(RAW):
                    sp.wait_ge(w_lo_ready, i * RAW + (b + 1 - RAW))
                    sp.dma_start(w_raw[:, b, :], wstream[bass.ds(i * RAW + b, 1)].rearrange("o p n -> p (o n)")).then_inc(w_landed[b], 16)
            for b in range(NB // RAW * RAW, NB):
                sp.wait_ge(w_lo_ready, b + 1 - RAW)
                sp.dma_start(w_raw[:, b % RAW, :], wstream[b]).then_inc(w_landed[b % RAW], 16)

        @block.gpsimd
        def _(pool):
            nc.gpsimd.memset(ones, 1.0).then_inc(eps_ready, 1)
            nc.gpsimd.memset(eps, EPS).then_inc(eps_ready, 1)
            nc.gpsimd.memset(eps_q, DH * EPS).then_inc(eps_ready, 1)

            def lo_part(slot_, wait):
                pool.wait_ge(w_hi_ready, wait)
                nc.gpsimd.tensor_tensor(w_lo[:, slot_, :], w_raw[:, slot_ % RAW, :], w_hi[:, slot_, :].bitcast(F32),
                                        ALU.subtract).then_inc(w_lo_ready, 1)

            with pool.Fori(0, NB // RING) as i:
                for j in range(RING):
                    lo_part(j, i * RING + (j + 1))
            for b in range(NB // RING * RING, NB):
                lo_part(b % RING, b + 1)

        @block.scalar
        def _(act):
            def w_split(b, i=None):
                s, turns = b % RING, 0 if i is None else i * (RING // RAW)
                act.wait_ge(w_landed[s % RAW], (b // RAW + 1) * 16 + (0 if i is None else i * (16 * RING // RAW)))
                nc.scalar.activation(w_hi[:, s, :], w_raw[:, s % RAW, :], ACT.Copy).then_inc(w_hi_ready, 1)

            def w_next(b):
                if b + RING - 1 >= NB:
                    return
                if b >= 1:
                    act.wait_ge(*used_at(b - 1))
                w_split(b + RING - 1)

            def ada_load(t, i=None, waits=True, both=None):
                if waits:
                    n = dots_after(t - ADA, both)
                    act.wait_ge(dots_ready, n if i is None else i * (4 * (1 + both)) + n)
                src = adaw[t] if i is None else adaw[bass.ds(i * 4 + t, 1)].rearrange("o p n -> p (o n)")
                act.dma_start(ada_raw[:, (t % ADA) * BW:(t % ADA + 1) * BW], src).then_inc(ada_landed[t % ADA], 16)

            def unit(name):
                act.wait_ge(unit_ready, UNIT[name] + 1)

            def rms(n, streams):
                unit(f"n{n}")
                if n == 0:
                    act.wait_ge(eps_ready, 3)
                end = streams[-1][2]
                nc.scalar.activation(tile_[3][:, 0:end], slot(UNIT[f"n{n}"])[:, 0:end], ACT.Sqrt,
                                     bias=eps, scale=1.0 / D).then_inc(rms_ready, 1)

            def h_hi_parts(n, streams):
                act.wait_ge(gain_ready, n + 1)
                for k in range(KT):
                    act.wait_ge(scaled, KT * n + k + 1)
                    for s, a, e in streams:
                        ins = nc.scalar.activation(h_hi[:, k, a:e], tile_[k % 2][:, a:e], ACT.Identity,
                                                   bias=mods[:, SHIFT[n] + k, s:s + 1])
                    ins.then_inc(hi_ready, 1)

            for s in range(2):
                act.wait_ge(cond_landed[s], 16)
                nc.scalar.activation(cond[:, s * BW:(s + 1) * BW], cond[:, s * BW:(s + 1) * BW], ACT.Silu).then_inc(cond_ready, 1)

            def x_square(k):
                act.wait_ge(x_landed[k // 2], 16)
                if k >= 2:
                    act.wait_ge(square_used, k - 1)
                nc.scalar.activation(tile_[k % 2], x[:, k, :], ACT.Square).then_inc(squared, 1)

            def ab_hi():
                unit("ab")
                for z in range(2):
                    ins = nc.scalar.activation(ab[0][:, :, z * P:(z + 1) * P],
                                               slot(UNIT["ab"])[:, z * L:(z + 1) * L].rearrange("p (h c) -> p h c", h=4), ACT.Copy)
                ins.then_inc(hi_ready, 1)

            for k in range(KT):
                x_square(k)
            w_split(0)
            w_split(1)
            rms(0, STREAMS)
            w_split(2)
            w_next(0)
            ab_hi()
            h_hi_parts(0, STREAMS)

            def v_hi(kind, h):
                n = UNIT[(kind, h)]
                unit((kind, h))
                t0, nt = (0, 4) if kind == "va" else (4, 2)
                nc.scalar.activation(vv[0][:, t0:t0 + nt, h, :],
                                     slot(n)[:, 0:nt * C].rearrange("p (t c) -> p t c", t=nt), ACT.Copy).then_inc(hi_ready, 1)

            def u_hi(h):
                w_next(BLK[("four", h)])
                unit(("four", h))
                if h >= 1:
                    unit(("vb", h - 1))
                nc.scalar.activation(u_part[0], slot(UNIT[("four", h)])[:, 0:T], ACT.Copy).then_inc(hi_ready, 1)

            def u_copy(g):
                w_next(BLK[("pin", g)])
                unit(("pin", g))
                if g == 0:
                    act.wait_ge(pads_ready, 2)
                if g >= 2:
                    act.wait_ge(lo_ready, SPLIT[("pool", g - 2)] + 1)
                n = UNIT[("pin", g)]
                nc.scalar.activation(upad[g % 2][:, UL:UL + L], slot(n)[:, 0:L], ACT.Copy).then_inc(u_copied, 1)
                nc.scalar.activation(upad[g % 2][:, UC:UC + C], slot(n)[:, L:T], ACT.Copy).then_inc(unit_free[n % 4], 1)

            def pool_hi(g):
                if g == 0:
                    unit(("pin", 3))
                act.wait_ge(pooled, g + 1)
                nc.scalar.activation(h_hi[:, g, 0:L], upad[g % 2][:, UL:UL + L], ACT.Copy)
                nc.scalar.activation(h_hi[:, g, L:T], upad[g % 2][:, UC:UC + C], ACT.Copy).then_inc(hi_ready, 1)

            ada = iter(range(ADA_START, 32))

            def ada_loads(n):
                for _ in range(n):
                    t = next(ada, None)
                    if t is not None:
                        ada_load(t)

            u_hi(0); ada_loads(2); u_copy(0); u_hi(1); ada_loads(3)
            v_hi("va", 0); v_hi("vb", 0); u_hi(2); ada_loads(3)
            v_hi("va", 1); v_hi("vb", 1); u_hi(3); ada_loads(3)
            v_hi("va", 2); v_hi("vb", 2); u_copy(1); ada_loads(3)
            v_hi("va", 3); v_hi("vb", 3)
            pool_hi(0); u_copy(2)
            pool_hi(1); u_copy(3)
            w_next(BLK["c0"])
            pool_hi(2)
            w_next(BLK["c1"])
            pool_hi(3)
            w_next(BLK["s0"])
            w_next(BLK["s1"])
            for z in range(2):
                unit(f"dft{z}")
                nc.scalar.activation(h_hi[:, 4 + 2 * z:6 + 2 * z, 0:L],
                                     slot(UNIT[f"dft{z}"]).rearrange("p (h t) -> p h t", h=2), ACT.Copy).then_inc(hi_ready, 1)
            w_next(BLK["ctxdft"])
            unit("dftc")
            nc.scalar.activation(h_hi[:, 4:8, L:T], slot(UNIT["dftc"]).rearrange("p (h t) -> p h t", h=4),
                                 ACT.Copy).then_inc(hi_ready, 1)
            w_next(BLK["poolw"])
            for g in range(4):
                unit(("poolw", g))
                nc.scalar.activation(h_hi[:, g, :], slot(UNIT[("poolw", g)])[:, 0:T], ACT.Copy,
                                     scale=col(small, V_PS + g)).then_inc(hi_ready, 1)

            def trunk_squares(n, first_unit, m, i=None):
                nn, end = first_unit + m, T if n <= 2 else L
                turn = lambda step, v: v if i is None else i * step + v
                act.wait_ge(unit_free[nn % 4], turn(1, freed_before(nn) + 1))
                act.wait_ge(sumsq_added, turn(4, (KT + 1) * (n - 1) + 1 + m - m % 2))
                nc.scalar.activation(tile_[m % 2][:, 0:end], tile3(x, turn(4, m))[:, 0:end], ACT.Square).then_inc(squared, 1)

            def out_phase(first_block, first_unit, n, ada_tiles=None):
                with act.Fori(0, KT // 4) as i:
                    for q in (0, 2):
                        for j in (q, q + 1):
                            act.wait_ge(unit_ready, i * 4 + (first_unit + j))
                            w_split(first_block + j + RING - 1, i)
                            if ada_tiles is not None:
                                ada_load(ada_tiles + j, i, both=True)
                        if n is not None:
                            for j in (q, q + 1):
                                trunk_squares(n, first_unit, j, i)

            out_phase(BLK[("out", 0)], UNIT[("out", 0)], 1, 32)

            def ffn(l, streams):
                end = streams[-1][2]
                for gi, n in enumerate(GROUPS):
                    first_b, first_u = BLK[("up", l, gi, 0)], UNIT[("up", l, gi, 0)]
                    p0 = sum(GROUPS[:gi])
                    if gi == 0:
                        act.wait_ge(lo_ready, SPLIT[("h", 1 + 2 * l, KT - 1)] + 1)
                    with act.Fori(0, n // 2) as i:
                        for q in range(2):
                            for z in range(2):
                                j = 2 * q + z
                                nn = first_u + j
                                act.wait_ge(unit_ready, i * 4 + nn)
                                w_split(first_b + j + RING - 1, i)
                                if l == 0:
                                    ada_load(ADA_UP[gi] + j, i, both=ADA_UP[gi] < BOTH)
                                if z == 0:
                                    act.wait_ge(lo_ready, i * 2 + (SPLIT[("g", l, p0)] + q - 1))
                                act.wait_ge(unit_ready, i * 4 + (nn + 1))
                                ct = conv[l]
                                cc = i * 4 + (2 * p0 + j)
                                nc.scalar.activation(
                                    tile_[2 * q + z][:, 0:end], slot(nn)[:, 0:end], ACT.Identity,
                                    bias=ct[:, bass.ds(cc, 1), 3:4].rearrange("p a b -> p (a b)"),
                                    scale=ct[:, bass.ds(cc, 1), 1:2].rearrange("p a b -> p (a b)")).then_inc(center_tap, 1)
                            nn = first_u + 2 * q
                            act.wait_ge(unit_free[nn % 4], i + (freed_before(nn) + 1))
                            nc.scalar.activation(tile_[2 * q][:, 0:end], tile_[2 * q][:, 0:end], ACT.Silu).then_inc(silu_done, 1)
                            act.wait_ge(product_ready, i * 2 + (FT * l + p0 + q + 1))
                            nc.scalar.activation(g_hi[:, bass.ds(i * 2 + q, 1), 0:end].rearrange("p o n -> p (o n)"),
                                                 tile_[2 * q + 1][:, 0:end], ACT.Copy).then_inc(hi_ready, 1)
                    first_b, first_u = BLK[("down", l, gi, 0)], UNIT[("down", l, gi, 0)]
                    last = gi == len(GROUPS) - 1
                    if last and l == 1:
                        for m in range(KT):
                            if first_b + m + RING - 1 < NB:
                                act.wait_ge(unit_ready, first_u + m)
                                w_split(first_b + m + RING - 1)
                            trunk_squares(4, first_u, m)
                    else:
                        if last:
                            for t in range(4):
                                ada_load(92 + t)
                        out_phase(first_b, first_u, 2 if last else None, ADA_DOWN if (l, gi) == (0, 0) else None)

            rms(1, STREAMS)
            h_hi_parts(1, STREAMS)
            ffn(0, STREAMS)
            rms(2, STREAMS)
            act.wait_ge(dots_ready, dots_after(95))
            act.dma_start(ada_raw[:, 0:NTAB], tabs).then_inc(tabs_landed, 16)
            h_hi_parts(2, STREAMS)

            def swap(i):
                act.wait_ge(head_gained, i + 1)
                for q in range(4):
                    dst, src = 32 * q, 32 * (q ^ 1)
                    act.dma_start(rotated[i % 2][dst:dst + 32, :], headbuf[i % 2][src:src + 32, 0:L]).then_inc(rot_landed[i % 2], 16)

            def head_in(i):
                kind, j = HEADS[i]
                n, end = UNIT[HEADS[i]], T if kind == "k" else L
                w_next(BLK[HEADS[i]])
                unit(HEADS[i])
                if i == 0:
                    act.wait_ge(lo_ready, SPLIT[("h", 2, KT - 1)] + 1)
                if i >= 2:
                    wait_part(act, HEADS[i - 2])
                nc.scalar.activation(headbuf[i % 2][:, 0:end], slot(n)[:, 0:end], ACT.Copy,
                                     scale=col(small, V_KG if kind == "k" else V_QG)).then_inc(head_gained, 1)
                if i >= 1:
                    act.wait_ge(unit_ready, UNIT[("ss", i - 1)] + 1)
                nc.scalar.activation(head_sq[:, 0:end], slot(n)[:, 0:end], ACT.Square).then_inc(head_squared, 1)
                swap(i)

            def head_root(i):
                n, (kind_, j) = UNIT[("ss", i)], HEADS[i]
                unit(("ss", i))
                if kind_ == "k":
                    if i >= 1:
                        act.wait_ge(head_ready, i)
                    nc.scalar.activation(head_inv, slot(n)[:, 0:T], ACT.Sqrt, bias=eps, scale=1.0 / DH).then_inc(head_rms, 1)
                else:
                    nc.scalar.activation(q_scale[:, 4 * j:4 * j + 4], slot(n)[:, 0:4], ACT.Sqrt, bias=eps_q).then_inc(head_rms, 1)

            def head_hi(i):
                kind, j = HEADS[i]
                end = T if kind == "k" else L
                if kind == "k":
                    act.wait_ge(head_ready, i + 1)
                else:
                    act.wait_ge(rope_step, 3 * i + 3)
                dst = kk[0][:, j, :] if kind == "k" else qo[0][:, j, :]
                nc.scalar.activation(dst, headbuf[i % 2][:, 0:end], ACT.Copy).then_inc(hi_ready, 1)

            def v_part(z):
                n, t0, nt = UNIT[f"v{z}"], 4 * z, 4 - 2 * z
                unit(f"v{z}")
                nc.scalar.activation(v_[0][:, t0:t0 + nt, :], slot(n)[:, 0:nt * C].rearrange("p (t c) -> p t c", t=nt),
                                     ACT.Copy).then_inc(hi_ready, 1)

            head_in(0)
            head_in(1)
            w_next(BLK[("v", 0)])
            head_root(0)
            head_hi(0)
            v_part(0)
            head_root(1)
            head_hi(1)
            v_part(1)
            w_next(BLK[("v", 1)])
            for h in range(NH):
                head_in(2 + h)
                if h:
                    head_root(1 + h)
                    head_hi(1 + h)
            head_root(NH + 1)
            head_hi(NH + 1)

            def exps(i):
                act.wait_ge(max_ready, i + 1)
                if i >= 4:
                    unit(("t", i - 4))
                nc.scalar.activation(probs[i % 4], slot(UNIT[("s", i)])[:, 0:T], ACT.Exp, bias=stat[:, i % 4, 0:1],
                                     scale=q_scale[:, i:i + 1], accum_out=stat[:, i % 4, 1:2]).then_inc(exp_ready, 1)

            def t_hi(i):
                unit(("t", i))
                h, qt = i // 4, i % 4
                if qt == 0 and h >= 2:
                    unit(("pv", h - 2))
                nc.scalar.activation(pt[0][:, h % 2, :, qt * P:(qt + 1) * P],
                                     slot(UNIT[("t", i)])[:, 0:T].rearrange("p (k q) -> p k q", k=6), ACT.Copy).then_inc(hi_ready, 1)

            n = NH * 4
            for i in range(n + LAG + 2):
                if 1 <= i <= n:
                    exps(i - 1)
                if LAG <= i < n + LAG:
                    t_hi(i - LAG)
                if i >= LAG + 5 and (i - LAG) % 4 == 1:
                    h = (i - LAG) // 4 - 1
                    unit(("pv", h))
                    nc.scalar.activation(qo[0][:, h, :], slot(UNIT[("pv", h)])[:, 0:L], ACT.Copy).then_inc(hi_ready, 1)
            out_phase(BLK[("o", 0)], UNIT[("o", 0)], 3)
            rms(3, LATENT)
            h_hi_parts(3, LATENT)
            ffn(1, LATENT)
            rms(4, LATENT)
            for k in range(KT):
                act.wait_ge(scaled, KT * 4 + k + 1)
                act.dma_start(out[:, k, :], x[:, k, 0:L]).then_inc(out_stored, 16)
            act.wait_ge(out_stored, 16 * KT)

        @block.tensor
        def _(pe):
            def claim(n, i=None):
                if i is not None:
                    pe.wait_ge(unit_free[n % 4], i + freed_before(n))
                elif n >= 4:
                    pe.wait_ge(*released(n - 4))

            def claim_ahead(n):
                for m in range(n - 4, n):
                    if m not in FREED:
                        pe.wait_ge(*released(m))

            def weights(b, i=None):
                pe.wait_ge(w_lo_ready, b + 1 if i is None else i * RING + (b + 1))

            def mm3(dst, w, a, start, stop):
                nc.tensor.matmul(dst, w[0], a[0], start=start, stop=False)
                nc.tensor.matmul(dst, w[0], a[1], start=False, stop=False)
                return nc.tensor.matmul(dst, w[1], a[0], start=False, stop=stop)

            def wtile(b, k, m=P):
                return [w[:, b % RING, k * m:(k + 1) * m] for w in (w_hi, w_lo)]

            def ones_sum(n, src, spans, start=True, stop=True):
                for a, e in spans:
                    ins = nc.tensor.matmul(slot(n)[:, a:e], ones, src[:, a:e], start=start, stop=stop)
                return ins

            spans = lambda streams: [(a, e) for _, a, e in streams]

            def out_tile(n, b, src, ks, streams, i=None):
                claim(n, i)
                weights(b, i)
                for kx, k in enumerate(ks):
                    for a, e in spans(streams):
                        ins = mm3(slot(n)[:, a:e], wtile(b, kx), [s[:, k, a:e] for s in src], kx == 0, kx == len(ks) - 1)
                ins.then_inc(unit_ready, 1)

            def pair_tiles(n, b, src, ks, streams, i=None, per_k=None):
                for kx, k in enumerate(ks):
                    if per_k is not None:
                        pe.wait_ge(lo_ready, per_k(kx))
                    for z in range(2):
                        if kx == 0:
                            claim(n + z, i)
                            weights(b + z, i)
                        for a, e in spans(streams):
                            ins = mm3(slot(n + z)[:, a:e], wtile(b + z, kx), [s[:, k, a:e] for s in src],
                                      kx == 0, kx == len(ks) - 1)
                        if kx == len(ks) - 1:
                            ins.then_inc(unit_ready, 1)

            h_, g_ = (h_hi, h_lo), (g_hi, g_lo)
            pe.wait_ge(eps_ready, 3)
            for k in range(KT):
                pe.wait_ge(squared, k + 1)
                for a, e in spans(STREAMS):
                    ins = nc.tensor.matmul(slot(0)[:, a:e], ones, tile_[k % 2][:, a:e], start=k == 0, stop=k == KT - 1)
                ins.then_inc(square_used if k < KT - 1 else unit_ready, 1)

            weights(BLK["df"])
            n = UNIT["ab"]
            for z in range(2):
                ins = mm3(slot(n)[:, z * L:(z + 1) * L], wtile(BLK["df"], z),
                          [w[:, BLK["df"] % RING, 2 * P:2 * P + L] for w in (w_hi, w_lo)], True, True)
            ins.then_inc(unit_ready, 1)

            def v_units(h):
                wait_part(pe, ("u", h))
                if h == 0:
                    wait_part(pe, "ab")
                for kind, tiles in (("va", range(4)), ("vb", range(4, 6))):
                    n = UNIT[(kind, h)]
                    claim(n)
                    for c, t in enumerate(tiles):
                        ins = mm3(slot(n)[:, c * C:(c + 1) * C], [u[:, t * P:(t + 1) * P] for u in u_part],
                                  [a[:, h, :] for a in ab], True, True)
                    ins.then_inc(unit_ready, 1)

            def h_tile(name, b):
                out_tile(UNIT[name], b, h_, range(KT), STREAMS)

            pair_tiles(UNIT[("four", 0)], BLK[("four", 0)], h_, range(KT), STREAMS, per_k=lambda k: SPLIT[("h", 0, k)] + 1)
            h_tile(("four", 1), BLK[("four", 1)])
            v_units(0)
            h_tile(("four", 2), BLK[("four", 2)])
            v_units(1)
            h_tile(("four", 3), BLK[("four", 3)])
            v_units(2)
            h_tile(("pin", 1), BLK[("pin", 1)])
            v_units(3)
            for g in (2, 3):
                h_tile(("pin", g), BLK[("pin", g)])
            wait_part(pe, ("vb", 3))
            claim(UNIT["dft0"])
            claim(UNIT["dft1"])
            for bx, b in enumerate(("c0", "c1", "s0", "s1")):
                weights(BLK[b])
                z = bx // 2
                for h in range(4):
                    for y in range(2):
                        t = 2 * (bx % 2) + y
                        ins = mm3(slot(UNIT[f"dft{h // 2}"])[:, (h % 2) * L:(h % 2 + 1) * L],
                                  [v[:, t, h, z * P:(z + 1) * P] for v in vv], wtile(BLK[b], y, L),
                                  bx == 0 and y == 0, bx == 3 and y == 1)
                        if bx == 3 and y == 1 and h == 1:
                            ins.then_inc(unit_ready, 1)
                if bx < 3:
                    ins.then_inc(dft_block_used, 1)
            ins.then_inc(unit_ready, 1)
            n, b = UNIT["dftc"], BLK["ctxdft"]
            claim(n)
            weights(b)
            for h in range(4):
                for q in range(4):
                    z, t = q // 2, q % 2
                    ins = mm3(slot(n)[:, h * C:(h + 1) * C], [v[:, 4 + t, h, z * P:(z + 1) * P] for v in vv],
                              wtile(b, q, C), q == 0, q == 3)
            ins.then_inc(unit_ready, 1)
            weights(BLK["poolw"])
            for g in range(4):
                n = UNIT[("poolw", g)]
                claim(n)
                wait_part(pe, ("pool", g))
                for a, e in spans(STREAMS):
                    ins = mm3(slot(n)[:, a:e], wtile(BLK["poolw"], g), [s[:, g, a:e] for s in h_], True, True)
                ins.then_inc(unit_ready, 1)

            def out_phase(b, n, src, nk, streams, per_k):
                claim_ahead(n)
                with pe.Fori(0, KT // 4) as i:
                    pair_tiles(n, b, src, range(nk), streams, i, per_k)
                    for j in (2, 3):
                        out_tile(n + j, b + j, src, range(nk), streams, i)

            def norm_sum(nn, streams):
                n = UNIT[f"n{nn}"]
                claim(n)
                pe.wait_ge(sumsq_added, (KT + 1) * nn)
                for a, e in spans(streams):
                    ins = nc.tensor.matmul(slot(n)[:, a:e], ones, tile_[2][:, a:e], start=True, stop=True)
                ins.then_inc(unit_ready, 1)

            out_phase(BLK[("out", 0)], UNIT[("out", 0)], h_, KT, STREAMS, lambda k: SPLIT[("y", 3)] + 1)
            norm_sum(1, STREAMS)

            def ffn(l, streams):
                for gi, ng in enumerate(GROUPS):
                    b, n = BLK[("up", l, gi, 0)], UNIT[("up", l, gi, 0)]
                    p0 = sum(GROUPS[:gi])
                    per_k = (lambda k: SPLIT[("h", 1 + 2 * l, k)] + 1) if gi == 0 else None
                    claim_ahead(n)
                    with pe.Fori(0, ng // 2) as i:
                        pair_tiles(n, b, h_, range(KT), streams, i, per_k)
                        for j in (2, 3):
                            out_tile(n + j, b + j, h_, range(KT), streams, i)
                    out_phase(BLK[("down", l, gi, 0)], UNIT[("down", l, gi, 0)], g_, ng, streams,
                              lambda k: SPLIT[("g", l, p0)] + k + 1)

            ffn(0, STREAMS)
            norm_sum(2, STREAMS)

            def head_sum(i):
                n, end = UNIT[("ss", i)], T if HEADS[i][0] == "k" else L
                claim(n)
                pe.wait_ge(head_squared, i + 1)
                if end == T:
                    for a, e in ((0, L), (L, T)):
                        ins = nc.tensor.matmul(slot(n)[:, a:e], ones, head_sq[:, a:e], start=True, stop=True)
                else:
                    for t in range(4):
                        ins = nc.tensor.matmul(slot(n)[:, t:t + 1], head_sq[:, t * P:(t + 1) * P], ones[:, 0:1], start=True, stop=True)
                ins.then_inc(unit_ready, 1)

            def v_tiles(z):
                n = UNIT[f"v{z}"]
                claim(n)
                weights(BLK[("v", 1)])
                for c, t in enumerate(range(4 * z, 6 if z else 4)):
                    for k in range(KT):
                        ins = mm3(slot(n)[:, c * C:(c + 1) * C], [s[:, k, t * P:(t + 1) * P] for s in h_],
                                  wtile(BLK[("v", k // 4)], k % 4, C), k == 0, k == KT - 1)
                ins.then_inc(unit_ready, 1)

            pair_tiles(UNIT[("k", 0)], BLK[("k", 0)], h_, range(KT), STREAMS, per_k=lambda k: SPLIT[("h", 2, k)] + 1)
            head_sum(0)
            v_tiles(0)
            head_sum(1)
            v_tiles(1)
            for h in range(NH):
                out_tile(UNIT[("q", h)], BLK[("q", h)], h_, range(KT), LATENT)
                if h:
                    head_sum(1 + h)
            head_sum(NH + 1)

            def scores(i):
                n, h, qt = UNIT[("s", i)], i // 4, i % 4
                claim(n)
                wait_part(pe, ("q", h))
                for a, e in spans(STREAMS):
                    ins = mm3(slot(n)[:, a:e], [q[:, h, qt * P:(qt + 1) * P] for q in qo],
                              [k[:, h // GQA, a:e] for k in kk], True, True)
                ins.then_inc(unit_ready, 1)

            def transposes(i):
                n = UNIT[("t", i)]
                claim(n)
                pe.wait_ge(probs_ready, i + 1)
                if i == 0:
                    pe.wait_ge(tabs_landed, 16)
                for k in range(6):
                    ins = nc.tensor.transpose(slot(n)[:, k * P:(k + 1) * P], probs[i % 4][:, k * P:(k + 1) * P], ident)
                ins.then_inc(unit_ready, 1)

            def weighted(h):
                n = UNIT[("pv", h)]
                claim(n)
                wait_part(pe, ("t", 4 * h + 3))
                for k in range(6):
                    ins = mm3(slot(n)[:, 0:L], [v[:, k, (h // GQA) * DH:(h // GQA + 1) * DH] for v in v_],
                              [p[:, h % 2, k, :] for p in pt], k == 0, k == 5)
                ins.then_inc(unit_ready, 1)

            n = NH * 4
            for i in range(n + LAG + 2):
                if i < n:
                    scores(i)
                if LAG <= i < n + LAG:
                    transposes(i - LAG)
                if i >= LAG + 5 and (i - LAG) % 4 == 1:
                    weighted((i - LAG) // 4 - 1)
            out_phase(BLK[("o", 0)], UNIT[("o", 0)], qo, NH, LATENT, lambda k: SPLIT[("pv", k)] + 1)
            norm_sum(3, LATENT)
            ffn(1, LATENT)
            norm_sum(4, LATENT)

        @block.vector
        def _(dve):
            V = nc.vector

            def unit(name):
                dve.wait_ge(unit_ready, UNIT[name] + 1)

            for z in range(4):
                V.memset(stat[:, z, :], 0.0).then_inc(unit_free[z], 1)

            def ada_tile(t, j, both, i=None, per=4):
                turns = 0 if i is None else i * (16 * per // ADA)
                dve.wait_ge(ada_landed[t % ADA], 16 * (t // ADA + 1) + turns)
                w = ada_raw[:, (t % ADA) * BW:(t % ADA + 1) * BW]
                if t % 4 == 0 and t:
                    dve.wait_ge(mods_ready, t // 4 if i is None else i * (per // 4) + t // 4)
                for s in range(1 + both):
                    n = dots_after(t, both) - both + s
                    if n <= 2:
                        dve.wait_ge(cond_ready, n)
                    if n > 1:
                        dve.wait_ge(dots_ready, n - 1 if i is None else i * (per * (1 + both)) + (n - 1))
                    V.tensor_tensor_reduce(junk[:, :], w, cond[:, s * BW:(s + 1) * BW], 1.0, 0.0, ALU.mult,
                                           ALU.add, ada_acc[:, j, s:s + 1]).then_inc(dots_ready, 1)

            def ada_add(t0, both, i=None, per=4):
                n = dots_after(t0 + 3, both)
                dve.wait_ge(dots_ready, n if i is None else i * (per * (1 + both)) + n)
                tt = t0 if i is None else i * per + t0
                for s in range(1 + both):
                    ins = V.tensor_tensor(mods[:, bass.ds(tt, 4), s], ada_acc[:, :, s],
                                          small[:, bass.ds(V_ADAB + tt, 4)], ALU.add)
                ins.then_inc(mods_ready, 1)

            def gain(n, streams):
                dve.wait_ge(mods_ready, (SHIFT[n] + 2 * KT) // 4)
                for s, _, _ in streams:
                    ins = V.scalar_tensor_tensor(gains[:, n, :, s], mods[:, SHIFT[n] + KT:SHIFT[n] + 2 * KT, s], 1.0,
                                                 small[:, NORM_G[n]:NORM_G[n] + KT], ALU.add, ALU.mult)
                ins.then_inc(gain_ready, 1)

            def rstd(n, end):
                dve.wait_ge(rms_ready, n + 1)
                V.reciprocal(tile_[3][:, 0:end], tile_[3][:, 0:end]).then_inc(rstd_ready, 1)

            def norm(n, streams):
                end = streams[-1][2]
                if n:
                    rstd(n, end)
                dve.wait_ge(rstd_ready, n + 1)
                dve.wait_ge(gain_ready, n + 1)

                def scale_x(k):
                    if k >= 2:
                        dve.wait_ge(lo_ready, SPLIT[("h", n, k - 2)] + 1)
                    for s, a, e in streams:
                        ins = V.scalar_tensor_tensor(tile_[k % 2][:, a:e], x[:, k, a:e], gains[:, n, k, s:s + 1],
                                                     tile_[3][:, a:e], ALU.mult, ALU.mult)
                    ins.then_inc(scaled, 1)

                scale_x(0)
                for k in range(KT):
                    if k + 1 < KT:
                        scale_x(k + 1)
                    dve.wait_ge(hi_ready, SPLIT[("h", n, k)] + 1)
                    for s, a, e in streams:
                        ins = V.scalar_tensor_tensor(h_lo[:, k, a:e], tile_[k % 2][:, a:e], mods[:, SHIFT[n] + k, s:s + 1],
                                                     h_hi[:, k, a:e].bitcast(F32), ALU.add, ALU.subtract)
                    ins.then_inc(lo_ready, 1)

            dve.wait_ge(vecs_landed, 16)
            for t0 in range(0, 16, 4):
                for j in range(4):
                    ada_tile(t0 + j, j, True)
                ada_add(t0, True)
                if t0 == 8:
                    rstd(0, T)
            n = UNIT["ab"]
            dve.wait_ge(hi_ready, SPLIT["ab"] + 1)
            for z in range(2):
                ins = V.tensor_tensor(ab[1][:, :, z * P:(z + 1) * P],
                                      slot(n)[:, z * L:(z + 1) * L].rearrange("p (h c) -> p h c", h=4),
                                      ab[0][:, :, z * P:(z + 1) * P].bitcast(F32), ALU.subtract)
            ins.then_inc(lo_ready, 1)
            gain(0, STREAMS)
            norm(0, STREAMS)
            dve.wait_ge(lo_ready, SPLIT[("h", 0, KT - 1)] + 1)
            for z in range(2):
                V.memset(upad[z], 0.0).then_inc(pads_ready, 1)

            def lo_of(name, dst, src, hi, n=None):
                dve.wait_ge(hi_ready, SPLIT[name] + 1)
                V.tensor_tensor(dst, src, hi.bitcast(F32), ALU.subtract).then_inc(lo_ready, 1)

            ada = iter(range(16, 32))

            def ada_tiles(count):
                for _ in range(count):
                    t = next(ada, None)
                    if t is None:
                        return
                    ada_tile(t, t % 4, True)
                    if t % 4 == 3:
                        ada_add(t - 3, True)

            def u_lo(h):
                n = UNIT[("four", h)]
                lo_of(("u", h), u_part[1], slot(n)[:, 0:T], u_part[0])
    
            def v_lo(kind, h):
                n = UNIT[(kind, h)]
                t0, nt = (0, 4) if kind == "va" else (4, 2)
                lo_of((kind, h), vv[1][:, t0:t0 + nt, h, :], slot(n)[:, 0:nt * C].rearrange("p (t c) -> p t c", t=nt),
                      vv[0][:, t0:t0 + nt, h, :])
    
            steps = [0]

            def step(ins):
                ins.then_inc(window_step, 1)
                steps[0] += 1

            def pool_group(g):
                u, a, b = upad[g % 2], upad[2], upad[3]
                n = UNIT[("pin", g)]
                dve.wait_ge(u_copied, g + 1)
                if g:
                    dve.wait_ge(pooled, g)
                dve.wait_ge(*released(n))
                step(V.tensor_tensor(a[:, 1:UW], u[:, 0:UW - 1], u[:, 1:UW], ALU.add))
                src, dst, lo, hi = a, b, 1, UW
                for q in range(g):
                    d = 1 << q
                    dve.wait_ge(window_step, steps[0])
                    step(V.tensor_tensor(dst[:, lo + d:hi - d], src[:, lo:hi - 2 * d], src[:, lo + 2 * d:hi], ALU.add))
                    src, dst, lo, hi = dst, src, lo + d, hi - d
                dve.wait_ge(window_step, steps[0])
                for e0, side in ((UL, 0), (UL + L - PAD, 1), (UC, 0), (UC + C - PAD, 1)):
                    ins = V.tensor_tensor(src[:, e0:e0 + PAD], src[:, e0:e0 + PAD], edge[:, g, side, :], ALU.mult)
                step(ins)
                dve.wait_ge(window_step, steps[0])
                for e0, m in ((UL, L), (UC, C)):
                    ins = V.scalar_tensor_tensor(u[:, e0:e0 + m], src[:, e0:e0 + m], 1.0 / (2 << g), u[:, e0:e0 + m],
                                                 ALU.mult, ALU.subtract)
                ins.then_inc(pooled, 1)

            def pool_lo(g):
                dve.wait_ge(hi_ready, SPLIT[("pool", g)] + 1)
                for e0, a, m in ((UL, 0, L), (UC, L, C)):
                    ins = V.tensor_tensor(h_lo[:, g, a:a + m], upad[g % 2][:, e0:e0 + m], h_hi[:, g, a:a + m].bitcast(F32),
                                          ALU.subtract)
                ins.then_inc(lo_ready, 1)

            u_lo(0); ada_tiles(2); u_lo(1); ada_tiles(3)
            v_lo("va", 0); v_lo("vb", 0); u_lo(2); ada_tiles(3)
            v_lo("va", 1); v_lo("vb", 1); u_lo(3); ada_tiles(3)
            v_lo("va", 2); v_lo("vb", 2); ada_tiles(3)
            v_lo("va", 3); v_lo("vb", 3); ada_tiles(2)
            for g in range(4):
                pool_group(g)
                pool_lo(g)
            for z in range(2):
                n = UNIT[f"dft{z}"]
                lo_of(f"dft{z}", h_lo[:, 4 + 2 * z:6 + 2 * z, 0:L], slot(n).rearrange("p (h t) -> p h t", h=2),
                      h_hi[:, 4 + 2 * z:6 + 2 * z, 0:L])
                n = UNIT["dftc"]
            lo_of("dftc", h_lo[:, 4:8, L:T], slot(n).rearrange("p (h t) -> p h t", h=4), h_hi[:, 4:8, L:T])
            for g in range(4):
                n = UNIT[("poolw", g)]
                dve.wait_ge(hi_ready, SPLIT[("y", g)] + 1)
                V.scalar_tensor_tensor(h_lo[:, g, :], slot(n)[:, 0:T], col(small, V_PS + g), h_hi[:, g, :].bitcast(F32),
                                       ALU.mult, ALU.subtract).then_inc(lo_ready, 1)

            def add_square(n, m, i=None):
                turn = lambda step, v: v if i is None else i * step + v
                end = T if n <= 2 else L
                dve.wait_ge(squared, turn(4, KT * n + m + 1))
                dve.wait_ge(sumsq_added, turn(4, (KT + 1) * (n - 1) + 1 + m))
                V.tensor_tensor(tile_[2][:, 0:end], tile_[2][:, 0:end], tile_[m % 2][:, 0:end], ALU.add).then_inc(sumsq_added, 1)

            def update(nn, gate, m, streams, i=None):
                turn = lambda step, v: v if i is None else i * step + v
                dve.wait_ge(unit_ready, turn(4, nn + 1))
                xm = tile3(x, turn(4, m))
                for s, a, e in streams:
                    g = mods[:, bass.ds(turn(4, gate + m), 1), s]
                    ins = V.scalar_tensor_tensor(xm[:, a:e], slot(nn)[:, a:e], g, xm[:, a:e], ALU.mult, ALU.add)
                ins.then_inc(unit_free[nn % 4], 1)

            def out_phase(first_unit, gate, streams, n, ada_tiles=None):
                dve.wait_ge(mods_ready, gate // 4 + 2)
                if n is not None:
                    if n == 3:
                        dve.wait_ge(probs_ready, NH * 4)
                        dve.wait_ge(rope_step, 3 * len(HEADS))
                    else:
                        dve.wait_ge(lo_ready, {1: SPLIT[("y", 3)], 2: SPLIT[("g", 0, FT - 1)], 4: SPLIT[("g", 1, FT - 1)]}[n] + 1)
                    V.memset(tile_[2], 0.0).then_inc(sumsq_added, 1)
                with dve.Fori(0, KT // 4) as i:
                    for q in (0, 2):
                        if ada_tiles is not None:
                            for j in (q, q + 1):
                                ada_tile(ada_tiles + j, j, True, i)
                        for j in (q, q + 1):
                            update(first_unit + j, gate, j, streams, i)
                        if n is not None:
                            for j in (q, q + 1):
                                add_square(n, j, i)
                    if ada_tiles is not None:
                        ada_add(ada_tiles, True, i)

            def ffn(l, streams):
                ct = conv[l]
                for gi, ng in enumerate(GROUPS):
                    first_u = UNIT[("up", l, gi, 0)]
                    p0 = sum(GROUPS[:gi])
                    with dve.Fori(0, ng // 2) as i:
                        for q in range(2):
                            for z in range(2):
                                j = 2 * q + z
                                nn, t = first_u + j, tile_[j]
                                v = 2 * (FT * l + p0) + j
                                dve.wait_ge(center_tap, i * 4 + (v + 1))
                                w0, w2 = (ct[:, bass.ds(i * 4 + (2 * p0 + j), 1), c:c + 1].rearrange("p a b -> p (a b)") for c in (0, 2))
                                for _, a, e in streams:
                                    ins = V.scalar_tensor_tensor(t[:, a + 1:e], slot(nn)[:, a:e - 1], w0, t[:, a + 1:e],
                                                                 ALU.mult, ALU.add)
                                ins.then_inc(left_tap, 1)
                                dve.wait_ge(left_tap, i * 4 + (v + 1))
                                for _, a, e in streams:
                                    ins = V.scalar_tensor_tensor(t[:, a:e - 1], slot(nn)[:, a + 1:e], w2, t[:, a:e - 1],
                                                                 ALU.mult, ALU.add)
                                ins.then_inc(unit_free[nn % 4], 1)
                                if l == 0:
                                    ada_tile(ADA_UP[gi] + j, j, ADA_UP[gi] < BOTH, i)
                            if l == 0 and q == 1:
                                ada_add(ADA_UP[gi], ADA_UP[gi] < BOTH, i)
                            p = FT * l + p0 + q
                            nn = first_u + 2 * q + 1
                            dve.wait_ge(silu_done, i * 2 + (p + 1))
                            dve.wait_ge(unit_free[nn % 4], i + (freed_before(nn) + 1))
                            end = streams[-1][2]
                            V.tensor_tensor(tile_[2 * q + 1][:, 0:end], tile_[2 * q][:, 0:end], tile_[2 * q + 1][:, 0:end],
                                            ALU.mult).then_inc(product_ready, 1)
                            dve.wait_ge(hi_ready, i * 2 + (SPLIT[("g", l, p0)] + q + 1))
                            V.tensor_tensor(tile3(g_lo, i * 2 + q)[:, 0:end], tile_[2 * q + 1][:, 0:end],
                                            tile3(g_hi, i * 2 + q)[:, 0:end].bitcast(F32), ALU.subtract).then_inc(lo_ready, 1)
                    first_u, last = UNIT[("down", l, gi, 0)], gi == len(GROUPS) - 1
                    if last and l == 0:
                        for t in range(92, 96):
                            ada_tile(t, t % 4, False)
                        ada_add(92, False)
                    out_phase(first_u, GATE[("ffn", l)], streams, 2 + 2 * l if last else None,
                              ADA_DOWN if (l, gi) == (0, 0) else None)

            out_phase(UNIT[("out", 0)], GATE[("mixer", 0)], STREAMS, 1, 32)
            gain(1, STREAMS)
            norm(1, STREAMS)
            ffn(0, STREAMS)
            gain(2, STREAMS)
            norm(2, STREAMS)

            def head(i):
                kind_, j = HEADS[i]
                end, buf = T if kind_ == "k" else L, headbuf[i % 2]
                dve.wait_ge(head_gained, i + 1)
                dve.wait_ge(rot_landed[i % 2], 64 * (i // 2 + 1))
                if i == 0:
                    dve.wait_ge(tabs_landed, 16)
                if i:
                    dve.wait_ge(rope_step, 3 * i)
                V.tensor_tensor(head_sin, rotated[i % 2], sin, ALU.mult).then_inc(rope_step, 1)
                V.tensor_tensor(buf[:, 0:L], buf[:, 0:L], cos, ALU.mult).then_inc(rope_step, 1)
                dve.wait_ge(rope_step, 3 * i + 2)
                V.tensor_tensor(buf[:, 0:L], buf[:, 0:L], head_sin, ALU.add).then_inc(rope_step, 1)
                dve.wait_ge(rope_step, 3 * i + 3)
                if kind_ == "k":
                    dve.wait_ge(head_rms, i + 1)
                    V.reciprocal(head_inv, head_inv).then_inc(head_rstd, 1)
                    dve.wait_ge(head_rstd, i + 1)
                    V.tensor_tensor(buf, buf, head_inv, ALU.mult).then_inc(head_ready, 1)
                dst, hi = (kk[1][:, j, :], kk[0][:, j, :]) if kind_ == "k" else (qo[1][:, j, :], qo[0][:, j, :])
                lo_of(HEADS[i], dst, buf[:, 0:end], hi)
                if kind_ == "q":
                    dve.wait_ge(head_rms, i + 1)
                    V.reciprocal(q_scale[:, 4 * j:4 * j + 4], q_scale[:, 4 * j:4 * j + 4]).then_inc(head_rstd, 1)

            def v_lo_part(z):
                n, t0, nt = UNIT[f"v{z}"], 4 * z, 4 - 2 * z
                lo_of(f"v{z}", v_[1][:, t0:t0 + nt, :], slot(n)[:, 0:nt * C].rearrange("p (t c) -> p t c", t=nt),
                      v_[0][:, t0:t0 + nt, :])

            head(0)
            v_lo_part(0)
            head(1)
            v_lo_part(1)
            for h in range(NH):
                head(2 + h)

            def row_max(i):
                unit(("s", i))
                r = stat[:, i % 4, :]
                V.reduce_max(r[:, 3:4], slot(UNIT[("s", i)])[:, 0:T], AX_X).then_inc(max_found, 1)
                if i % 4 == 0:
                    dve.wait_ge(head_rstd, NKV + i // 4 + 1)
                dve.wait_ge(max_found, i + 1)
                V.tensor_scalar(r[:, 0:1], r[:, 3:4], q_scale[:, i:i + 1], -1.0, ALU.mult, ALU.mult).then_inc(max_ready, 1)

            def normalise(i):
                dve.wait_ge(exp_ready, i + 1)
                r = stat[:, i % 4, :]
                V.reciprocal(r[:, 2:3], r[:, 1:2]).then_inc(inv_ready, 1)
                dve.wait_ge(inv_ready, i + 1)
                V.tensor_scalar(probs[i % 4], probs[i % 4], r[:, 2:3], None, ALU.mult).then_inc(probs_ready, 1)

            n = NH * 4
            for i in range(n + LAG + 2):
                if i < n:
                    row_max(i)
                if 1 <= i <= n:
                    normalise(i - 1)
                if LAG <= i < n + LAG:
                    k = i - LAG
                    cols = slice(k % 4 * P, (k % 4 + 1) * P)
                    lo_of(("t", k), pt[1][:, k // 4 % 2, :, cols],
                          slot(UNIT[("t", k)])[:, 0:T].rearrange("p (k q) -> p k q", k=6), pt[0][:, k // 4 % 2, :, cols])
                if i >= LAG + 5 and (i - LAG) % 4 == 1:
                    h = (i - LAG) // 4 - 1
                    lo_of(("pv", h), qo[1][:, h, :], slot(UNIT[("pv", h)])[:, 0:L], qo[0][:, h, :])
            out_phase(UNIT[("o", 0)], GATE[("mixer", 1)], LATENT, 3)
            gain(3, LATENT)
            norm(3, LATENT)
            ffn(1, LATENT)
            rstd(4, L)
            dve.wait_ge(rstd_ready, 5)
            for k in range(KT):
                V.scalar_tensor_tensor(x[:, k, 0:L], x[:, k, 0:L], col(small, V_FG + k), tile_[3][:, 0:L],
                                       ALU.mult, ALU.mult).then_inc(scaled, 1)




def dft(n):
    a = 2 * np.pi * (np.outer(np.arange(n), np.arange(n)) % n) / n
    return np.cos(a), np.sin(a)


def window_edges():
    e = np.ones((4, 2, PAD))
    for g in range(4):
        w = 2 << g
        for side, ts in enumerate((range(PAD), range(L - PAD, L))):
            for c, t in enumerate(ts):
                e[g, side, c] = w / (min(t + w - w // 2, L) - max(t - w // 2, 0))
    return e.astype(np.float32)


def rotary():
    pairs = DH // 4
    freqs = np.float32(10000.0) ** (-np.arange(pairs, dtype=np.float32) / np.float32(pairs))
    t = np.arange(L)
    ang = [(p.astype(np.float32)[:, None] * freqs[None, :]).T.astype(np.float64) for p in (t // GRID_W, t % GRID_W)]
    cos = np.concatenate([np.cos(ang[0])] * 2 + [np.cos(ang[1])] * 2)
    sin = np.concatenate([-np.sin(ang[0]), np.sin(ang[0]), -np.sin(ang[1]), np.sin(ang[1])])
    return cos.astype(np.float32), sin.astype(np.float32)


def by_partition(v):
    return np.asarray(v).reshape(-1, P).T


def lay_out(x, c, ctx, c_ctx, ada_w, ada_b, norm1_g, norm2_g, pf_w_in, pool_w, pool_scale, fourier_w, pf_w_out,
            attn_w_qkv, q_norm_g, k_norm_g, attn_w_o, ffn_w_up, ffn_conv_w, ffn_conv_b, ffn_w_down, final_g):
    f = np.float32
    feature_tiles = lambda a: a.T.reshape(KT, P, -1).transpose(1, 0, 2)
    xt = np.concatenate([feature_tiles(x[0]), feature_tiles(ctx[0])], axis=2)
    cvec = np.ascontiguousarray(np.broadcast_to(np.concatenate([c[0], c_ctx])[None], (P, 2 * D)))
    adaw = np.concatenate([ada_w[l].T.reshape(-1, P, D) for l in range(2)])

    w = np.zeros((NB, P, BW), f)

    def put(name, tile):
        t = tile.reshape(P, -1)
        w[BLK[name], :, :t.shape[1]] = t

    def column_block(a, m, width=P):
        return a[:, m * width:(m + 1) * width].reshape(-1, P, width).transpose(1, 0, 2)

    cc, ss = dft(DH)
    heads = lambda a: a.transpose(1, 0, 2).reshape(P, -1)
    put("df", np.concatenate([cc.astype(f), (-ss).astype(f), heads(fourier_w[0])], axis=1))
    put("poolw", heads(pool_w[0]))
    for h in range(4):
        put(("four", h), column_block(pf_w_in[0], 4 + h))
        put(("pin", h), column_block(pf_w_in[0], h))
    for n, names in ((L, ("c0", "c1", "s0", "s1")), (C, ("ctxdft",))):
        m = [(t / np.sqrt(n * DH)).astype(f).reshape(n // P, P, n).transpose(1, 0, 2).reshape(P, -1) for t in dft(n)]
        m = np.concatenate(m, axis=1)
        for b, name in enumerate(names):
            put(name, m[:, b * BW:(b + 1) * BW])
    qkv = attn_w_qkv[0]
    kv = qkv[:, NH * DH:]
    for m in range(KT):
        put(("out", m), column_block(pf_w_out[0], m))
        put(("q", m), column_block(qkv, m))
        put(("o", m), column_block(attn_w_o[0], m))
    for j in range(NKV):
        put(("k", j), column_block(kv, j))
        put(("v", j), column_block(kv[:, NKV * DH:], 0, NKV * DH)[:, 4 * j:4 * j + 4])
    convs = []
    for l in range(2):
        for gi, n in enumerate(GROUPS):
            p0 = sum(GROUPS[:gi])
            for i in range(2 * n):
                put(("up", l, gi, i), column_block(ffn_w_up[l], p0 + i // 2 + FT * (i % 2)))
            for m in range(KT):
                put(("down", l, gi, m), column_block(ffn_w_down[l][p0 * P:(p0 + n) * P], m))
        taps = np.concatenate([ffn_conv_w[l], ffn_conv_b[l][None]]).reshape(4, 2, FT, P)
        convs.append(taps.transpose(3, 2, 1, 0).reshape(P, -1))
    edges = np.broadcast_to(window_edges().reshape(1, -1), (P, 64))
    vecs = np.concatenate([by_partition(ada_b), by_partition(norm1_g), by_partition(norm2_g), by_partition(final_g),
                           by_partition(pool_scale), by_partition(q_norm_g), by_partition(k_norm_g), edges, convs[0]], axis=1)
    cos, sin = rotary()
    tabs = np.concatenate([cos, sin, np.eye(P, dtype=f), convs[1]], axis=1)
    assert vecs.shape[1] == NVEC and tabs.shape[1] == NTAB
    return {"xt": xt, "cvec": cvec, "wstream": w, "adaw": adaw, "vecs": vecs, "tabs": tabs}


def kernel(**inputs):
    import concourse.bacc as bacc
    from concourse.bass_utils import run_bass_kernel_spmd

    arrays = {k: np.ascontiguousarray(v) for k, v in lay_out(**{k: np.asarray(v) for k, v in inputs.items()}).items()}
    nc = bacc.Bacc("TRN2", target_bir_lowering=False, num_devices=1, dynamic_dma_scratch_size=DMA_SCRATCH)
    args = [nc.dram_tensor(k, a.shape, F32, kind="ExternalInput").ap() for k, a in arrays.items()]
    out = nc.dram_tensor("out", (P, KT, L), F32, kind="ExternalOutput").ap()
    program(nc, *args, out)
    got = run_bass_kernel_spmd(nc, [arrays], core_ids=[0]).results[0]["out"]
    return np.ascontiguousarray(got.transpose(2, 1, 0).reshape(1, L, D))
```

```python
from contextlib import ExitStack

import concourse.bass as bass
import numpy as np
from concourse import mybir

F32 = mybir.dt.float32
F32R = mybir.dt.float32r
BF16 = mybir.dt.bfloat16
ALU = mybir.AluOpType
ACT = mybir.ActivationFunctionType
AX_X = mybir.AxisListType.X

P = 128
D = 1024
KT = D // P
L = 512
C = 256
T = L + C
FF = 2816
FT = FF // P
GROUPS = (8, 8, 6)
NH, NKV, DH = 8, 2, 128
GQA = NH // NKV
GRID_W = 64
EPS = 1e-6
BW = 1024
RAW, RING = 2, 4
ADA = 4
DMA_SCRATCH = 2048
PAIRS = NH * 4 // 2
PV_LAG = 3
PAD = 8
UL, UC, UW = PAD, PAD + L + 2 * PAD, L + C + 4 * PAD
STREAMS = ((0, 0, L), (1, L, T))
LATENT = STREAMS[:1]



def numbered(names, start=0):
    return {n: start + i for i, n in enumerate(names)}


def pv_at(p):
    j = p - PV_LAG
    return [("pv", j // 2, j % 2)] if 0 <= j < PAIRS else []


def t_at(p):
    return [("t", 2 * (p - 1)), ("t", 2 * p - 1)] if 0 < p <= PAIRS else []


def pv_unit(name):
    turn = 2 * name[1] + name[2] + PV_LAG
    return t_at(turn)[0] if t_at(turn) else ("pv", turn)


def plan():
    ffn = lambda l: [(k, l, gi, i) for gi, n in enumerate(GROUPS)
                     for k, m in (("up", 2 * n), ("down", KT)) for i in range(m)]
    blocks = (["df", ("four", 0), ("pin", 0)] + [("four", h) for h in (1, 2, 3)] + [("pin", g) for g in (1, 2, 3)]
              + ["c0", "c1", "s0", "s1", "ctxdft", "poolw"] + [("out", m) for m in range(KT)] + ffn(0)
              + [("k", j) for j in range(NKV)] + [("v", j) for j in range(2)]
              + [("q", h) for h in range(NH)] + [("o", m) for m in range(KT)] + ffn(1))
    units = (["mods0", "ns0", "nb0", "ab", ("four", 0), ("pin", 0), ("four", 1), ("va", 0), ("vb", 0),
              ("four", 2), ("va", 1), ("vb", 1),
              ("four", 3), ("va", 2), ("vb", 2), ("pin", 1), ("va", 3), ("vb", 3), ("pin", 2), ("pin", 3)]
             + ["dft0", "dft1", "dftc"] + [("poolw", g) for g in range(4)] + [("out", m) for m in range(KT)]
             + ["ns1", "nb1"] + ffn(0) + ["ns2", "nb2"])
    heads = [("k", j) for j in range(NKV)] + [("q", h) for h in range(NH)]
    units += [("k", 0), ("k", 1), ("ss", 0), "v0", ("ss", 1), "v1"]
    for h in range(NH):
        units += [("q", h)] + ([("ss", 1 + h)] if h else [])
    units += [("s", 0), ("s", 1), ("ss", 9)]
    n = NH * 4
    for p in range(1, PAIRS + PV_LAG):
        units += [("s", 2 * p), ("s", 2 * p + 1)] * (p < PAIRS)
        units += t_at(p) or [("pv", p)]
    units += [("o", m) for m in range(KT)] + ["ns3", "nb3"] + ffn(1) + ["ns4", "nb4"]
    splits = ([("h", 0, k) for k in range(KT)] + ["ab", ("u", 0), ("u", 1), ("va", 0), ("vb", 0), ("u", 2),
              ("va", 1), ("vb", 1), ("u", 3), ("va", 2), ("vb", 2), ("va", 3), ("vb", 3)]
              + [("pool", g) for g in range(4)] + ["dft0", "dft1", "dftc"] + [("y", g) for g in range(4)]
              + [("h", 1, k) for k in range(KT)] + [("g", 0, p) for p in range(FT)]
              + [("h", 2, k) for k in range(KT)] + [("k", 0), "v0", ("k", 1), "v1"] + [("q", h) for h in range(NH)])
    for p in range(1, PAIRS + PV_LAG):
        splits += t_at(p)[:1] + pv_at(p) + t_at(p)[1:]
    splits += [("h", 3, k) for k in range(KT)] + [("g", 1, p) for p in range(FT)]
    return numbered(blocks), numbered(units), numbered(splits), heads


BLK, UNIT, SPLIT, HEADS = plan()
NB = len(BLK)

SHIFT = (0, 24, 48, 72)
GATE = {("mixer", 0): 16, ("ffn", 0): 40, ("mixer", 1): 64, ("ffn", 1): 88}


def kind(unit_name):
    return unit_name if isinstance(unit_name, str) else unit_name[0]


FREED = {n for name, n in UNIT.items() if kind(name) in ("pin", "out", "up", "down", "o")}


PE_TILES = 6
ADA_START = 18
ADA_UP, ADA_DOWN = (40, 64, 80), 56
BOTH = 64


def dots_after(t, both=None):
    return 2 * (t + 1 - PE_TILES) if (t < BOTH if both is None else both) else BOTH + t + 1 - 2 * PE_TILES


def ada_turn(t):
    return sum(u >= PE_TILES for u in range(t % ADA, t + 1, ADA))


def freed_before(n):
    return 1 + sum(m in FREED for m in range(n % 4, n, 4))

MODS = 2 * 6 * KT
V_ADAB, V_N1 = 0, MODS
V_N2 = V_N1 + 2 * KT
V_FG = V_N2 + 2 * KT
V_PS = V_FG + KT
V_QG = V_PS + 4
V_KG = V_QG + 1
V_EDGE = V_KG + 1
V_COND = V_EDGE + 64
V_ID = V_COND + 2 * KT
V_CONV = V_ID + P
NORM_G = (V_N1, V_N2, V_N1 + KT, V_N2 + KT)
NVEC = V_CONV + 4 * 2 * FT
M_MODS = NVEC
M_GAIN = M_MODS + 2 * MODS
M_ACC = M_GAIN + 4 * KT * 2
M_STAT = M_ACC + 8
M_EPS = M_STAT + 16
M_EPSQ = M_EPS + 1
M_QS = M_EPSQ + 1
M_RMS = M_QS + 4 * NH
M_TABLE = M_RMS + T // P
M_ONES = M_TABLE + 5
NSMALL = M_ONES + P
T_COS, T_SIN, T_CONV = 0, L, 2 * L
NTAB = T_CONV + 4 * 2 * FT


def program(nc, xt, cvec, wstream, adaw, vecs, tabs, out):
    with ExitStack() as ctx:
        def sb(name, shape, dt=F32):
            return ctx.enter_context(nc.sbuf_tensor(name, shape, dt))

        def sem(name):
            return ctx.enter_context(nc.semaphore(name))

        x = sb("x", [P, KT, T])
        h_hi, h_lo = sb("h_hi", [P, KT, T], F32R), sb("h_lo", [P, KT, T], F32R)
        with nc.sbuf_tensor("ada0", [P, PE_TILES * BW], F32) as ada0:
            pass
        g_hi, g_lo = sb("g_hi", [P, KT, T], F32R), sb("g_lo", [P, KT, T], F32R)
        w_hi, w_lo = sb("w_hi", [P, RING, BW], F32R), sb("w_lo", [P, RING, BW], F32R)
        w_raw = sb("w_raw", [P, RAW, BW])
        uv_hi, uv_lo = sb("uv_hi", [P, T + BW], F32R), sb("uv_lo", [P, T + BW], F32R)
        ada_raw = sb("ada_raw", [P, ADA * BW])
        junk = sb("junk", [P, BW], BF16)
        cond = sb("cond", [P, 2 * BW])
        scratch = sb("scratch", [P, 4 * UW])
        small = sb("small", [P, NSMALL])
        psum = ctx.enter_context(nc.psum_tensor("psum", [P, 4, BW], F32))

        x_landed = [sem(f"x_landed{i}") for i in range(4)]
        vecs_landed, cond_landed = sem("vecs_landed"), [sem(f"cond_landed{i}") for i in range(2)]
        cond_col_ready = sem("cond_col_ready")
        tabs_landed = sem("tabs_landed")
        w_landed = [sem(f"w_landed{i}") for i in range(RAW)]
        ada_landed = [sem(f"ada_landed{i}") for i in range(ADA)]
        ada0_landed = [sem(f"ada0_landed{i}") for i in range(PE_TILES // 2)]
        rot_landed = [sem(f"rot_landed{i}") for i in range(2)]
        out_stored = sem("out_stored")
        w_hi_ready, w_lo_ready = sem("w_hi_ready"), sem("w_lo_ready")
        dft_block_used = sem("dft_block_used")
        unit_ready = sem("unit_ready")
        unit_free = [sem(f"unit_free{i}") for i in range(4)]
        hi_ready, lo_ready = sem("hi_ready"), sem("lo_ready")
        cond_ready, dots_ready, mods_ready = sem("cond_ready"), sem("dots_ready"), sem("mods_ready")
        gain_ready, rms_ready, rstd_ready, scaled = sem("gain_ready"), sem("rms_ready"), sem("rstd_ready"), sem("scaled")
        squared, sumsq_added, diag_ready, table_ready = sem("squared"), sem("sumsq_added"), sem("diag_ready"), sem("table_ready")
        pads_ready, u_copied, window_step, pooled = sem("pads_ready"), sem("u_copied"), sem("window_step"), sem("pooled")
        center_tap, left_tap, silu_done, product_ready = sem("center_tap"), sem("left_tap"), sem("silu_done"), sem("product_ready")
        head_gained, head_squared, head_rms, head_rstd = sem("head_gained"), sem("head_squared"), sem("head_rms"), sem("head_rstd")
        rope_step, head_ready = sem("rope_step"), sem("head_ready")
        max_found, max_ready, exp_ready, inv_ready, probs_ready = (
            sem("max_found"), sem("max_ready"), sem("exp_ready"), sem("inv_ready"), sem("probs_ready"))
        eps_ready = sem("eps_ready")

        def view(buf, at, n):
            return buf[:, at:at + n]

        ones = view(small, M_ONES, P)
        eps = view(small, M_EPS, 1)
        mods = view(small, M_MODS, 2 * MODS).rearrange("p (t s) -> p t s", s=2)
        gains = view(small, M_GAIN, 4 * KT * 2).rearrange("p (n k s) -> p n k s", n=4, s=2)
        ada_acc = view(small, M_ACC, 8).rearrange("p (j s) -> p j s", s=2)
        eps_q = view(small, M_EPSQ, 1)
        q_scale = view(small, M_QS, 4 * NH)
        stat = view(small, M_STAT, 16).rearrange("p (r s) -> p r s", s=4)
        cos, sin = view(ada_raw, T_COS, L), view(ada_raw, T_SIN, L)
        ident = view(small, V_ID, P)
        token_rms = view(small, M_RMS, T // P)
        cond_col = view(small, V_COND, 2 * KT).rearrange("p (k s) -> p k s", s=2)
        conv = [view(small, V_CONV, 8 * FT).rearrange("p (t c) -> p t c", c=4),
                view(ada_raw, T_CONV, 8 * FT).rearrange("p (t c) -> p t c", c=4)]
        edge = view(small, V_EDGE, 64).rearrange("p (g e c) -> p g e c", g=4, e=2)
        tile_ = [scratch[:, i * T:(i + 1) * T] for i in range(4)]
        upad = [scratch[:, i * UW:(i + 1) * UW] for i in range(4)]
        headbuf = [scratch[:, i * T:(i + 1) * T] for i in range(2)]
        rotated = [scratch[:, 2 * T + i * L:2 * T + (i + 1) * L] for i in range(2)]
        head_sq, head_inv, head_sin = view(cond, 0, T), view(cond, T, T), view(cond, 2 * T, L)
        probs = tile_
        u_part = [b[:, 0:T] for b in (uv_hi, uv_lo)]
        ab = [b[:, T:T + BW].rearrange("p (h c) -> p h c", h=4) for b in (uv_hi, uv_lo)]
        vv = [b[:, :, :].rearrange("p a b -> p (a b)").rearrange("p (t h c) -> p t h c", t=6, h=4) for b in (g_hi, g_lo)]
        gflat = [b[:, :, :].rearrange("p a b -> p (a b)") for b in (g_hi, g_lo)]
        hflat = [b[:, :, :].rearrange("p a b -> p (a b)") for b in (h_hi, h_lo)]
        qo = [b[:, 0:NH * L].rearrange("p (h t) -> p h t", h=NH) for b in gflat]
        kk = [b[:, NH * L:NH * L + NKV * T].rearrange("p (h t) -> p h t", h=NKV) for b in gflat]
        v_ = [b[:, 0:6 * NKV * DH].rearrange("p (t c) -> p t c", t=6) for b in (uv_hi, uv_lo)]
        pt = [b[:, :].rearrange("p (r k q) -> p r k q", r=2, k=6) for b in hflat]

        def pv_psum(name):
            return slot(UNIT[pv_unit(name)])[:, T:T + L // 2]

        def half(buf, name):
            _, h, z = name
            return buf[:, h, z * L // 2:(z + 1) * L // 2]

        def slot(n):
            return psum[:, n % 4, :]

        def col(buf, i):
            return buf[:, bass.ds(i, 1)]

        def tile3(buf, i):
            return buf[:, bass.ds(i, 1), :].rearrange("p o n -> p (o n)")

        def used_at(b):
            name = next(n for n, i in BLK.items() if i == b)
            if name in ("c0", "c1", "s0"):
                return dft_block_used, ("c0", "c1", "s0").index(name) + 1
            unit = {"df": "ab", "s1": "dft1", "ctxdft": "dftc", "poolw": ("poolw", 3), ("v", 0): "v1", ("v", 1): "v1"}.get(name, name)
            return unit_ready, UNIT[unit] + 1

        def released(n):
            name = next(u for u, i in UNIT.items() if i == n)
            k = kind(name)
            if n in FREED:
                return unit_free[n % 4], freed_before(n) + 1
            if k in ("k", "q"):
                return head_squared, HEADS.index(name) + 1
            if k == "ss":
                return head_rms, name[1] + 1
            if k == "s":
                return exp_ready, name[1] + 1
            if k[:2] == "ns":
                return rms_ready, int(k[2:]) + 1
            if k[:2] == "nb":
                return scaled, KT * (int(k[2:]) + 1)
            if k == "mods0":
                return mods_ready, 4
            split = {"four": ("u", name[1]), "poolw": ("y", name[1])}.get(k, name)
            shared = [pv for pv in SPLIT if kind(pv) == "pv" and pv_unit(pv) == name]
            if shared:
                split = shared[0]
            return lo_ready, SPLIT[split] + 1

        def wait_part(eng, name):
            eng.wait_ge(lo_ready, SPLIT[name] + 1)

        block = ctx.enter_context(nc.Block())

        @block.sync
        def _(sp):
            def ada_first(t):
                sp.dma_start(ada_raw[:, (t % ADA) * BW:(t % ADA + 1) * BW], adaw[t]).then_inc(ada_landed[t % ADA], 16)

            def weight(b):
                if b >= RAW:
                    sp.wait_ge(w_lo_ready, b + 1 - RAW)
                sp.dma_start(w_raw[:, b % RAW, :], wstream[b]).then_inc(w_landed[b % RAW], 16)

            def ada_next(t):
                if t >= PE_TILES + ADA:
                    sp.wait_ge(dots_ready, dots_after(t - ADA))
                ada_first(t)

            def ada_pair(q):
                sp.dma_start(ada0[:, 2 * q * BW:2 * (q + 1) * BW].rearrange("p (t n) -> p t n", t=2),
                             adaw[2 * q:2 * q + 2].rearrange("t p n -> p t n")).then_inc(ada0_landed[q], 16)

            def x_quarter(q):
                sp.dma_start(x[:, 2 * q:2 * q + 2, :], xt[:, 2 * q:2 * q + 2, :]).then_inc(x_landed[q], 16)

            sp.dma_start(small[:, 0:NVEC], vecs).then_inc(vecs_landed, 16)
            for s in range(2):
                sp.dma_start(cond[:, s * BW:(s + 1) * BW], cvec[:, s * BW:(s + 1) * BW]).then_inc(cond_landed[s], 16)
                ada_next(PE_TILES + s)
            ada_pair(0)
            ada_next(8)
            ada_next(9)
            x_quarter(0)
            ada_next(10)
            x_quarter(1)
            weight(0)
            ada_pair(1)
            ada_next(11)
            x_quarter(2)
            ada_pair(2)
            ada_next(12)
            x_quarter(3)
            ada_next(13)
            weight(1)
            ada_next(14)
            ada_next(15)
            weight(2)
            ada_next(16)
            weight(3)
            ada_next(17)
            with sp.Fori(RING // RAW, NB // RAW) as i:
                for b in range(RAW):
                    sp.wait_ge(w_lo_ready, i * RAW + (b + 1 - RAW))
                    sp.dma_start(w_raw[:, b, :], wstream[bass.ds(i * RAW + b, 1)].rearrange("o p n -> p (o n)")).then_inc(w_landed[b], 16)
            for b in range(NB // RAW * RAW, NB):
                sp.wait_ge(w_lo_ready, b + 1 - RAW)
                sp.dma_start(w_raw[:, b % RAW, :], wstream[b]).then_inc(w_landed[b % RAW], 16)

        @block.gpsimd
        def _(pool):
            nc.gpsimd.memset(ones, 1.0).then_inc(eps_ready, 1)
            nc.gpsimd.memset(eps, EPS).then_inc(eps_ready, 1)
            nc.gpsimd.memset(eps_q, DH * EPS).then_inc(eps_ready, 1)

            def lo_part(slot_, wait):
                pool.wait_ge(w_hi_ready, wait)
                nc.gpsimd.tensor_tensor(w_lo[:, slot_, :], w_raw[:, slot_ % RAW, :], w_hi[:, slot_, :].bitcast(F32),
                                        ALU.subtract).then_inc(w_lo_ready, 1)

            def add_square(k):
                pool.wait_ge(squared, k + 1)
                pool.wait_ge(sumsq_added, k + 1)
                nc.gpsimd.tensor_tensor(tile_[2], tile_[2], tile_[k % 2], ALU.add).then_inc(sumsq_added, 1)

            nc.gpsimd.memset(tile_[2], 0.0).then_inc(sumsq_added, 1)
            for k in range(4):
                add_square(k)
            lo_part(0, 1)
            for k in range(4, KT):
                add_square(k)
            for b in range(1, RING):
                lo_part(b, b + 1)
            with pool.Fori(1, NB // RING) as i:
                for j in range(RING):
                    lo_part(j, i * RING + (j + 1))
            for b in range(NB // RING * RING, NB):
                lo_part(b % RING, b + 1)

        @block.scalar
        def _(act):
            def w_split(b, i=None):
                s, turns = b % RING, 0 if i is None else i * (RING // RAW)
                act.wait_ge(w_landed[s % RAW], (b // RAW + 1) * 16 + (0 if i is None else i * (16 * RING // RAW)))
                nc.scalar.activation(w_hi[:, s, :], w_raw[:, s % RAW, :], ACT.Copy).then_inc(w_hi_ready, 1)

            def w_next(b):
                if b + RING - 1 >= NB:
                    return
                if b >= 1:
                    act.wait_ge(*used_at(b - 1))
                w_split(b + RING - 1)

            def ada_load(t, i=None, waits=True, both=None):
                if waits:
                    n = dots_after(t - ADA, both)
                    act.wait_ge(dots_ready, n if i is None else i * (4 * (1 + both)) + n)
                src = adaw[t] if i is None else adaw[bass.ds(i * 4 + t, 1)].rearrange("o p n -> p (o n)")
                act.dma_start(ada_raw[:, (t % ADA) * BW:(t % ADA + 1) * BW], src).then_inc(ada_landed[t % ADA], 16)

            def unit(name):
                act.wait_ge(unit_ready, UNIT[name] + 1)

            def root_table(n):
                nc.scalar.activation(col(small, M_TABLE + n), eps, ACT.Sqrt).then_inc(table_ready, 1)

            def rms(n, streams):
                if n == 0:
                    act.wait_ge(eps_ready, 3)
                root_table(n)
                unit(f"ns{n}")
                nt = streams[-1][2] // P
                if n:
                    act.wait_ge(diag_ready, n)
                nc.scalar.activation(token_rms[:, 0:nt], slot(UNIT[f"ns{n}"])[:, 0:nt], ACT.Sqrt,
                                     bias=eps, scale=1.0 / D).then_inc(rms_ready, 1)

            def h_hi_parts(n, streams):
                act.wait_ge(gain_ready, n + 1)
                for k in range(KT):
                    act.wait_ge(scaled, KT * n + k + 1)
                    for s, a, e in streams:
                        ins = nc.scalar.activation(h_hi[:, k, a:e], tile_[k % 2][:, a:e], ACT.Identity,
                                                   bias=mods[:, SHIFT[n] + k, s:s + 1])
                    ins.then_inc(hi_ready, 1)

            act.wait_ge(vecs_landed, 16)
            nc.scalar.activation(cond_col, cond_col, ACT.Silu).then_inc(cond_col_ready, 1)
            for s in range(2):
                act.wait_ge(cond_landed[s], 16)
                nc.scalar.activation(cond[:, s * BW:(s + 1) * BW], cond[:, s * BW:(s + 1) * BW], ACT.Silu).then_inc(cond_ready, 1)

            def x_square(k):
                act.wait_ge(x_landed[k // 2], 16)
                if k >= 2:
                    act.wait_ge(sumsq_added, k)
                nc.scalar.activation(tile_[k % 2], x[:, k, :], ACT.Square).then_inc(squared, 1)

            def ab_hi():
                unit("ab")
                for z in range(2):
                    ins = nc.scalar.activation(ab[0][:, :, z * P:(z + 1) * P],
                                               slot(UNIT["ab"])[:, z * L:(z + 1) * L].rearrange("p (h c) -> p h c", h=4), ACT.Copy)
                ins.then_inc(hi_ready, 1)

            for k in range(KT):
                x_square(k)
                if k == 3:
                    w_split(0)
            w_split(1)
            rms(0, STREAMS)
            w_split(2)
            h_hi_parts(0, STREAMS)
            ab_hi()
            w_next(0)

            def v_hi(kind, h):
                n = UNIT[(kind, h)]
                unit((kind, h))
                t0, nt = (0, 4) if kind == "va" else (4, 2)
                nc.scalar.activation(vv[0][:, t0:t0 + nt, h, :],
                                     slot(n)[:, 0:nt * C].rearrange("p (t c) -> p t c", t=nt), ACT.Copy).then_inc(hi_ready, 1)

            def u_hi(h):
                w_next(BLK[("four", h)])
                unit(("four", h))
                if h >= 1:
                    unit(("vb", h - 1))
                nc.scalar.activation(u_part[0], slot(UNIT[("four", h)])[:, 0:T], ACT.Copy).then_inc(hi_ready, 1)

            def u_copy(g):
                w_next(BLK[("pin", g)])
                unit(("pin", g))
                if g == 0:
                    act.wait_ge(pads_ready, 2)
                if g >= 2:
                    act.wait_ge(lo_ready, SPLIT[("pool", g - 2)] + 1)
                n = UNIT[("pin", g)]
                nc.scalar.activation(upad[g % 2][:, UL:UL + L], slot(n)[:, 0:L], ACT.Copy).then_inc(u_copied, 1)
                nc.scalar.activation(upad[g % 2][:, UC:UC + C], slot(n)[:, L:T], ACT.Copy).then_inc(unit_free[n % 4], 1)

            def pool_hi(g):
                if g == 0:
                    unit(("pin", 3))
                act.wait_ge(pooled, g + 1)
                nc.scalar.activation(h_hi[:, g, 0:L], upad[g % 2][:, UL:UL + L], ACT.Copy)
                nc.scalar.activation(h_hi[:, g, L:T], upad[g % 2][:, UC:UC + C], ACT.Copy).then_inc(hi_ready, 1)

            ada = iter(range(ADA_START, 32))

            def ada_loads(n):
                for _ in range(n):
                    t = next(ada, None)
                    if t is not None:
                        ada_load(t)

            u_hi(0); ada_loads(2); u_copy(0); u_hi(1); ada_loads(3)
            v_hi("va", 0); v_hi("vb", 0); u_hi(2); ada_loads(3)
            v_hi("va", 1); v_hi("vb", 1); u_hi(3); ada_loads(3)
            v_hi("va", 2); v_hi("vb", 2); u_copy(1); ada_loads(3)
            v_hi("va", 3); v_hi("vb", 3)
            pool_hi(0); u_copy(2)
            pool_hi(1); u_copy(3)
            w_next(BLK["c0"])
            pool_hi(2)
            w_next(BLK["c1"])
            pool_hi(3)
            w_next(BLK["s0"])
            w_next(BLK["s1"])
            for z in range(2):
                unit(f"dft{z}")
                nc.scalar.activation(h_hi[:, 4 + 2 * z:6 + 2 * z, 0:L],
                                     slot(UNIT[f"dft{z}"]).rearrange("p (h t) -> p h t", h=2), ACT.Copy).then_inc(hi_ready, 1)
            w_next(BLK["ctxdft"])
            unit("dftc")
            nc.scalar.activation(h_hi[:, 4:8, L:T], slot(UNIT["dftc"]).rearrange("p (h t) -> p h t", h=4),
                                 ACT.Copy).then_inc(hi_ready, 1)
            w_next(BLK["poolw"])
            for g in range(4):
                unit(("poolw", g))
                nc.scalar.activation(h_hi[:, g, :], slot(UNIT[("poolw", g)])[:, 0:T], ACT.Copy,
                                     scale=col(small, V_PS + g)).then_inc(hi_ready, 1)

            def trunk_squares(n, first_unit, m, i=None):
                nn, end = first_unit + m, T if n <= 2 else L
                turn = lambda step, v: v if i is None else i * step + v
                act.wait_ge(unit_free[nn % 4], turn(1, freed_before(nn) + 1))
                act.wait_ge(sumsq_added, turn(4, (KT + 1) * n + 1 + m - m % 2))
                nc.scalar.activation(tile_[m % 2][:, 0:end], tile3(x, turn(4, m))[:, 0:end], ACT.Square).then_inc(squared, 1)

            def out_phase(first_block, first_unit, n, ada_tiles=None):
                with act.Fori(0, KT // 4) as i:
                    if ada_tiles is not None:
                        for j in range(4):
                            ada_load(ada_tiles + j, i, both=True)
                    for q in (0, 2):
                        for j in (q, q + 1):
                            act.wait_ge(unit_ready, i * 4 + (first_unit + j))
                            w_split(first_block + j + RING - 1, i)
                        if n is not None:
                            for j in (q, q + 1):
                                trunk_squares(n, first_unit, j, i)

            out_phase(BLK[("out", 0)], UNIT[("out", 0)], 1, 32)

            def ffn(l, streams):
                end = streams[-1][2]
                for gi, n in enumerate(GROUPS):
                    first_b, first_u = BLK[("up", l, gi, 0)], UNIT[("up", l, gi, 0)]
                    p0 = sum(GROUPS[:gi])
                    if gi == 0:
                        act.wait_ge(lo_ready, SPLIT[("h", 1 + 2 * l, KT - 1)] + 1)
                    with act.Fori(0, n // 2) as i:
                        for q in range(2):
                            for z in range(2):
                                j = 2 * q + z
                                nn = first_u + j
                                act.wait_ge(unit_ready, i * 4 + nn)
                                w_split(first_b + j + RING - 1, i)
                                if l == 0:
                                    ada_load(ADA_UP[gi] + j, i, both=ADA_UP[gi] < BOTH)
                                if z == 0:
                                    act.wait_ge(lo_ready, i * 2 + (SPLIT[("g", l, p0)] + q - 1))
                                act.wait_ge(unit_ready, i * 4 + (nn + 1))
                                ct = conv[l]
                                cc = i * 4 + (2 * p0 + j)
                                nc.scalar.activation(
                                    tile_[2 * q + z][:, 0:end], slot(nn)[:, 0:end], ACT.Identity,
                                    bias=ct[:, bass.ds(cc, 1), 3:4].rearrange("p a b -> p (a b)"),
                                    scale=ct[:, bass.ds(cc, 1), 1:2].rearrange("p a b -> p (a b)")).then_inc(center_tap, 1)
                            nn = first_u + 2 * q
                            act.wait_ge(unit_free[nn % 4], i + (freed_before(nn) + 1))
                            nc.scalar.activation(tile_[2 * q][:, 0:end], tile_[2 * q][:, 0:end], ACT.Silu).then_inc(silu_done, 1)
                            act.wait_ge(product_ready, i * 2 + (FT * l + p0 + q + 1))
                            nc.scalar.activation(g_hi[:, bass.ds(i * 2 + q, 1), 0:end].rearrange("p o n -> p (o n)"),
                                                 tile_[2 * q + 1][:, 0:end], ACT.Copy).then_inc(hi_ready, 1)
                    first_b, first_u = BLK[("down", l, gi, 0)], UNIT[("down", l, gi, 0)]
                    last = gi == len(GROUPS) - 1
                    if last and l == 1:
                        for m in range(KT):
                            if first_b + m + RING - 1 < NB:
                                act.wait_ge(unit_ready, first_u + m)
                                w_split(first_b + m + RING - 1)
                            trunk_squares(4, first_u, m)
                    else:
                        if last:
                            for t in range(4):
                                ada_load(92 + t)
                        out_phase(first_b, first_u, 2 if last else None, ADA_DOWN if (l, gi) == (0, 0) else None)

            rms(1, STREAMS)
            h_hi_parts(1, STREAMS)
            ffn(0, STREAMS)
            rms(2, STREAMS)
            act.wait_ge(dots_ready, dots_after(95))
            act.dma_start(ada_raw[:, 0:NTAB], tabs).then_inc(tabs_landed, 16)
            h_hi_parts(2, STREAMS)

            def swap(i):
                act.wait_ge(head_gained, i + 1)
                for q in range(4):
                    dst, src = 32 * q, 32 * (q ^ 1)
                    act.dma_start(rotated[i % 2][dst:dst + 32, :], headbuf[i % 2][src:src + 32, 0:L]).then_inc(rot_landed[i % 2], 16)

            def head_in(i):
                kind, j = HEADS[i]
                n, end = UNIT[HEADS[i]], T if kind == "k" else L
                w_next(BLK[HEADS[i]])
                unit(HEADS[i])
                if i == 0:
                    act.wait_ge(lo_ready, SPLIT[("h", 2, KT - 1)] + 1)
                if i >= 2:
                    wait_part(act, HEADS[i - 2])
                nc.scalar.activation(headbuf[i % 2][:, 0:end], slot(n)[:, 0:end], ACT.Copy,
                                     scale=col(small, V_KG if kind == "k" else V_QG)).then_inc(head_gained, 1)
                if i >= 1:
                    act.wait_ge(unit_ready, UNIT[("ss", i - 1)] + 1)
                nc.scalar.activation(head_sq[:, 0:end], slot(n)[:, 0:end], ACT.Square).then_inc(head_squared, 1)
                swap(i)

            def head_root(i):
                n, (kind_, j) = UNIT[("ss", i)], HEADS[i]
                unit(("ss", i))
                if kind_ == "k":
                    if i >= 1:
                        act.wait_ge(head_ready, i)
                    nc.scalar.activation(head_inv, slot(n)[:, 0:T], ACT.Sqrt, bias=eps, scale=1.0 / DH).then_inc(head_rms, 1)
                else:
                    nc.scalar.activation(q_scale[:, 4 * j:4 * j + 4], slot(n)[:, 0:4], ACT.Sqrt, bias=eps_q).then_inc(head_rms, 1)

            def head_hi(i):
                kind, j = HEADS[i]
                end = T if kind == "k" else L
                if kind == "k":
                    act.wait_ge(head_ready, i + 1)
                else:
                    act.wait_ge(rope_step, 3 * i + 3)
                dst = kk[0][:, j, :] if kind == "k" else qo[0][:, j, :]
                nc.scalar.activation(dst, headbuf[i % 2][:, 0:end], ACT.Copy).then_inc(hi_ready, 1)

            def v_part(z):
                n, t0, nt = UNIT[f"v{z}"], 4 * z, 4 - 2 * z
                unit(f"v{z}")
                nc.scalar.activation(v_[0][:, t0:t0 + nt, :], slot(n)[:, 0:nt * C].rearrange("p (t c) -> p t c", t=nt),
                                     ACT.Copy).then_inc(hi_ready, 1)

            head_in(0)
            head_in(1)
            w_next(BLK[("v", 0)])
            head_root(0)
            head_hi(0)
            v_part(0)
            head_root(1)
            head_hi(1)
            v_part(1)
            w_next(BLK[("v", 1)])
            for h in range(NH):
                head_in(2 + h)
                if h:
                    head_root(1 + h)
                    head_hi(1 + h)
            head_root(NH + 1)

            def scaled_max(i):
                if i % 4 == 0:
                    act.wait_ge(head_rstd, NKV + i // 4 + 1)
                act.wait_ge(max_found, i + 1)
                nc.scalar.activation(stat[:, i % 4, 0:1], stat[:, i % 4, 3:4], ACT.Copy, scale=q_scale[:, i:i + 1]).then_inc(max_ready, 1)

            def exps(i):
                scaled_max(i)
                act.wait_ge(max_ready, i + 1)
                if i < 2:
                    wait_part(act, ("q", NH - 2 + i))
                if i >= 4:
                    unit(("t", i - 4))
                nc.scalar.activation(probs[i % 4], slot(UNIT[("s", i)])[:, 0:T], ACT.Exp, bias=stat[:, i % 4, 0:1],
                                     scale=q_scale[:, i:i + 1], accum_out=stat[:, i % 4, 1:2]).then_inc(exp_ready, 1)

            def t_hi(i):
                unit(("t", i))
                h, qt = i // 4, i % 4
                if qt == 0 and h >= 2:
                    unit(pv_unit(("pv", h - 2, 1)))
                nc.scalar.activation(pt[0][:, h % 2, :, qt * P:(qt + 1) * P],
                                     slot(UNIT[("t", i)])[:, 0:T].rearrange("p (k q) -> p k q", k=6), ACT.Copy).then_inc(hi_ready, 1)

            def pv_hi(name):
                unit(pv_unit(name))
                nc.scalar.activation(half(qo[0], name), pv_psum(name), ACT.Copy).then_inc(hi_ready, 1)

            exps(0)
            head_hi(NH + 1)
            exps(1)
            for p in range(1, PAIRS + PV_LAG):
                if p < PAIRS:
                    exps(2 * p)
                    exps(2 * p + 1)
                for _, i in t_at(p)[:1]:
                    t_hi(i)
                for name in pv_at(p):
                    pv_hi(name)
                for _, i in t_at(p)[1:]:
                    t_hi(i)
            out_phase(BLK[("o", 0)], UNIT[("o", 0)], 3)
            rms(3, LATENT)
            h_hi_parts(3, LATENT)
            ffn(1, LATENT)
            rms(4, LATENT)
            for k in range(KT):
                act.wait_ge(scaled, KT * 4 + k + 1)
                act.dma_start(out[:, k, :], x[:, k, 0:L]).then_inc(out_stored, 16)
            act.wait_ge(out_stored, 16 * KT)

        @block.tensor
        def _(pe):
            def claim(n, i=None):
                if i is not None:
                    pe.wait_ge(unit_free[n % 4], i + freed_before(n))
                elif n >= 4:
                    pe.wait_ge(*released(n - 4))

            def claim_ahead(n, j):
                for m in (n + j - 4, n + j - 3):
                    if m not in FREED:
                        pe.wait_ge(*released(m))

            def weights(b, i=None):
                pe.wait_ge(w_lo_ready, b + 1 if i is None else i * RING + (b + 1))

            def mm3(dst, w, a, start, stop):
                nc.tensor.matmul(dst, w[0], a[0], start=start, stop=False)
                nc.tensor.matmul(dst, w[0], a[1], start=False, stop=False)
                return nc.tensor.matmul(dst, w[1], a[0], start=False, stop=stop)

            def wtile(b, k, m=P):
                return [w[:, b % RING, k * m:(k + 1) * m] for w in (w_hi, w_lo)]

            spans = lambda streams: [(a, e) for _, a, e in streams]

            def out_tile(n, b, src, ks, streams, i=None):
                claim(n, i)
                weights(b, i)
                for k in ks:
                    for a, e in spans(streams):
                        ins = mm3(slot(n)[:, a:e], wtile(b, k), [s[:, k, a:e] for s in src], k == ks[0], k == ks[-1])
                ins.then_inc(unit_ready, 1)

            def pair_tiles(n, b, src, ks, streams, i=None, per_k=None):
                for k in ks:
                    if per_k is not None:
                        pe.wait_ge(lo_ready, per_k(k))
                    for z in range(2):
                        if k == ks[0]:
                            claim(n + z, i)
                            weights(b + z, i)
                        for a, e in spans(streams):
                            ins = mm3(slot(n + z)[:, a:e], wtile(b + z, k), [s[:, k, a:e] for s in src],
                                      k == ks[0], k == ks[-1])
                        if k == ks[-1]:
                            ins.then_inc(unit_ready, 1)

            h_, g_ = (h_hi, h_lo), (g_hi, g_lo)
            def keep_warm(n, count):
                claim(n)
                for _ in range(count):
                    nc.tensor.matmul(slot(n)[:, 0:L], ones, small[:, 0:L], start=True, stop=True)

            def norm_sum(nn, streams, warm=3):
                n = UNIT[f"ns{nn}"]
                keep_warm(n, warm)
                pe.wait_ge(sumsq_added, (KT + 1) * (nn + 1))
                for t in range(streams[-1][2] // P):
                    ins = nc.tensor.matmul(slot(n)[:, t:t + 1], tile_[2][:, t * P:(t + 1) * P], ones[:, 0:1], start=True, stop=True)
                ins.then_inc(unit_ready, 1)

            def norm_spread(nn, streams):
                n = UNIT[f"nb{nn}"]
                keep_warm(n, 2)
                pe.wait_ge(diag_ready, nn + 1)
                for a, e in spans(streams):
                    ins = nc.tensor.matmul(slot(n)[:, a:e], ones, tile_[3][:, a:e], start=True, stop=True)
                ins.then_inc(unit_ready, 1)
                if 0 < nn < 4:
                    keep_warm(n + 1, 3)

            def head_products():
                weights(BLK["df"])
                n = UNIT["ab"]
                for z in range(2):
                    ins = mm3(slot(n)[:, z * L:(z + 1) * L], wtile(BLK["df"], z),
                              [w[:, BLK["df"] % RING, 2 * P:2 * P + L] for w in (w_hi, w_lo)], True, True)
                ins.then_inc(unit_ready, 1)

            pe.wait_ge(cond_col_ready, 1)
            pe.wait_ge(eps_ready, 3)
            claim(UNIT["mods0"])
            for t in range(PE_TILES):
                if t % 2 == 0:
                    pe.wait_ge(ada0_landed[t // 2], 16)
                for k in range(KT):
                    w = ada0[:, (t * KT + k) * P:(t * KT + k + 1) * P]
                    ins = nc.tensor.matmul(slot(UNIT["mods0"])[:, 2 * t:2 * t + 2], w, cond_col[:, k, :], start=k == 0, stop=k == KT - 1)
            ins.then_inc(unit_ready, 1)
            norm_sum(0, STREAMS, 0)
            norm_spread(0, STREAMS)
            head_products()
            keep_warm(UNIT[("four", 0)], 2)

            def v_units(h):
                wait_part(pe, ("u", h))
                if h == 0:
                    wait_part(pe, "ab")
                for kind, tiles in (("va", range(4)), ("vb", range(4, 6))):
                    n = UNIT[(kind, h)]
                    claim(n)
                    for c, t in enumerate(tiles):
                        ins = mm3(slot(n)[:, c * C:(c + 1) * C], [u[:, t * P:(t + 1) * P] for u in u_part],
                                  [a[:, h, :] for a in ab], True, True)
                    ins.then_inc(unit_ready, 1)

            def h_tile(name, b):
                out_tile(UNIT[name], b, h_, range(KT), STREAMS)

            pair_tiles(UNIT[("four", 0)], BLK[("four", 0)], h_, range(KT), STREAMS, per_k=lambda k: SPLIT[("h", 0, k)] + 1)
            h_tile(("four", 1), BLK[("four", 1)])
            v_units(0)
            h_tile(("four", 2), BLK[("four", 2)])
            v_units(1)
            h_tile(("four", 3), BLK[("four", 3)])
            v_units(2)
            h_tile(("pin", 1), BLK[("pin", 1)])
            v_units(3)
            for g in (2, 3):
                h_tile(("pin", g), BLK[("pin", g)])
            wait_part(pe, ("vb", 3))
            claim(UNIT["dft0"])
            claim(UNIT["dft1"])
            for bx, b in enumerate(("c0", "c1", "s0", "s1")):
                weights(BLK[b])
                z = bx // 2
                for h in range(4):
                    for y in range(2):
                        t = 2 * (bx % 2) + y
                        ins = mm3(slot(UNIT[f"dft{h // 2}"])[:, (h % 2) * L:(h % 2 + 1) * L],
                                  [v[:, t, h, z * P:(z + 1) * P] for v in vv], wtile(BLK[b], y, L),
                                  bx == 0 and y == 0, bx == 3 and y == 1)
                        if bx == 3 and y == 1 and h == 1:
                            ins.then_inc(unit_ready, 1)
                if bx < 3:
                    ins.then_inc(dft_block_used, 1)
            ins.then_inc(unit_ready, 1)
            n, b = UNIT["dftc"], BLK["ctxdft"]
            claim(n)
            weights(b)
            for h in range(4):
                for q in range(4):
                    z, t = q // 2, q % 2
                    ins = mm3(slot(n)[:, h * C:(h + 1) * C], [v[:, 4 + t, h, z * P:(z + 1) * P] for v in vv],
                              wtile(b, q, C), q == 0, q == 3)
            ins.then_inc(unit_ready, 1)
            weights(BLK["poolw"])
            for g in range(4):
                n = UNIT[("poolw", g)]
                claim(n)
                wait_part(pe, ("pool", g))
                for a, e in spans(STREAMS):
                    ins = mm3(slot(n)[:, a:e], wtile(BLK["poolw"], g), [s[:, g, a:e] for s in h_], True, True)
                ins.then_inc(unit_ready, 1)

            def out_phase(b, n, src, ks, streams, per_k):
                with pe.Fori(0, KT // 4) as i:
                    claim_ahead(n, 0)
                    pair_tiles(n, b, src, ks, streams, i, per_k)
                    claim_ahead(n, 2)
                    for j in (2, 3):
                        out_tile(n + j, b + j, src, ks, streams, i)

            out_phase(BLK[("out", 0)], UNIT[("out", 0)], h_, (4, 5, 6, 7, 0, 1, 2, 3), STREAMS,
                      lambda k: SPLIT["dftc" if k >= 4 else ("y", k)] + 1)
            norm_sum(1, STREAMS)
            norm_spread(1, STREAMS)

            def ffn(l, streams):
                for gi, ng in enumerate(GROUPS):
                    b, n = BLK[("up", l, gi, 0)], UNIT[("up", l, gi, 0)]
                    p0 = sum(GROUPS[:gi])
                    per_k = (lambda k: SPLIT[("h", 1 + 2 * l, k)] + 1) if gi == 0 else None
                    with pe.Fori(0, ng // 2) as i:
                        claim_ahead(n, 0)
                        pair_tiles(n, b, h_, range(KT), streams, i, per_k)
                        claim_ahead(n, 2)
                        for j in (2, 3):
                            out_tile(n + j, b + j, h_, range(KT), streams, i)
                    out_phase(BLK[("down", l, gi, 0)], UNIT[("down", l, gi, 0)], g_, range(ng), streams,
                              lambda k: SPLIT[("g", l, p0)] + k + 1)

            ffn(0, STREAMS)
            norm_sum(2, STREAMS)
            norm_spread(2, STREAMS)

            def head_sum(i):
                n, end = UNIT[("ss", i)], T if HEADS[i][0] == "k" else L
                claim(n)
                pe.wait_ge(head_squared, i + 1)
                if end == T:
                    for a, e in ((0, L), (L, T)):
                        ins = nc.tensor.matmul(slot(n)[:, a:e], ones, head_sq[:, a:e], start=True, stop=True)
                else:
                    for t in range(4):
                        ins = nc.tensor.matmul(slot(n)[:, t:t + 1], head_sq[:, t * P:(t + 1) * P], ones[:, 0:1], start=True, stop=True)
                ins.then_inc(unit_ready, 1)

            def v_tiles(z):
                n = UNIT[f"v{z}"]
                claim(n)
                weights(BLK[("v", 1)])
                for c, t in enumerate(range(4 * z, 6 if z else 4)):
                    for k in range(KT):
                        ins = mm3(slot(n)[:, c * C:(c + 1) * C], [s[:, k, t * P:(t + 1) * P] for s in h_],
                                  wtile(BLK[("v", k // 4)], k % 4, C), k == 0, k == KT - 1)
                ins.then_inc(unit_ready, 1)

            pair_tiles(UNIT[("k", 0)], BLK[("k", 0)], h_, range(KT), STREAMS, per_k=lambda k: SPLIT[("h", 2, k)] + 1)
            head_sum(0)
            v_tiles(0)
            head_sum(1)
            v_tiles(1)
            for h in range(NH):
                out_tile(UNIT[("q", h)], BLK[("q", h)], h_, range(KT), LATENT)
                if h:
                    head_sum(1 + h)

            def scores(i):
                n, h, qt = UNIT[("s", i)], i // 4, i % 4
                claim(n)
                wait_part(pe, ("q", h))
                for a, e in spans(STREAMS):
                    ins = mm3(slot(n)[:, a:e], [q[:, h, qt * P:(qt + 1) * P] for q in qo],
                              [k[:, h // GQA, a:e] for k in kk], True, True)
                ins.then_inc(unit_ready, 1)

            def transposes(i):
                n = UNIT[("t", i)]
                claim(n)
                pe.wait_ge(probs_ready, i + 1)
                if i == 0:
                    pe.wait_ge(tabs_landed, 16)
                for k in range(6):
                    ins = nc.tensor.transpose(slot(n)[:, k * P:(k + 1) * P], probs[i % 4][:, k * P:(k + 1) * P], ident)
                ins.then_inc(unit_ready, 1)

            def weighted(name):
                _, h, z = name
                claim(UNIT[pv_unit(name)])
                wait_part(pe, ("t", 4 * h + 2 * z + 1))
                for k in range(6):
                    ins = mm3(pv_psum(name), [v[:, k, (h // GQA) * DH:(h // GQA + 1) * DH] for v in v_],
                              [p[:, h % 2, k, z * L // 2:(z + 1) * L // 2] for p in pt], k == 0, k == 5)
                if kind(pv_unit(name)) == "pv":
                    ins.then_inc(unit_ready, 1)

            scores(0)
            scores(1)
            head_sum(NH + 1)
            for p in range(1, PAIRS + PV_LAG):
                if p < PAIRS:
                    scores(2 * p)
                    scores(2 * p + 1)
                for name in pv_at(p):
                    weighted(name)
                for _, i in t_at(p):
                    transposes(i)
            out_phase(BLK[("o", 0)], UNIT[("o", 0)], qo, range(NH), LATENT, lambda k: SPLIT[("pv", k, 1)] + 1)
            norm_sum(3, LATENT)
            norm_spread(3, LATENT)
            ffn(1, LATENT)
            norm_sum(4, LATENT)
            norm_spread(4, LATENT)

        @block.vector
        def _(dve):
            V = nc.vector

            def unit(name):
                dve.wait_ge(unit_ready, UNIT[name] + 1)

            for z in range(4):
                V.memset(stat[:, z, :], 0.0).then_inc(unit_free[z], 1)

            def ada_tile(t, j, both, i=None, per=4):
                turns = 0 if i is None else i * (16 * per // ADA)
                dve.wait_ge(ada_landed[t % ADA], 16 * ada_turn(t) + turns)
                w = ada_raw[:, (t % ADA) * BW:(t % ADA + 1) * BW]
                if t % 4 == 0:
                    dve.wait_ge(mods_ready, t // 4 - (t < 16) if i is None else i * (per // 4) + t // 4)
                for s in range(1 + both):
                    n = dots_after(t, both) - both + s
                    if n <= 2:
                        dve.wait_ge(cond_ready, n)
                    if n > 1:
                        dve.wait_ge(dots_ready, n - 1 if i is None else i * (per * (1 + both)) + (n - 1))
                    V.tensor_tensor_reduce(junk[:, :], w, cond[:, s * BW:(s + 1) * BW], 1.0, 0.0, ALU.mult,
                                           ALU.add, ada_acc[:, j, s:s + 1]).then_inc(dots_ready, 1)

            def ada_add(t0, both, i=None, per=4, first=0):
                n = dots_after(t0 + 3, both)
                dve.wait_ge(dots_ready, n if i is None else i * (per * (1 + both)) + n)
                tt = t0 if i is None else i * per + t0
                for s in range(1 + both):
                    ins = V.tensor_tensor(mods[:, bass.ds(tt + first, 4 - first), s], ada_acc[:, first:4, s],
                                          small[:, bass.ds(V_ADAB + tt + first, 4 - first)], ALU.add)
                ins.then_inc(mods_ready, 1)

            def gain(n, streams):
                dve.wait_ge(mods_ready, (SHIFT[n] + 2 * KT) // 4)
                for s, _, _ in streams:
                    ins = V.scalar_tensor_tensor(gains[:, n, :, s], mods[:, SHIFT[n] + KT:SHIFT[n] + 2 * KT, s], 1.0,
                                                 small[:, NORM_G[n]:NORM_G[n] + KT], ALU.add, ALU.mult)
                ins.then_inc(gain_ready, 1)

            def rstd(n, end):
                nt = end // P
                dve.wait_ge(rms_ready, n + 1)
                V.reciprocal(token_rms[:, 0:nt], token_rms[:, 0:nt]).then_inc(rstd_ready, 1)
                dve.wait_ge(rstd_ready, n + 1)
                V.tensor_tensor(tile_[3][:, 0:end].rearrange("p (t q) -> p t q", q=P),
                                ident[:, :].rearrange("p (o q) -> p o q", o=1).broadcast_to((P, nt, P)),
                                token_rms[:, 0:nt].rearrange("p (t o) -> p t o", o=1).broadcast_to((P, nt, P)),
                                ALU.mult).then_inc(diag_ready, 1)

            def norm(n, streams):
                end = streams[-1][2]
                if n:
                    rstd(n, end)
                unit(f"nb{n}")
                dve.wait_ge(gain_ready, n + 1)

                def scale_x(k):
                    if k >= 2:
                        dve.wait_ge(lo_ready, SPLIT[("h", n, k - 2)] + 1)
                    for s, a, e in streams:
                        ins = V.scalar_tensor_tensor(tile_[k % 2][:, a:e], x[:, k, a:e], gains[:, n, k, s:s + 1],
                                                     slot(UNIT[f"nb{n}"])[:, a:e], ALU.mult, ALU.mult)
                    ins.then_inc(scaled, 1)

                scale_x(0)
                for k in range(KT):
                    if k + 1 < KT:
                        scale_x(k + 1)
                    dve.wait_ge(hi_ready, SPLIT[("h", n, k)] + 1)
                    for s, a, e in streams:
                        ins = V.scalar_tensor_tensor(h_lo[:, k, a:e], tile_[k % 2][:, a:e], mods[:, SHIFT[n] + k, s:s + 1],
                                                     h_hi[:, k, a:e].bitcast(F32), ALU.add, ALU.subtract)
                    ins.then_inc(lo_ready, 1)

            dve.wait_ge(vecs_landed, 16)
            def add_square(n, m, i=None):
                turn = lambda step, v: v if i is None else i * step + v
                end = T if n <= 2 else L
                dve.wait_ge(squared, turn(4, KT * n + m + 1))
                dve.wait_ge(sumsq_added, turn(4, (KT + 1) * n + 1 + m))
                V.tensor_tensor(tile_[2][:, 0:end], tile_[2][:, 0:end], tile_[m % 2][:, 0:end], ALU.add).then_inc(sumsq_added, 1)

            def ab_lo():
                n = UNIT["ab"]
                dve.wait_ge(hi_ready, SPLIT["ab"] + 1)
                for z in range(2):
                    ins = V.tensor_tensor(ab[1][:, :, z * P:(z + 1) * P],
                                          slot(n)[:, z * L:(z + 1) * L].rearrange("p (h c) -> p h c", h=4),
                                          ab[0][:, :, z * P:(z + 1) * P].bitcast(F32), ALU.subtract)
                ins.then_inc(lo_ready, 1)

            for t in range(PE_TILES, 16):
                ada_tile(t, t % 4, True)
                if t % 4 == 3:
                    ada_add(t - 3, True, first=max(PE_TILES - (t - 3), 0))
                if t == 15:
                    rstd(0, T)

            unit("mods0")
            for s in range(2):
                ins = V.tensor_tensor(mods[:, 0:PE_TILES, s],
                                      slot(UNIT["mods0"])[:, 0:2 * PE_TILES].rearrange("p (t s) -> p t s", s=2)[:, :, s],
                                      small[:, V_ADAB:V_ADAB + PE_TILES], ALU.add)
            ins.then_inc(mods_ready, 1)
            gain(0, STREAMS)
            norm(0, STREAMS)
            ab_lo()
            dve.wait_ge(lo_ready, SPLIT[("h", 0, KT - 1)] + 1)
            for z in range(2):
                V.memset(upad[z], 0.0).then_inc(pads_ready, 1)

            def lo_of(name, dst, src, hi, n=None):
                dve.wait_ge(hi_ready, SPLIT[name] + 1)
                V.tensor_tensor(dst, src, hi.bitcast(F32), ALU.subtract).then_inc(lo_ready, 1)

            ada = iter(range(16, 32))

            def ada_tiles(count):
                for _ in range(count):
                    t = next(ada, None)
                    if t is None:
                        return
                    ada_tile(t, t % 4, True)
                    if t % 4 == 3:
                        ada_add(t - 3, True)

            def u_lo(h):
                n = UNIT[("four", h)]
                lo_of(("u", h), u_part[1], slot(n)[:, 0:T], u_part[0])

            def v_lo(kind, h):
                n = UNIT[(kind, h)]
                t0, nt = (0, 4) if kind == "va" else (4, 2)
                lo_of((kind, h), vv[1][:, t0:t0 + nt, h, :], slot(n)[:, 0:nt * C].rearrange("p (t c) -> p t c", t=nt),
                      vv[0][:, t0:t0 + nt, h, :])
    
            steps = [0]

            def step(ins):
                ins.then_inc(window_step, 1)
                steps[0] += 1

            def pool_group(g):
                u, a, b = upad[g % 2], upad[2], upad[3]
                n = UNIT[("pin", g)]
                dve.wait_ge(u_copied, g + 1)
                if g:
                    dve.wait_ge(pooled, g)
                dve.wait_ge(*released(n))
                step(V.tensor_tensor(a[:, 1:UW], u[:, 0:UW - 1], u[:, 1:UW], ALU.add))
                src, dst, lo, hi = a, b, 1, UW
                for q in range(g):
                    d = 1 << q
                    dve.wait_ge(window_step, steps[0])
                    step(V.tensor_tensor(dst[:, lo + d:hi - d], src[:, lo:hi - 2 * d], src[:, lo + 2 * d:hi], ALU.add))
                    src, dst, lo, hi = dst, src, lo + d, hi - d
                dve.wait_ge(window_step, steps[0])
                for e0, side in ((UL, 0), (UL + L - PAD, 1), (UC, 0), (UC + C - PAD, 1)):
                    ins = V.tensor_tensor(src[:, e0:e0 + PAD], src[:, e0:e0 + PAD], edge[:, g, side, :], ALU.mult)
                step(ins)
                dve.wait_ge(window_step, steps[0])
                for e0, m in ((UL, L), (UC, C)):
                    ins = V.scalar_tensor_tensor(u[:, e0:e0 + m], src[:, e0:e0 + m], 1.0 / (2 << g), u[:, e0:e0 + m],
                                                 ALU.mult, ALU.subtract)
                ins.then_inc(pooled, 1)

            def pool_lo(g):
                dve.wait_ge(hi_ready, SPLIT[("pool", g)] + 1)
                for e0, a, m in ((UL, 0, L), (UC, L, C)):
                    ins = V.tensor_tensor(h_lo[:, g, a:a + m], upad[g % 2][:, e0:e0 + m], h_hi[:, g, a:a + m].bitcast(F32),
                                          ALU.subtract)
                ins.then_inc(lo_ready, 1)

            u_lo(0); ada_tiles(2); u_lo(1); ada_tiles(3)
            v_lo("va", 0); v_lo("vb", 0); u_lo(2); ada_tiles(3)
            v_lo("va", 1); v_lo("vb", 1); u_lo(3); ada_tiles(3)
            v_lo("va", 2); v_lo("vb", 2); ada_tiles(3)
            v_lo("va", 3); v_lo("vb", 3); ada_tiles(2)
            for g in range(4):
                pool_group(g)
                pool_lo(g)
            for z in range(2):
                n = UNIT[f"dft{z}"]
                lo_of(f"dft{z}", h_lo[:, 4 + 2 * z:6 + 2 * z, 0:L], slot(n).rearrange("p (h t) -> p h t", h=2),
                      h_hi[:, 4 + 2 * z:6 + 2 * z, 0:L])
            lo_of("dftc", h_lo[:, 4:8, L:T], slot(UNIT["dftc"]).rearrange("p (h t) -> p h t", h=4), h_hi[:, 4:8, L:T])
            for g in range(4):
                n = UNIT[("poolw", g)]
                dve.wait_ge(hi_ready, SPLIT[("y", g)] + 1)
                V.scalar_tensor_tensor(h_lo[:, g, :], slot(n)[:, 0:T], col(small, V_PS + g), h_hi[:, g, :].bitcast(F32),
                                       ALU.mult, ALU.subtract).then_inc(lo_ready, 1)

            def update(nn, gate, m, streams, i=None):
                turn = lambda step, v: v if i is None else i * step + v
                dve.wait_ge(unit_ready, turn(4, nn + 1))
                xm = tile3(x, turn(4, m))
                for s, a, e in streams:
                    g = mods[:, bass.ds(turn(4, gate + m), 1), s]
                    ins = V.scalar_tensor_tensor(xm[:, a:e], slot(nn)[:, a:e], g, xm[:, a:e], ALU.mult, ALU.add)
                ins.then_inc(unit_free[nn % 4], 1)

            def out_phase(first_unit, gate, streams, n, ada_tiles=None):
                dve.wait_ge(mods_ready, gate // 4 + 2)
                if n is not None:
                    if n == 3:
                        dve.wait_ge(probs_ready, NH * 4)
                        dve.wait_ge(rope_step, 3 * len(HEADS))
                    else:
                        dve.wait_ge(lo_ready, {1: SPLIT[("y", 3)], 2: SPLIT[("g", 0, FT - 1)], 4: SPLIT[("g", 1, FT - 1)]}[n] + 1)
                    V.memset(tile_[2], 0.0).then_inc(sumsq_added, 1)
                with dve.Fori(0, KT // 4) as i:
                    for q in (0, 2):
                        if q:
                            update(first_unit + q, gate, q, streams, i)
                        if ada_tiles is not None:
                            for j in (q, q + 1):
                                ada_tile(ada_tiles + j, j, True, i)
                        for j in (q + 1,) if q else (q, q + 1):
                            update(first_unit + j, gate, j, streams, i)
                        if n is not None:
                            for j in (q, q + 1):
                                add_square(n, j, i)
                    if ada_tiles is not None:
                        ada_add(ada_tiles, True, i)

            def ffn(l, streams):
                ct = conv[l]
                for gi, ng in enumerate(GROUPS):
                    first_u = UNIT[("up", l, gi, 0)]
                    p0 = sum(GROUPS[:gi])
                    with dve.Fori(0, ng // 2) as i:
                        for q in range(2):
                            for z in range(2):
                                j = 2 * q + z
                                nn, t = first_u + j, tile_[j]
                                v = 2 * (FT * l + p0) + j
                                dve.wait_ge(center_tap, i * 4 + (v + 1))
                                w0, w2 = (ct[:, bass.ds(i * 4 + (2 * p0 + j), 1), c:c + 1].rearrange("p a b -> p (a b)") for c in (0, 2))
                                for _, a, e in streams:
                                    ins = V.scalar_tensor_tensor(t[:, a + 1:e], slot(nn)[:, a:e - 1], w0, t[:, a + 1:e],
                                                                 ALU.mult, ALU.add)
                                ins.then_inc(left_tap, 1)
                                dve.wait_ge(left_tap, i * 4 + (v + 1))
                                for _, a, e in streams:
                                    ins = V.scalar_tensor_tensor(t[:, a:e - 1], slot(nn)[:, a + 1:e], w2, t[:, a:e - 1],
                                                                 ALU.mult, ALU.add)
                                ins.then_inc(unit_free[nn % 4], 1)
                                if l == 0:
                                    ada_tile(ADA_UP[gi] + j, j, ADA_UP[gi] < BOTH, i)
                            if l == 0 and q == 1:
                                ada_add(ADA_UP[gi], ADA_UP[gi] < BOTH, i)
                            p = FT * l + p0 + q
                            nn = first_u + 2 * q + 1
                            dve.wait_ge(silu_done, i * 2 + (p + 1))
                            dve.wait_ge(unit_free[nn % 4], i + (freed_before(nn) + 1))
                            end = streams[-1][2]
                            V.tensor_tensor(tile_[2 * q + 1][:, 0:end], tile_[2 * q][:, 0:end], tile_[2 * q + 1][:, 0:end],
                                            ALU.mult).then_inc(product_ready, 1)
                            dve.wait_ge(hi_ready, i * 2 + (SPLIT[("g", l, p0)] + q + 1))
                            V.tensor_tensor(tile3(g_lo, i * 2 + q)[:, 0:end], tile_[2 * q + 1][:, 0:end],
                                            tile3(g_hi, i * 2 + q)[:, 0:end].bitcast(F32), ALU.subtract).then_inc(lo_ready, 1)
                    first_u, last = UNIT[("down", l, gi, 0)], gi == len(GROUPS) - 1
                    if last and l == 0:
                        for t in range(92, 96):
                            ada_tile(t, t % 4, False)
                        ada_add(92, False)
                    out_phase(first_u, GATE[("ffn", l)], streams, 2 + 2 * l if last else None,
                              ADA_DOWN if (l, gi) == (0, 0) else None)

            out_phase(UNIT[("out", 0)], GATE[("mixer", 0)], STREAMS, 1, 32)
            gain(1, STREAMS)
            norm(1, STREAMS)
            ffn(0, STREAMS)
            gain(2, STREAMS)
            norm(2, STREAMS)

            def head(i):
                kind_, j = HEADS[i]
                end, buf = T if kind_ == "k" else L, headbuf[i % 2]
                dve.wait_ge(head_gained, i + 1)
                dve.wait_ge(rot_landed[i % 2], 64 * (i // 2 + 1))
                if i == 0:
                    dve.wait_ge(tabs_landed, 16)
                if i:
                    dve.wait_ge(rope_step, 3 * i)
                V.tensor_tensor(head_sin, rotated[i % 2], sin, ALU.mult).then_inc(rope_step, 1)
                V.tensor_tensor(buf[:, 0:L], buf[:, 0:L], cos, ALU.mult).then_inc(rope_step, 1)
                dve.wait_ge(rope_step, 3 * i + 2)
                V.tensor_tensor(buf[:, 0:L], buf[:, 0:L], head_sin, ALU.add).then_inc(rope_step, 1)
                dve.wait_ge(rope_step, 3 * i + 3)
                if kind_ == "k":
                    dve.wait_ge(head_rms, i + 1)
                    V.reciprocal(head_inv, head_inv).then_inc(head_rstd, 1)
                    dve.wait_ge(head_rstd, i + 1)
                    V.tensor_tensor(buf, buf, head_inv, ALU.mult).then_inc(head_ready, 1)
                dst, hi = (kk[1][:, j, :], kk[0][:, j, :]) if kind_ == "k" else (qo[1][:, j, :], qo[0][:, j, :])
                lo_of(HEADS[i], dst, buf[:, 0:end], hi)
                if kind_ == "q":
                    dve.wait_ge(head_rms, i + 1)
                    V.reciprocal(q_scale[:, 4 * j:4 * j + 4], q_scale[:, 4 * j:4 * j + 4]).then_inc(head_rstd, 1)

            def v_lo_part(z):
                n, t0, nt = UNIT[f"v{z}"], 4 * z, 4 - 2 * z
                lo_of(f"v{z}", v_[1][:, t0:t0 + nt, :], slot(n)[:, 0:nt * C].rearrange("p (t c) -> p t c", t=nt),
                      v_[0][:, t0:t0 + nt, :])

            head(0)
            v_lo_part(0)
            head(1)
            v_lo_part(1)
            for h in range(NH - 1):
                head(2 + h)

            def row_max(i):
                unit(("s", i))
                r = stat[:, i % 4, :]
                if i >= 4:
                    dve.wait_ge(max_ready, i - 3)
                V.tensor_reduce(r[:, 3:4], slot(UNIT[("s", i)])[:, 0:T], AX_X, ALU.max, negate=True).then_inc(max_found, 1)

            def normalise(i):
                dve.wait_ge(exp_ready, i + 1)
                V.reciprocal(stat[:, i % 4, 2:3], stat[:, i % 4, 1:2]).then_inc(inv_ready, 1)
                dve.wait_ge(inv_ready, i + 1)
                V.tensor_scalar(probs[i % 4], probs[i % 4], stat[:, i % 4, 2:3], None, ALU.mult).then_inc(probs_ready, 1)

            def t_lo(i):
                h, cols = i // 4, slice(i % 4 * P, (i % 4 + 1) * P)
                lo_of(("t", i), pt[1][:, h % 2, :, cols], slot(UNIT[("t", i)])[:, 0:T].rearrange("p (k q) -> p k q", k=6),
                      pt[0][:, h % 2, :, cols])

            def lo_first(p):
                for name in pv_at(p):
                    dve.wait_ge(hi_ready, SPLIT[name] + 1)
                for _, i in t_at(p)[:1]:
                    t_lo(i)
                for name in pv_at(p):
                    lo_of(name, half(qo[1], name), pv_psum(name), half(qo[0], name))

            row_max(0)
            row_max(1)
            head(NH + 1)
            normalise(0)
            normalise(1)
            for p in range(1, PAIRS + PV_LAG + 1):
                lo_first(p - 1)
                if p < PAIRS:
                    row_max(2 * p)
                    row_max(2 * p + 1)
                for _, i in t_at(p - 1)[1:]:
                    t_lo(i)
                if p < PAIRS:
                    normalise(2 * p)
                    normalise(2 * p + 1)
            out_phase(UNIT[("o", 0)], GATE[("mixer", 1)], LATENT, 3)
            gain(3, LATENT)
            norm(3, LATENT)
            ffn(1, LATENT)
            rstd(4, L)
            unit("nb4")
            for k in range(KT):
                V.scalar_tensor_tensor(x[:, k, 0:L], x[:, k, 0:L], col(small, V_FG + k), slot(UNIT["nb4"])[:, 0:L],
                                       ALU.mult, ALU.mult).then_inc(scaled, 1)




def dft(n):
    a = 2 * np.pi * (np.outer(np.arange(n), np.arange(n)) % n) / n
    return np.cos(a), np.sin(a)


def window_edges():
    e = np.ones((4, 2, PAD))
    for g in range(4):
        w = 2 << g
        for side, ts in enumerate((range(PAD), range(L - PAD, L))):
            for c, t in enumerate(ts):
                e[g, side, c] = w / (min(t + w - w // 2, L) - max(t - w // 2, 0))
    return e.astype(np.float32)


def rotary():
    pairs = DH // 4
    freqs = np.float32(10000.0) ** (-np.arange(pairs, dtype=np.float32) / np.float32(pairs))
    t = np.arange(L)
    ang = [(p.astype(np.float32)[:, None] * freqs[None, :]).T.astype(np.float64) for p in (t // GRID_W, t % GRID_W)]
    cos = np.concatenate([np.cos(ang[0])] * 2 + [np.cos(ang[1])] * 2)
    sin = np.concatenate([-np.sin(ang[0]), np.sin(ang[0]), -np.sin(ang[1]), np.sin(ang[1])])
    return cos.astype(np.float32), sin.astype(np.float32)


def by_partition(v):
    return np.asarray(v).reshape(-1, P).T


def lay_out(x, c, ctx, c_ctx, ada_w, ada_b, norm1_g, norm2_g, pf_w_in, pool_w, pool_scale, fourier_w, pf_w_out,
            attn_w_qkv, q_norm_g, k_norm_g, attn_w_o, ffn_w_up, ffn_conv_w, ffn_conv_b, ffn_w_down, final_g):
    f = np.float32
    feature_tiles = lambda a: a.T.reshape(KT, P, -1).transpose(1, 0, 2)
    xt = np.concatenate([feature_tiles(x[0]), feature_tiles(ctx[0])], axis=2)
    cvec = np.ascontiguousarray(np.broadcast_to(np.concatenate([c[0], c_ctx])[None], (P, 2 * D)))
    by_tile = np.stack([c[0], c_ctx]).reshape(2, KT, P).transpose(2, 1, 0).reshape(P, -1)
    adaw = np.concatenate([ada_w[l].T.reshape(-1, P, D) for l in range(2)])
    adaw[:PE_TILES] = ada_w[0][:, :PE_TILES * P].reshape(KT, P, PE_TILES, P).transpose(2, 1, 0, 3).reshape(PE_TILES, P, D)

    w = np.zeros((NB, P, BW), f)

    def put(name, tile):
        t = tile.reshape(P, -1)
        w[BLK[name], :, :t.shape[1]] = t

    def column_block(a, m, width=P):
        return a[:, m * width:(m + 1) * width].reshape(-1, P, width).transpose(1, 0, 2)

    cc, ss = dft(DH)
    heads = lambda a: a.transpose(1, 0, 2).reshape(P, -1)
    put("df", np.concatenate([cc.astype(f), (-ss).astype(f), heads(fourier_w[0])], axis=1))
    put("poolw", heads(pool_w[0]))
    for h in range(4):
        put(("four", h), column_block(pf_w_in[0], 4 + h))
        put(("pin", h), column_block(pf_w_in[0], h))
    for n, names in ((L, ("c0", "c1", "s0", "s1")), (C, ("ctxdft",))):
        m = [(t / np.sqrt(n * DH)).astype(f).reshape(n // P, P, n).transpose(1, 0, 2).reshape(P, -1) for t in dft(n)]
        m = np.concatenate(m, axis=1)
        for b, name in enumerate(names):
            put(name, m[:, b * BW:(b + 1) * BW])
    qkv = attn_w_qkv[0]
    kv = qkv[:, NH * DH:]
    for m in range(KT):
        put(("out", m), column_block(pf_w_out[0], m))
        put(("q", m), column_block(qkv, m))
        put(("o", m), column_block(attn_w_o[0], m))
    for j in range(NKV):
        put(("k", j), column_block(kv, j))
        put(("v", j), column_block(kv[:, NKV * DH:], 0, NKV * DH)[:, 4 * j:4 * j + 4])
    convs = []
    for l in range(2):
        for gi, n in enumerate(GROUPS):
            p0 = sum(GROUPS[:gi])
            for i in range(2 * n):
                put(("up", l, gi, i), column_block(ffn_w_up[l], p0 + i // 2 + FT * (i % 2)))
            for m in range(KT):
                put(("down", l, gi, m), column_block(ffn_w_down[l][p0 * P:(p0 + n) * P], m))
        taps = np.concatenate([ffn_conv_w[l], ffn_conv_b[l][None]]).reshape(4, 2, FT, P)
        convs.append(taps.transpose(3, 2, 1, 0).reshape(P, -1))
    edges = np.broadcast_to(window_edges().reshape(1, -1), (P, 64))
    vecs = np.concatenate([by_partition(ada_b), by_partition(norm1_g), by_partition(norm2_g), by_partition(final_g),
                           by_partition(pool_scale), by_partition(q_norm_g), by_partition(k_norm_g), edges, by_tile, np.eye(P, dtype=f), convs[0]], axis=1)
    cos, sin = rotary()
    tabs = np.concatenate([cos, sin, convs[1]], axis=1)
    assert vecs.shape[1] == NVEC and tabs.shape[1] == NTAB
    return {"xt": xt, "cvec": cvec, "wstream": w, "adaw": adaw, "vecs": vecs, "tabs": tabs}


def kernel(**inputs):
    import concourse.bacc as bacc
    from concourse.bass_utils import run_bass_kernel_spmd

    arrays = {k: np.ascontiguousarray(v) for k, v in lay_out(**{k: np.asarray(v) for k, v in inputs.items()}).items()}
    nc = bacc.Bacc("TRN2", target_bir_lowering=False, num_devices=1, dynamic_dma_scratch_size=DMA_SCRATCH)
    args = [nc.dram_tensor(k, a.shape, F32, kind="ExternalInput").ap() for k, a in arrays.items()]
    out = nc.dram_tensor("out", (P, KT, L), F32, kind="ExternalOutput").ap()
    program(nc, *args, out)
    got = run_bass_kernel_spmd(nc, [arrays], core_ids=[0]).results[0]["out"]
    return np.ascontiguousarray(got.transpose(2, 1, 0).reshape(1, L, D))
```
